# Optimizing a Trainium2 kernel written in Bass

```python
import math
import jax, jax.numpy as jnp
from jax import lax
import numpy as np

D_MODEL = 2048
BATCH = 1
SEQ = 256
DEPTH = 1

GMLP_CHUNK = 128
GMLP_GROUPS = 4
GMLP_GROUP_DIM = 128
GMLP_WIDTH = GMLP_GROUPS * GMLP_GROUP_DIM

DN_HEADS = 8
DN_HEAD_DIM = 128
DN_WIDTH = DN_HEADS * DN_HEAD_DIM
DN_CONV = 4
DN_CHUNK = 64

XA_HEADS = 4
XA_HEAD_DIM = 128
XA_WIDTH = XA_HEADS * XA_HEAD_DIM
N_MEM = 256

MIX_WIDTH = GMLP_WIDTH + DN_WIDTH + XA_WIDTH
EPS = 1e-6

SEG_WIDTHS = (GMLP_WIDTH, GMLP_WIDTH, GMLP_WIDTH,
              DN_WIDTH, DN_WIDTH, DN_WIDTH, DN_WIDTH, DN_HEADS, DN_HEADS,
              XA_WIDTH, XA_WIDTH)
IN_WIDTH = sum(SEG_WIDTHS)
SPLIT_POINTS = tuple(sum(SEG_WIDTHS[:i + 1]) for i in range(len(SEG_WIDTHS) - 1))


def rmsnorm(x, g):
    xf = x.astype(jnp.float32)
    y = xf * lax.rsqrt(jnp.mean(xf * xf, axis=-1, keepdims=True) + EPS)
    return (y * g.astype(jnp.float32)).astype(x.dtype)

def layernorm(x, g, b):
    xf = x.astype(jnp.float32)
    mu = jnp.mean(xf, axis=-1, keepdims=True)
    xc = xf - mu
    y = xc * lax.rsqrt(jnp.mean(xc * xc, axis=-1, keepdims=True) + EPS)
    return (y * g.astype(jnp.float32) + b.astype(jnp.float32)).astype(x.dtype)

def l2norm(x):
    xf = x.astype(jnp.float32)
    return xf * lax.rsqrt(jnp.sum(xf * xf, axis=-1, keepdims=True) + EPS)

def gmlp_spatial_gating(u, v, ws, bs, ln_g, ln_b):
    B, S, _ = u.shape
    u = jax.nn.gelu(u)
    v = layernorm(jax.nn.gelu(v), ln_g, ln_b)
    nc = S // GMLP_CHUNK
    v = v.reshape(B, nc, GMLP_CHUNK, GMLP_GROUPS, GMLP_GROUP_DIM)
    causal = jnp.tril(jnp.ones((GMLP_CHUNK, GMLP_CHUNK), dtype=bool))
    w = jnp.where(causal[None], ws, 0)
    s = jnp.einsum('gts,bcsgd->bctgd', w, v) + bs.T[None, None, :, :, None]
    return u * s.reshape(B, S, GMLP_WIDTH)

def causal_conv_silu(x, w):
    K = w.shape[0]
    S = x.shape[1]
    xp = jnp.pad(x, ((0, 0), (K - 1, 0), (0, 0)))
    y = sum(w[k] * xp[:, k:k + S] for k in range(K))
    return jax.nn.silu(y)

def gated_delta_rule(q, k, v, g, beta):
    f32 = jnp.float32
    q, k, v, g, beta = (t.astype(f32) for t in (q, k, v, g, beta))
    B, H, S, Dk = q.shape
    Dv = v.shape[-1]
    C = DN_CHUNK
    N = S // C
    q = q.reshape(B, H, N, C, Dk)
    k = k.reshape(B, H, N, C, Dk)
    v = v.reshape(B, H, N, C, Dv)
    g = g.reshape(B, H, N, C)
    beta = beta.reshape(B, H, N, C)

    g_cum = jnp.cumsum(g, axis=-1)
    tri = jnp.tril(jnp.ones((C, C), dtype=bool))
    strict = jnp.tril(jnp.ones((C, C), dtype=bool), k=-1)
    diff = g_cum[..., :, None] - g_cum[..., None, :]
    decay = jnp.exp(jnp.where(tri, diff, -jnp.inf))

    kb = k * beta[..., None]
    vb = v * beta[..., None]
    a = jnp.where(strict, jnp.einsum('bhnid,bhnjd->bhnij', kb, k) * decay, 0.0)
    eye = jnp.eye(C, dtype=f32)
    T = lax.linalg.triangular_solve(a + eye, jnp.broadcast_to(eye, a.shape),
                                    left_side=True, lower=True, unit_diagonal=True)
    value = jnp.einsum('bhnij,bhnjd->bhnid', T, vb)
    k_cumdecay = jnp.einsum('bhnij,bhnjd->bhnid', T, kb * jnp.exp(g_cum)[..., None])
    attn_intra = jnp.where(tri, jnp.einsum('bhnid,bhnjd->bhnij', q, k) * decay, 0.0)
    q_g = q * jnp.exp(g_cum)[..., None]
    g_last = g_cum[..., -1]
    k_dec = k * jnp.exp(g_last[..., None] - g_cum)[..., None]

    def step(state, inp):
        qg_c, kcd_c, val_c, ai_c, kd_c, gl_c = inp
        v_new = val_c - jnp.einsum('bhid,bhde->bhie', kcd_c, state)
        o_c = jnp.einsum('bhid,bhde->bhie', qg_c, state) + jnp.einsum('bhij,bhje->bhie', ai_c, v_new)
        state = state * jnp.exp(gl_c)[..., None, None] + jnp.einsum('bhid,bhie->bhde', kd_c, v_new)
        return state, o_c

    xs = tuple(jnp.moveaxis(t, 2, 0) for t in (q_g, k_cumdecay, value, attn_intra, k_dec, g_last))
    s0 = jnp.zeros((B, H, Dk, Dv), f32)
    _, o = lax.scan(step, s0, xs)
    return jnp.moveaxis(o, 0, 2).reshape(B, H, S, Dv)

def first_inputs(seed: int = 0) -> dict:
    key = jax.random.key(seed)
    ks = jax.random.split(key, 16)
    f32 = jnp.float32
    nrm = lambda k_, shp: jax.random.normal(k_, shp, f32)
    x = nrm(ks[0], (BATCH, SEQ, D_MODEL))
    mem = nrm(ks[1], (BATCH, N_MEM, D_MODEL))
    ln_g = 1.0 + 0.1 * nrm(ks[2], (DEPTH, D_MODEL))
    w_in = nrm(ks[3], (DEPTH, D_MODEL, IN_WIDTH)) * D_MODEL ** -0.5
    gmlp_ln_g = 1.0 + 0.1 * nrm(ks[4], (DEPTH, GMLP_WIDTH))
    gmlp_ln_b = 0.1 * nrm(ks[5], (DEPTH, GMLP_WIDTH))
    gmlp_ws = nrm(ks[6], (DEPTH, GMLP_GROUPS, GMLP_CHUNK, GMLP_CHUNK)) * GMLP_CHUNK ** -0.5
    gmlp_bs = 1.0 + 0.1 * nrm(ks[7], (DEPTH, GMLP_GROUPS, GMLP_CHUNK))
    conv_w = nrm(ks[8], (DEPTH, DN_CONV, 3 * DN_WIDTH)) * DN_CONV ** -0.5
    dn_a_log = jnp.log(jax.random.uniform(ks[9], (DEPTH, DN_HEADS), f32, minval=1.0, maxval=16.0))
    dt = jnp.exp(jax.random.uniform(ks[10], (DEPTH, DN_HEADS), f32,
                                    minval=math.log(1e-3), maxval=math.log(1e-1)))
    dn_dt_bias = dt + jnp.log(-jnp.expm1(-dt))
    dn_norm_g = 1.0 + 0.1 * nrm(ks[11], (DEPTH, DN_HEAD_DIM))
    mem_norm_g = 1.0 + 0.1 * nrm(ks[12], (DEPTH, D_MODEL))
    w_mem_kv = nrm(ks[13], (DEPTH, D_MODEL, 2 * XA_WIDTH)) * D_MODEL ** -0.5
    w_out = nrm(ks[14], (DEPTH, MIX_WIDTH, D_MODEL)) * MIX_WIDTH ** -0.5
    final_g = 1.0 + 0.1 * nrm(ks[15], (D_MODEL,))
    return {"x": x, "mem": mem, "ln_g": ln_g, "w_in": w_in,
            "gmlp_ln_g": gmlp_ln_g, "gmlp_ln_b": gmlp_ln_b, "gmlp_ws": gmlp_ws, "gmlp_bs": gmlp_bs,
            "conv_w": conv_w, "dn_a_log": dn_a_log, "dn_dt_bias": dn_dt_bias, "dn_norm_g": dn_norm_g,
            "mem_norm_g": mem_norm_g, "w_mem_kv": w_mem_kv, "w_out": w_out, "final_g": final_g}

def first_block(x, mem, ln_g, w_in, gmlp_ln_g, gmlp_ln_b, gmlp_ws, gmlp_bs, conv_w, dn_a_log,
              dn_dt_bias, dn_norm_g, mem_norm_g, w_mem_kv, w_out, final_g):
    B, S, _ = x.shape
    M = mem.shape[1]
    for l in range(DEPTH):
        h = rmsnorm(x, ln_g[l])
        proj = h @ w_in[l]
        (g_u, g_v, g_z, d_q, d_k, d_v, d_z, d_a, d_b, c_q, c_z) = jnp.split(proj, SPLIT_POINTS, axis=-1)

        out_a = gmlp_spatial_gating(g_u, g_v, gmlp_ws[l], gmlp_bs[l], gmlp_ln_g[l], gmlp_ln_b[l]) * jax.nn.silu(g_z)

        qkv = causal_conv_silu(jnp.concatenate([d_q, d_k, d_v], axis=-1), conv_w[l])
        q, k, v = jnp.split(qkv, 3, axis=-1)
        to_heads = lambda t: t.reshape(B, S, DN_HEADS, DN_HEAD_DIM).transpose(0, 2, 1, 3)
        q = l2norm(to_heads(q)) * DN_HEAD_DIM ** -0.5
        k = l2norm(to_heads(k))
        v = to_heads(v)
        g = -jnp.exp(dn_a_log[l].astype(jnp.float32)) * jax.nn.softplus(
            d_a.astype(jnp.float32) + dn_dt_bias[l].astype(jnp.float32))
        beta = jax.nn.sigmoid(d_b.astype(jnp.float32))
        o = gated_delta_rule(q, k, v, g.transpose(0, 2, 1), beta.transpose(0, 2, 1))
        o = o.transpose(0, 2, 1, 3).astype(x.dtype)
        o = rmsnorm(o, dn_norm_g[l]) * jax.nn.silu(d_z.reshape(B, S, DN_HEADS, DN_HEAD_DIM))
        out_b = o.reshape(B, S, DN_WIDTH)

        m = rmsnorm(mem, mem_norm_g[l])
        mk, mv = jnp.split(m @ w_mem_kv[l], 2, axis=-1)
        mk = mk.reshape(B, M, XA_HEADS, XA_HEAD_DIM)
        mv = mv.reshape(B, M, XA_HEADS, XA_HEAD_DIM)
        cq = c_q.reshape(B, S, XA_HEADS, XA_HEAD_DIM)
        scores = jnp.einsum('bshd,bmhd->bhsm', cq, mk).astype(jnp.float32) * XA_HEAD_DIM ** -0.5
        p = jax.nn.softmax(scores, axis=-1).astype(mv.dtype)
        out_c = jnp.einsum('bhsm,bmhd->bshd', p, mv).reshape(B, S, XA_WIDTH) * jax.nn.silu(c_z)

        mixed = jnp.concatenate([out_a, out_b, out_c], axis=-1)
        x = x + mixed @ w_out[l]
    return rmsnorm(x, final_g)


CHUNK = 64
Q_BLOCK = 2 * CHUNK
HEAD_DIM = 128
SB_HEADS = 8
FOX_HEADS = 8
SB_WIDTH = SB_HEADS * HEAD_DIM
FOX_WIDTH = FOX_HEADS * HEAD_DIM
IN_SPLITS = [SB_WIDTH, SB_WIDTH, SB_WIDTH,
             FOX_WIDTH, FOX_WIDTH, FOX_WIDTH,
             FOX_HEADS,
             D_MODEL, D_MODEL]
IN_WIDTH_2 = sum(IN_SPLITS)
PEER_HEADS = 8
N_KEYS = 128
N_EXPERTS = N_KEYS * N_KEYS
PEER_TOPK = 16
D_KEY = 256
HALF_KEY = D_KEY // 2
PEER_BLOCK = 128
NEG_INF = -1e30


def rms_norm(x, gain):
    x32 = x.astype(jnp.float32)
    y = x32 * lax.rsqrt(jnp.mean(x32 * x32, axis=-1, keepdims=True) + EPS)
    return (y * gain.astype(jnp.float32)).astype(x.dtype)

def to_heads(t, n_heads):
    b, s, _ = t.shape
    return t.reshape(b, s, n_heads, HEAD_DIM).transpose(0, 2, 1, 3)

def from_heads(t):
    b, h, s, d = t.shape
    return t.transpose(0, 2, 1, 3).reshape(b, s, h * d)

def stick_breaking_attention(q, k, v):
    s_len = q.shape[2]
    scale = 1.0 / math.sqrt(HEAD_DIM)
    outs = []
    for blk in range(s_len // Q_BLOCK):
        t0, t1 = blk * Q_BLOCK, (blk + 1) * Q_BLOCK
        qb = q[:, :, t0:t1].astype(jnp.float32)
        kb = k[:, :, :t1].astype(jnp.float32)
        vb = v[:, :, :t1].astype(jnp.float32)
        z = jnp.einsum('bhqd,bhkd->bhqk', qb, kb) * scale
        t_idx = jnp.arange(t0, t1)[:, None]
        s_idx = jnp.arange(t1)[None, :]
        strict = s_idx < t_idx
        log_1m_beta = jnp.where(strict, jax.nn.log_sigmoid(-z), 0.0)
        suffix = lax.cumsum(log_1m_beta, axis=3, reverse=True) - log_1m_beta
        weights = jnp.where(strict, jnp.exp(jax.nn.log_sigmoid(z) + suffix), 0.0)
        outs.append(jnp.einsum('bhqk,bhkd->bhqd', weights, vb))
    return jnp.concatenate(outs, axis=2).astype(q.dtype)

def forgetting_attention(q, k, v, log_f):
    s_len = q.shape[2]
    scale = 1.0 / math.sqrt(HEAD_DIM)
    cum_f = jnp.cumsum(log_f.astype(jnp.float32), axis=-1)
    outs = []
    for blk in range(s_len // Q_BLOCK):
        t0, t1 = blk * Q_BLOCK, (blk + 1) * Q_BLOCK
        qb = q[:, :, t0:t1].astype(jnp.float32)
        kb = k[:, :, :t1].astype(jnp.float32)
        vb = v[:, :, :t1].astype(jnp.float32)
        logits = jnp.einsum('bhqd,bhkd->bhqk', qb, kb) * scale
        logits = logits + cum_f[:, :, t0:t1, None] - cum_f[:, :, None, :t1]
        causal = jnp.arange(t1)[None, :] <= jnp.arange(t0, t1)[:, None]
        probs = jax.nn.softmax(jnp.where(causal, logits, NEG_INF), axis=-1)
        outs.append(jnp.einsum('bhqk,bhkd->bhqd', probs, vb))
    return jnp.concatenate(outs, axis=2).astype(q.dtype)

def hybrid_mixer(h, w_in, b_forget, w_branch_a, w_branch_b, w_out):
    proj = h @ w_in
    cuts = list(np.cumsum(IN_SPLITS)[:-1])
    q_a, k_a, v_a, q_b, k_b, v_b, f_logit, g_a, g_b = jnp.split(proj, cuts, axis=-1)
    o_a = stick_breaking_attention(to_heads(q_a, SB_HEADS), to_heads(k_a, SB_HEADS),
                                   to_heads(v_a, SB_HEADS))
    log_f = jax.nn.log_sigmoid(f_logit.astype(jnp.float32) + b_forget.astype(jnp.float32))
    log_f = log_f.transpose(0, 2, 1)
    o_b = forgetting_attention(to_heads(q_b, FOX_HEADS), to_heads(k_b, FOX_HEADS),
                               to_heads(v_b, FOX_HEADS), log_f)
    merged = (jax.nn.sigmoid(g_a) * (from_heads(o_a) @ w_branch_a)
              + jax.nn.sigmoid(g_b) * (from_heads(o_b) @ w_branch_b))
    return merged @ w_out

def peer_ffn(h, w_query, sub_keys, expert_u, expert_v):
    b, s, d = h.shape
    n_tok = b * s
    ht = h.reshape(n_tok, d)
    q = (ht @ w_query).astype(jnp.float32).reshape(n_tok, PEER_HEADS, 2, HALF_KEY)
    scores = jnp.einsum('thpc,hpnc->thpn', q, sub_keys.astype(jnp.float32))
    s1, i1 = lax.top_k(scores[:, :, 0], PEER_TOPK)
    s2, i2 = lax.top_k(scores[:, :, 1], PEER_TOPK)
    cand_score = (s1[..., :, None] + s2[..., None, :]).reshape(n_tok, PEER_HEADS, PEER_TOPK * PEER_TOPK)
    cand_id = (i1[..., :, None] * N_KEYS + i2[..., None, :]).reshape(n_tok, PEER_HEADS, PEER_TOPK * PEER_TOPK)
    top_score, pos = lax.top_k(cand_score, PEER_TOPK)
    expert_ids = jnp.take_along_axis(cand_id, pos, axis=-1)
    gates = jax.nn.softmax(top_score, axis=-1)

    n_blk = n_tok // PEER_BLOCK

    def expert_block(args):
        xb, idb, gb = args
        u_sel = expert_u[idb]
        act = jax.nn.gelu(jnp.einsum('thkd,td->thk', u_sel, xb).astype(jnp.float32))
        w = (gb * act).astype(xb.dtype)
        v_sel = expert_v[idb]
        return jnp.einsum('thk,thkd->td', w, v_sel)

    out = lax.map(expert_block, (ht.reshape(n_blk, PEER_BLOCK, d),
                                 expert_ids.reshape(n_blk, PEER_BLOCK, PEER_HEADS, PEER_TOPK),
                                 gates.reshape(n_blk, PEER_BLOCK, PEER_HEADS, PEER_TOPK)))
    return out.reshape(b, s, d)

def second_inputs(seed: int = 0) -> dict:
    key = jax.random.key(seed)
    ks = jax.random.split(key, 14)
    f32 = jnp.float32
    x = jax.random.normal(ks[0], (BATCH, SEQ, D_MODEL), f32)
    norm_mix_gain = 1.0 + 0.02 * jax.random.normal(ks[1], (DEPTH, D_MODEL), f32)
    w_in = jax.random.normal(ks[2], (DEPTH, D_MODEL, IN_WIDTH_2), f32) * D_MODEL ** -0.5
    b_forget = jax.random.uniform(ks[3], (DEPTH, FOX_HEADS), f32, minval=1.0, maxval=4.0)
    w_branch_a = jax.random.normal(ks[4], (DEPTH, SB_WIDTH, D_MODEL), f32) * SB_WIDTH ** -0.5
    w_branch_b = jax.random.normal(ks[5], (DEPTH, FOX_WIDTH, D_MODEL), f32) * FOX_WIDTH ** -0.5
    w_out = jax.random.normal(ks[6], (DEPTH, D_MODEL, D_MODEL), f32) * D_MODEL ** -0.5
    norm_ffn_gain = 1.0 + 0.02 * jax.random.normal(ks[7], (DEPTH, D_MODEL), f32)
    w_query = jax.random.normal(ks[8], (DEPTH, D_MODEL, PEER_HEADS * D_KEY), f32) * D_MODEL ** -0.5
    sub_keys = jax.random.normal(ks[9], (DEPTH, PEER_HEADS, 2, N_KEYS, HALF_KEY), f32) * HALF_KEY ** -0.5
    expert_u = jax.random.normal(ks[10], (DEPTH, N_EXPERTS, D_MODEL), f32) * D_MODEL ** -0.5
    expert_v = jax.random.normal(ks[11], (DEPTH, N_EXPERTS, D_MODEL), f32) * PEER_HEADS ** -0.5
    norm_final_gain = 1.0 + 0.02 * jax.random.normal(ks[12], (D_MODEL,), f32)
    return {"x": x, "norm_mix_gain": norm_mix_gain, "w_in": w_in, "b_forget": b_forget,
            "w_branch_a": w_branch_a, "w_branch_b": w_branch_b, "w_out": w_out,
            "norm_ffn_gain": norm_ffn_gain, "w_query": w_query, "sub_keys": sub_keys,
            "expert_u": expert_u, "expert_v": expert_v, "norm_final_gain": norm_final_gain}

def second_block(x, norm_mix_gain, w_in, b_forget, w_branch_a, w_branch_b, w_out,
              norm_ffn_gain, w_query, sub_keys, expert_u, expert_v, norm_final_gain):
    for layer in range(DEPTH):
        h = rms_norm(x, norm_mix_gain[layer])
        x = x + hybrid_mixer(h, w_in[layer], b_forget[layer], w_branch_a[layer],
                             w_branch_b[layer], w_out[layer])
        h = rms_norm(x, norm_ffn_gain[layer])
        x = x + peer_ffn(h, w_query[layer], sub_keys[layer], expert_u[layer], expert_v[layer])
    return rms_norm(x, norm_final_gain)


def setup_inputs(seed=0):
    out = dict(first_inputs(seed))
    for name, value in second_inputs(seed + 1).items():
        if name != "x":
            out[name + "_2"] = value
    return out


def reference(
    x, mem, ln_g, w_in, gmlp_ln_g, gmlp_ln_b, gmlp_ws, gmlp_bs, conv_w, dn_a_log, dn_dt_bias,
    dn_norm_g, mem_norm_g, w_mem_kv, w_out, final_g, norm_mix_gain_2, w_in_2, b_forget_2,
    w_branch_a_2, w_branch_b_2, w_out_2, norm_ffn_gain_2, w_query_2, sub_keys_2, expert_u_2,
    expert_v_2, norm_final_gain_2,
):
    x = first_block(
        x, mem, ln_g, w_in, gmlp_ln_g, gmlp_ln_b, gmlp_ws, gmlp_bs, conv_w, dn_a_log,
        dn_dt_bias, dn_norm_g, mem_norm_g, w_mem_kv, w_out, final_g,
    )
    return second_block(
        x, norm_mix_gain_2, w_in_2, b_forget_2, w_branch_a_2, w_branch_b_2, w_out_2,
        norm_ffn_gain_2, w_query_2, sub_keys_2, expert_u_2, expert_v_2, norm_final_gain_2,
    )


_drawn_inputs = setup_inputs


def setup_inputs(seed=0):
    import zlib

    import numpy as np

    out = dict(_drawn_inputs(seed))
    spreads = {}
    factors = {'mem_norm_g': 4.917,
     'norm_mix_gain_2': 2.681,
     'norm_final_gain_2': 7.358,
     'norm_ffn_gain_2': 4.768}
    for name, (base, spread) in spreads.items():
        noise = np.random.default_rng([zlib.crc32(name.encode()), seed]).standard_normal(out[name].shape)
        drawn = base * np.exp(spread * noise) if base else spread * noise
        out[name] = __import__('jax').numpy.asarray(drawn.astype(out[name].dtype))
    for name, factor in factors.items():
        out[name] = (out[name] * factor).astype(out[name].dtype)
    return out
```

```python
import concourse.bass as bass
from concourse import mybir
from concourse.alu_op_type import AluOpType as ALU
from contextlib import ExitStack

F32 = mybir.dt.float32
F32R = mybir.dt.float32r
U32 = mybir.dt.uint32
ACT = mybir.ActivationFunctionType
AX = mybir.AxisListType.X

P = 128
D = 2048
KT = D // P
S = 256
TT = S // P
EPS = 1e-6
SCALE = float(P) ** -0.5
NEG_INF = -1e30
DN_HEADS = 8
HEADS = 8
XA_HEADS = 4
GROUPS = 4
CHUNK = 64
CHUNKS = S // CHUNK
LEVELS = 6
TAPS = 4
TOPK = 16
RING = 4
HALF = KT // 2

KV_UNITS, IN_UNITS, OUT_UNITS, IN2_UNITS, BR_UNITS = 8, 52, KT, 80, KT // 2 * 2
EXPERT_CHUNKS = 8
CHUNK_UNITS = 2 * KT
U_KV = 0
U_IN = U_KV + KV_UNITS
U_OUT = U_IN + IN_UNITS
U_IN2 = U_OUT + OUT_UNITS
U_BR = U_IN2 + IN2_UNITS
U_OUT2 = U_BR + BR_UNITS
U_Q = U_OUT2 + OUT_UNITS
U_EXP = U_Q + OUT_UNITS
U_END = U_EXP + EXPERT_CHUNKS * CHUNK_UNITS

IDENT, ONES, TRI_LE, TRI_LT, TRI_GT, C64_LE, C64_GT, IOTA, LEVEL0 = range(9)
NCONST = LEVEL0 + LEVELS
G_MEM, G_LN, G_FINAL, G_MIX, G_FFN, G_OUT = range(6)


def shape_constants():
    import numpy as np
    a, b = np.arange(P)[:, None], np.arange(P)[None, :]
    same = (a // CHUNK) == (b // CHUNK)
    rows = [a == b, a >= 0 * b, a <= b, a < b, a > b, same & (a <= b), same & (a > b), 0 * a + b]
    for lev in range(LEVELS):
        s = 1 << lev
        rows.append((a // (2 * s) == b // (2 * s)) & (a // s < b // s))
    return np.ascontiguousarray(np.stack([(r + 0 * b).astype(np.float32) for r in rows], 1))


class Chain:

    def __init__(self, eng, sem):
        self.eng, self.sem, self.n, self.steps = eng, sem, 0, 0

    def __call__(self, ins):
        ins.then_inc(self.sem, 1)
        self.n = self.n + 1
        self.steps += 1
        self.eng.wait_ge(self.sem, self.n)

    def loop(self, start, end, per, body):
        base, s0 = self.n, self.steps
        with self.eng.Fori(start, end) as i:
            self.n = i * per + (base - start * per)
            body(i)
        assert self.steps - s0 == per, (self.steps - s0, per)
        self.n = base + (end - start) * per


def program(nc, ap, out, g_dram):
    ctx = ExitStack()
    with ctx:
        base = [16512]

        def at(name, shape, off, dt=F32):
            return nc.alloc_sbuf_tensor_at(name, shape, dt, offset=off)

        def take(nbytes):
            off = base[0]
            base[0] += (nbytes + 31) // 32 * 32
            assert base[0] <= 229344, base[0]
            return off

        def sem(name):
            return ctx.enter_context(nc.semaphore(name))

        K = 1024
        raw = at("raw", [P, RING, KT, P], take(32 * K))
        whi = at("whi", [P, 4, HALF, P], take(16 * K), F32R)
        wlo = at("wlo", [P, 4, HALF, P], take(16 * K), F32R)
        X = at("X", [P, KT, S], take(16 * K))
        o_T = take(16 * K)
        T16 = at("T16", [P, KT, S], o_T)
        o_hi, o_lo = take(16 * K), take(16 * K)
        xhi = at("xhi", [P, KT, S], o_hi, F32R)
        xlo = at("xlo", [P, KT, S], o_lo, F32R)
        cst = at("cst", [P, NCONST, P], take(NCONST * 512))
        gains = at("gains", [P, 6, KT], take(6 * KT * 4))
        cw = at("cw", [P, 24, TAPS], take(24 * TAPS * 4))
        wab = at("wab", [P, KT, 24], take(KT * 24 * 4))
        small = at("small", [P, 16], take(64))
        rstd = at("rstd", [P, S], take(S * 4))
        o_A = base[0]
        A = lambda k: o_A + int(k * K)

        def c(n):
            return cst[:, n, :]

        ident = c(IDENT)
        ones = c(ONES)

        mixed = at("mixed", [P, KT, S], A(0))
        qkv = at("qkv", [P, 24, S], A(16))
        cq = at("cq", [P, XA_HEADS, S], A(40))
        gv = at("gv", [P, GROUPS, S], A(44))
        gz = at("gz", [P, GROUPS, S], A(48))
        mk = at("mk", [P, XA_HEADS, S], A(52))
        mvt = at("mvt", [P, TT, XA_HEADS, P], A(56))
        stage = at("stage", [P, 2, S + TAPS - 1], A(60))
        ycv = at("ycv", [P, 2, S], A(62.25))
        mem_in = at("mem_in", [P, KT, S], A(16))
        mvf = at("mvf", [P, XA_HEADS, S], A(32))
        xa_p = at("xa_p", [P, 8, S], o_T)
        xa_pt = at("xa_pt", [P, XA_HEADS, TT, S], o_T + 8 * K)
        vt = at("vt", [P, GROUPS, TT, P], o_T)
        vsq = at("vsq", [P, GROUPS, S], o_T + 4 * K)
        wst = at("wst", [P, GROUPS, P], A(60))
        bs_row = at("bs_row", [1, GROUPS * P], A(62))
        mean = at("mean", [P, S], o_T + 12 * K)
        kbg = at("kbg", [P, 16, P], o_hi)
        kd = at("kd", [P, 16, P], o_hi + 8 * K)
        at_ = at("at_", [P, 16, P], o_lo)
        ait = at("ait", [P, 16, P], o_lo + 8 * K)
        pt = at("pt", [P, 16, P], o_T)
        qt = at("qt", [P, 16, P], o_T + 8 * K)
        dec = at("dec", [P, 16, P], A(40))
        xt = at("xt", [P, 16, P], A(48))
        expr = at("expr", [P, 8, S], A(48))
        st = at("st", [P, 8, P], A(48))
        vn = at("vn", [P, 8, P], A(52))
        odn = at("odn", [P, 8, S], o_lo)
        vb = at("vb", [P, 16, P], A(32))
        kcd = at("kcd", [P, 16, P], A(24))
        sm = A(64.5)
        nx = at("nx", [P, 16], sm)
        rs = at("rs", [P, 16], sm + 64)
        gb8 = at("gb8", [8, 2, S], sm + 128)
        tm8 = at("tm8", [8, 2, S], sm + 128 + 2 * K)
        gbt = at("gbt", [P, TT, 2, 8], sm + 128)
        gcol = at("gcol", [P, TT, 2, 8], sm + 256)
        ecol = at("ecol", [P, TT, 2, 8], sm + 384)
        bex = at("bex", [P, TT, 8], sm + 512)
        gc8 = at("gc8", [8, S], sm + 640)
        bt8 = at("bt8", [8, S], sm + 128 + 2 * K + 1 * K)
        egl = at("egl", [P, 8, CHUNKS], sm + 128 + 2 * K)
        qa = at("qa", [P, 8, S], o_T)
        ka = at("ka", [P, 8, S], o_T + 8 * K)
        va = at("va", [P, 8, S], A(0))
        qb = at("qb", [P, 8, S], A(8))
        kb = at("kb", [P, 8, S], A(16))
        vb2 = at("vb2", [P, 8, S], A(24))
        sga = at("sga", [P, KT, S], A(32))
        sgb = at("sgb", [P, KT, S], A(48))
        za = at("za", [P, 8, 384], o_hi)
        zb = at("zb", [P, 8, 384], o_hi + 12 * K)
        vtk = at("vtk", [P, 8, TT, P], o_hi + 24 * K)
        nfx = at("nfx", [P, 16], sm)
        rfx = at("rfx", [P, 16], sm + 64)
        f8 = at("f8", [8, S], sm + 128)
        ft8 = at("ft8", [8, S], sm + 128 + K)
        cf8 = at("cf8", [8, S], sm + 128 + 2 * K)
        fcol = at("fcol", [P, TT, 8], sm + 128 + 3 * K)
        skt = at("skt", [P, 16, P], A(32))
        sc = at("sc", [P, 16, P], A(0))
        sc2 = at("sc2", [P, 16, P], A(8))
        cand = at("cand", [P, 8, S], A(16))
        cand2 = at("cand2", [P, 8, S], A(24))
        v16 = at("v16", [P, 16, TOPK], A(40))
        i16 = at("i16", [P, 16, TOPK], A(41), U32)
        if16 = at("if16", [P, 16, TOPK], A(42))
        ts = at("ts", [P, 8, TOPK], A(43))
        ti = at("ti", [P, 8, TOPK], A(43.5), U32)
        th = at("th", [P, 8, TOPK], A(44), U32)
        tl = at("tl", [P, 8, TOPK], A(44.5), U32)
        thf = at("thf", [P, 8, TOPK], A(45))
        tlf = at("tlf", [P, 8, TOPK], A(45.5))
        e1 = at("e1", [P, P], A(46))
        e2 = at("e2", [P, P], A(46.5))
        gt = at("gt", [P, 8, TOPK], A(47))
        gs = at("gs", [P, 8], A(47.5))
        sel = at("sel", [P, 3, S], sm)
        oh1 = at("oh1", [P, 4, P], A(48))
        oh2 = at("oh2", [P, 4, P], A(50))
        gst = at("gst", [P, 2, P, 16], A(0))
        whid = at("whid", [P, KT, S], A(0), F32R)
        wlod = at("wlod", [P, KT, S], A(16), F32R)
        gch = at("gch", [P, 16, KT, 16], A(32))
        act_u = at("act_u", [P, 2, S], A(48))
        wt = at("wt", [P, 2, S], A(50))

        unit_ps = ctx.enter_context(nc.psum_tensor("unit_ps", [P, 2, 512], F32))
        ps = ctx.enter_context(nc.psum_tensor("ps", [P, 6, 512], F32))
        psf = ps[:, :, :].rearrange("p b n -> p (b n)")

        raw_in = [sem(f"raw_in{r}") for r in range(RING)]
        hi_ready, lo_ready, pe_half = sem("hi_ready"), sem("lo_ready"), sem("pe_half")
        evac = [sem("evac0"), sem("evac1")]
        v_chain, a_chain = sem("v_chain"), sem("a_chain")
        cst_in, mem_ld, x_ld, ws_ld, sk_ld, out_st = (sem(n) for n in ("cst_in", "mem_ld", "x_ld", "ws_ld", "sk_ld", "out_st"))
        norm_sq, norm_sum, norm_var, norm_std = (sem(n) for n in ("norm_sq", "norm_sum", "norm_var", "norm_std"))
        lin_src, lin_hi, lin_lo = sem("lin_src"), sem("lin_hi"), sem("lin_lo")
        conv_y, conv_used = sem("conv_y"), sem("conv_used")
        signals = {}

        def sg(name):
            if name not in signals:
                signals[name] = sem(name)
            return signals[name]


        block = ctx.enter_context(nc.Block())

        @block.sync
        def _(sp):
            sp.dma_start(mem_in[:], ap["mem"]).then_inc(mem_ld, 16)
            sp.dma_start(cst[:], ap["consts"]).then_inc(cst_in, 16)
            sp.dma_start(gains[:], ap["gains"]).then_inc(cst_in, 16)
            sp.dma_start(cw[:], ap["conv"]).then_inc(cst_in, 16)
            sp.dma_start(wab[:], ap["w_abf"]).then_inc(cst_in, 16)
            sp.dma_start(small[0:8, 0:3], ap["small8"]).then_inc(cst_in, 16)
            sp.dma_start(small[:, 3:4], ap["dn_g"]).then_inc(cst_in, 16)
            sp.dma_start(small[:, 5:13], ap["gmlp_ln"]).then_inc(cst_in, 16)
            sp.dma_start(X[:], ap["x"]).then_inc(x_ld, 16)

            def load(src, u0, i, j, at_unit=None):
                lead = i * 8 + (2 * (u0 + j) - 6)
                if not (isinstance(lead, int) and lead <= 0):
                    sp.wait_ge(lo_ready, lead)
                n = i * RING + j
                sp.dma_start(raw[:, j, :, :].rearrange("p k m -> p (k m)"),
                             src[bass.ds(n, 1)].rearrange("a p n -> p (a n)")).then_inc(raw_in[j], 16)

            def stream(src, n, u0, first=0):
                with sp.Fori(first, n // RING) as i:
                    for j in range(RING):
                        load(src, u0, i, j)

            for i in range(KV_UNITS // RING):
                for j in range(RING):
                    load(ap["w_kv"], U_KV, i, j)
            stream(ap["w_in"], IN_UNITS, U_IN)
            for j in range(RING):
                load(ap["w_out"], U_OUT, 0, j)
            sp.wait_ge(conv_used, 24)
            sp.dma_start(wst[:], ap["ws"]).then_inc(ws_ld, 16)
            sp.dma_start(bs_row[:], ap["bs"]).then_inc(ws_ld, 16)
            stream(ap["w_out"], OUT_UNITS, U_OUT, 1)
            stream(ap["w_in2"], IN2_UNITS, U_IN2)
            stream(ap["w_br"], BR_UNITS, U_BR)
            stream(ap["w_out2"], OUT_UNITS, U_OUT2)
            sp.wait_ge(lin_lo, 4 * 6)
            sp.dma_start(skt[:], ap["sub_keys"]).then_inc(sk_ld, 16)
            stream(ap["w_q"], OUT_UNITS, U_Q)
            stream(ap["w_exp"], EXPERT_CHUNKS * CHUNK_UNITS, U_EXP)

        @block.gpsimd
        def _(pool):
            def lower(n):
                with pool.Fori(0, n) as i:
                    for j in range(RING):
                        for h in range(2):
                            s = (2 * j + h) % 4
                            pool.wait_ge(hi_ready, i * 8 + (2 * j + h + 1))
                            pool.tensor_tensor(wlo[:, s, :, :], raw[:, j, h * HALF:(h + 1) * HALF, :],
                                               whi[:, s, :, :].bitcast(F32), ALU.subtract).then_inc(lo_ready, 1)

            lower(U_END // RING)

        @block.scalar
        def _(act):
            step = Chain(act, a_chain)

            def conv_unit(i, u0, d):
                j = d % RING
                act.wait_ge(raw_in[j], i * 16 + 16 * ((u0 + d) // RING + 1))
                for h in range(2):
                    lead = i * 8 + (2 * (u0 + d) + h - 3)
                    if not (isinstance(i, int) and lead <= 0):
                        act.wait_ge(pe_half, lead)
                    act.activation(whi[:, (2 * j + h) % 4, :, :], raw[:, j, h * HALF:(h + 1) * HALF, :],
                                   ACT.Copy).then_inc(hi_ready, 1)

            def segment(u0, n, body=None, first=False, last=False):
                def run(i):
                    for j in range(RING):
                        conv_unit(i, u0, j + 1)
                        if body:
                            body(i, j, u0)
                if first:
                    run(0)
                with act.Fori(1 if first else 0, n // RING) as i:
                    run(i)

            def into(dst, func):
                def body(i, j, u0):
                    act.wait_ge(pe_half, i * 8 + (2 * (u0 + j) + 2))
                    act.activation(dst[:, bass.ds(i * RING + j, 1), :], unit_ps[:, j % 2:j % 2 + 1, 0:S], func
                                   ).then_inc(evac[j % 2], 1)
                return body

            def wait_units(u):
                act.wait_ge(evac[0], u // 2)
                act.wait_ge(evac[1], u // 2)

            def norm_squares(n, src):
                for q in range(4):
                    act.activation(T16[:, 4 * q:4 * q + 4, :], src[:, 4 * q:4 * q + 4, :], ACT.Square).then_inc(norm_sq, 1)

            def norm_root(n):
                act.wait_ge(norm_var, n + 1)
                act.activation(rstd[:], rstd[:], ACT.Sqrt).then_inc(norm_std, 1)

            def upper(ready, src=T16):
                for q in range(4):
                    act.wait_ge(*ready[q])
                    act.activation(xhi[:, 4 * q:4 * q + 4, :], src[:, 4 * q:4 * q + 4, :], ACT.Copy).then_inc(lin_hi, 1)

            act.wait_ge(mem_ld, 16)
            norm_squares(0, mem_in)
            conv_unit(0, 0, 0)
            norm_root(0)
            upper([(lin_src, q + 1) for q in range(4)])
            segment(U_KV, KV_UNITS, first=True)
            act.wait_ge(x_ld, 16)
            act.wait_ge(lin_lo, 4)
            norm_squares(1, X)
            norm_root(1)
            act.wait_ge(sg("kv_done"), 1)
            upper([(lin_src, 4 + q + 1) for q in range(4)])
            segment(U_IN, 4)
            cz = mixed[:, 12:16, :]
            segment(U_IN + 4, 4, into(cz, ACT.Silu))
            segment(U_IN + 8, 4, into(gz, ACT.Silu))
            segment(U_IN + 12, 8, into(mixed[:, 4:12, :], ACT.Silu))
            segment(U_IN + 20, 4, into(mixed[:, 0:4, :], ACT.Gelu_apprx_tanh))
            segment(U_IN + 24, 4, into(gv, ACT.Gelu_apprx_tanh))

            def silu_conv(i, j, u0):
                act.wait_ge(conv_y, i * 4 + (j + 1))
                act.activation(qkv[:, bass.ds(i * RING + j, 1), :], ycv[:, j % 2:j % 2 + 1, :], ACT.Silu
                               ).then_inc(conv_used, 1)
            segment(U_IN + 28, 24, silu_conv)

            act.wait_ge(sg("xa_max"), 1)
            for n in range(8):
                act.activation(xa_p[:, n, :], psf[:, 1024 + n * S:1024 + (n + 1) * S], ACT.Exp, bias=nx[:, n:n + 1],
                               accum_out=rs[:, n:n + 1]).then_inc(sg("xa_exp"), 1)
            act.wait_ge(sg("ln_centred"), 1)
            act.activation(vsq[:], gv[:], ACT.Square).then_inc(sg("ln_sq"), 1)
            act.wait_ge(sg("ln_var"), 1)
            act.activation(rstd[:], rstd[:], ACT.Sqrt).then_inc(sg("ln_std"), 1)

            act.wait_ge(sg("ab_in"), 1)
            step(act.activation(tm8[:, 0, :], gb8[:, 0, :], ACT.Abs))
            step(act.activation(tm8[:, 0, :], tm8[:, 0, :], ACT.Exp, scale=-1.0))
            step(act.activation(tm8[:, 0, :], tm8[:, 0, :], ACT.Ln, bias=1.0))
            act.activation(small[0:8, 4:5], small[0:8, 1:2], ACT.Exp).then_inc(sg("softplus"), 1)
            act.activation(gb8[:, 1, :], psf[0:8, 256:512], ACT.Sigmoid).then_inc(sg("beta"), 1)
            for w in range(2):
                if w:
                    act.wait_ge(sg("qk_scaled"), w)
                else:
                    act.wait_ge(sg("sgu"), 1)
                act.activation(pt[:], qkv[:, 8 - 8 * w:16 - 8 * w, :].rearrange("p h (t n) -> p (h t) n", t=2), ACT.Square).then_inc(sg("qk_sq"), 1)
                act.wait_ge(sg("qk_var"), w + 1)
                act.activation(qt[:], qt[:], ACT.Sqrt).then_inc(sg("qk_std"), 1)
            act.wait_ge(sg("gcol_in"), 1)
            act.activation(ecol[:], gcol[:], ACT.Exp).then_inc(sg("ecol"), 1)
            act.wait_ge(sg("dec_arg"), 16)
            act.activation(expr[:].rearrange("p h n -> p (h n)"), psf[:, 1024:3072], ACT.Exp).then_inc(sg("exp_row"), 1)
            act.activation(dec[:], dec[:], ACT.Exp).then_inc(sg("dec_exp"), 1)

            with act.Fori(0, LEVELS) as lev:
                for g in range(4):
                    act.wait_ge(sg("inv_x"), lev * 4 + (g + 1))
                    act.activation(xt[:, 4 * g:4 * g + 4, :].rearrange("p a n -> p (a n)"), ps[:, 3 * (g % 2), :], ACT.Copy
                                   ).then_inc(sg("inv_xc"), 1)
            act.wait_ge(sg("kcd_mm"), 1)
            act.activation(kcd[:].rearrange("p a n -> p (a n)"), psf[:, 0:2048], ACT.Copy, scale=-1.0).then_inc(sg("kcd"), 1)
            act.wait_ge(sg("odn_full"), 1)
            act.activation(pt[:], odn[:].rearrange("p h (t n) -> p (h t) n", t=2), ACT.Square).then_inc(sg("odn_sq"), 1)
            act.wait_ge(sg("odn_var"), 1)
            act.activation(qt[:], qt[:], ACT.Sqrt).then_inc(sg("odn_std"), 1)

            upper([(sg("mixed_done"), 1)] * 4, mixed)
            segment(U_OUT, OUT_UNITS)
            wait_units(U_IN2)
            norm_squares(2, X)
            norm_root(2)
            act.wait_ge(sg("x2_done"), 1)
            norm_squares(3, X)
            norm_root(3)
            upper([(lin_src, 8 + q + 1) for q in range(4)])
            segment(U_IN2, 16, into(sga, ACT.Sigmoid))
            segment(U_IN2 + 16, 16, into(sgb, ACT.Sigmoid))
            segment(U_IN2 + 32, 48)

            act.wait_ge(sg("f_in"), 1)
            step(act.activation(ft8[:], f8[:], ACT.Abs))
            step(act.activation(ft8[:], ft8[:], ACT.Exp, scale=-1.0))
            act.activation(ft8[:], ft8[:], ACT.Ln, bias=1.0).then_inc(sg("f_ln"), 1)
            act.wait_ge(sg("sb_z"), 1)
            flat_a = za[:].rearrange("p h n -> p (h n)")
            flat_b = zb[:].rearrange("p h n -> p (h n)")
            step(act.activation(flat_a, psf[:, 0:3072], ACT.Abs))
            step(act.activation(flat_a, flat_a, ACT.Exp, scale=-1.0))
            act.activation(flat_a, flat_a, ACT.Ln, bias=1.0).then_inc(sg("sb_ln"), 1)
            act.wait_ge(sg("sb_arg"), 1)
            act.activation(flat_b, flat_b, ACT.Exp).then_inc(sg("sb_exp"), 1)
            act.wait_ge(sg("fx_max"), 1)
            for n in range(16):
                src = flat_a[:, n * P:(n + 1) * P] if n < 8 else flat_a[:, 1024 + (n - 8) * S:1024 + (n - 7) * S]
                act.activation(src, src, ACT.Exp, bias=nfx[:, n:n + 1], accum_out=rfx[:, n:n + 1]).then_inc(sg("fx_exp"), 1)
            upper([(sg("fx_done"), 1)] * 4)
            segment(U_BR, BR_UNITS)
            upper([(sg("merged"), KT // 2)] * 4, sga)
            segment(U_OUT2, OUT_UNITS)
            wait_units(U_Q)
            act.wait_ge(lin_lo, 4 * 5)
            norm_squares(4, X)
            norm_root(4)
            upper([(lin_src, 12 + q + 1) for q in range(4)])
            segment(U_Q, OUT_UNITS)
            for t in range(TT):
                act.wait_ge(sg("gate_arg"), t + 1)
                act.activation(gt[:], gt[:], ACT.Exp).then_inc(sg("gate_exp"), 1)
            def gather_pair(tg):
                for b in range(2):
                    if not isinstance(tg, int):
                        act.wait_ge(sg(f"gate_store{b}"), tg * 16)
                    for q in range(4):
                        act.wait_ge(sg("gate_mm"), tg * 32 + (16 * b + 4 * q + 4))
                        act.activation(gst[:, b, :, 4 * q:4 * q + 4].rearrange("p e t -> p t e"),
                                       ps[:, q, :].rearrange("p (t e) -> p t e", t=4), ACT.Copy).then_inc(sg("gate_out"), 1)
                    act.wait_ge(sg("gate_out"), tg * 8 + (4 * b + 4))
                    act.dma_start(g_dram[bass.ds(tg * 2 + b, 1)].rearrange("a p n -> p (a n)"),
                                  gst[:, b, :, :].rearrange("p e t -> p (e t)")).then_inc(sg(f"gate_store{b}"), 16)
            gather_pair(0)
            with act.Fori(1, 8) as tg:
                gather_pair(tg)
            for b in range(2):
                act.wait_ge(sg(f"gate_store{b}"), 8 * 16)

            def load_gates(e):
                act.dma_start(gch[:], g_dram[:, :, bass.ds(e * (KT * 16), KT * 16)].rearrange("g p n -> p g n")
                              ).then_inc(sg("gate_in"), 16)

            def up(e):
                with act.Fori(0, KT // RING) as i:
                    for j in range(RING):
                        u = e * CHUNK_UNITS + i * RING
                        conv_wait_and_split(u, j + 1)
                        act.wait_ge(pe_half, u * 2 + (2 * (U_EXP + j) + 2))
                        act.wait_ge(sg("hid"), e * KT + i * RING + max(j, 1))
                        act.activation(act_u[:, j % 2, :], unit_ps[:, j % 2, 0:S], ACT.Gelu_apprx_tanh).then_inc(evac[j % 2], 1)

            def conv_wait_and_split(u, d):
                j = d % RING
                act.wait_ge(raw_in[j], u * 4 + 16 * ((U_EXP + d) // RING + 1))
                for h in range(2):
                    act.wait_ge(pe_half, u * 2 + (2 * (U_EXP + d) + h - 3))
                    act.activation(whi[:, (2 * j + h) % 4, :, :], raw[:, j, h * HALF:(h + 1) * HALF, :],
                                   ACT.Copy).then_inc(hi_ready, 1)

            def down(e, first, quads):
                with act.Fori(first, quads) as i:
                    for j in range(RING):
                        conv_wait_and_split(e * CHUNK_UNITS + i * RING + KT, j + 1)

            load_gates(0)
            with act.Fori(0, EXPERT_CHUNKS - 1) as e:
                up(e)
                down(e, 0, 1)
                act.wait_ge(sg("hid"), e * KT + (KT + 1))
                load_gates(e + 1)
                down(e, 1, KT // RING)
            up(EXPERT_CHUNKS - 1)
            down(EXPERT_CHUNKS - 1, 0, KT // RING - 1)
            for d in range(3):
                conv_wait_and_split((EXPERT_CHUNKS - 1) * CHUNK_UNITS + KT + KT - RING, d + 1)
            wait_units(U_END)
            norm_squares(5, X)
            norm_root(5)
            act.wait_ge(sg("result"), 1)
            act.dma_start(out, T16[:]).then_inc(out_st, 16)
            act.wait_ge(out_st, 16)

        @block.vector
        def _(dve):
            step = Chain(dve, v_chain)

            def norm(n, src, gain, dst, done=None):
                dve.wait_ge(norm_sum, n + 1)
                dve.tensor_scalar(rstd[:], psf[:, 0:S], 1.0 / D, EPS, ALU.mult, ALU.add).then_inc(norm_var, 1)
                dve.wait_ge(norm_std, n + 1)
                step(dve.reciprocal(rstd[:], rstd[:]))
                for k in range(KT):
                    ins = dve.scalar_tensor_tensor(dst[:, k, :], src[:, k, :], gains[:, gain, k:k + 1], rstd[:],
                                                   ALU.mult, ALU.mult)
                    if done is None and k % 4 == 3:
                        ins.then_inc(lin_src, 1)
                if done is not None:
                    ins.then_inc(done, 1)

            def lower(n, src=T16):
                for q in range(4):
                    dve.wait_ge(lin_hi, 4 * n + q + 1)
                    dve.tensor_tensor(xlo[:, 4 * q:4 * q + 4, :], src[:, 4 * q:4 * q + 4, :],
                                      xhi[:, 4 * q:4 * q + 4, :].bitcast(F32), ALU.subtract).then_inc(lin_lo, 1)

            def segment(u0, n, body):
                with dve.Fori(0, n // RING) as i:
                    for j in range(RING):
                        dve.wait_ge(pe_half, i * 8 + (2 * (u0 + j) + 2))
                        body(i, j).then_inc(evac[j % 2], 1)

            def blk(t, i, j):
                return t[:, bass.ds(i * RING + j, 1), :]

            def into(dst, scale=None):
                def body(i, j):
                    src = unit_ps[:, j % 2:j % 2 + 1, 0:S]
                    if scale is None:
                        return dve.tensor_copy(blk(dst, i, j), src)
                    return dve.tensor_scalar(blk(dst, i, j), src, scale, None, ALU.mult)
                return body

            def add_to_x(i, j):
                return dve.tensor_tensor(blk(X, i, j), unit_ps[:, j % 2:j % 2 + 1, 0:S], blk(X, i, j), ALU.add)

            dve.memset(stage[:], 0.0).then_inc(sg("stage_zero"), 1)
            dve.wait_ge(cst_in, 16 * 7)
            dve.wait_ge(mem_ld, 16)
            norm(0, mem_in, G_MEM, T16)
            lower(0)
            segment(U_KV, 4, into(mk))
            segment(U_KV + 4, 4, into(mvf))
            dve.wait_ge(evac[0], KV_UNITS // 2)
            dve.wait_ge(evac[1], KV_UNITS // 2)
            dve.wait_ge(x_ld, 16)
            dve.wait_ge(sg("mv_t"), 1)
            dve.tensor_copy(mvt[:].rearrange("p a h n -> p (a h n)"), psf[:, 1024:2048]).then_inc(sg("kv_done"), 1)
            norm(1, X, G_LN, T16)
            lower(1)
            segment(U_IN, 4, into(cq, SCALE))

            dve.wait_ge(sg("stage_zero"), 1)

            def conv(i):
                for j in range(RING):
                    s = stage[:, j % 2, :]
                    w = lambda k: cw[:, bass.ds(i * RING + j, 1), k:k + 1].rearrange("p a k -> p (a k)")
                    y = ycv[:, j % 2, :]
                    dve.wait_ge(pe_half, i * 8 + (2 * (U_IN + 28 + j) + 2))
                    dve.tensor_copy(s[:, TAPS - 1:], unit_ps[:, j % 2, 0:S]).then_inc(evac[j % 2], 1)
                    dve.wait_ge(evac[j % 2], i * 2 + ((U_IN + 28) // 2 + j // 2 + 1))
                    if j >= 2 or not isinstance(i, int):
                        dve.wait_ge(conv_used, i * 4 + (j - 1))
                    step(dve.tensor_scalar(y, s[:, 0:S], w(0), None, ALU.mult))
                    for k in range(1, TAPS):
                        ins = dve.scalar_tensor_tensor(y, s[:, k:k + S], w(k), y, ALU.mult, ALU.add)
                        if k < TAPS - 1:
                            step(ins)
                        else:
                            ins.then_inc(conv_y, 1)

            conv(0)
            step.loop(1, 6, 12, conv)

            sc4 = psf[:, 1024:3072].rearrange("p (n m) -> p n m", m=S)
            dve.wait_ge(sg("xa_scores"), 1)
            dve.tensor_reduce(nx[:, 0:8], sc4, AX, ALU.max, negate=True).then_inc(sg("xa_max"), 1)
            dve.wait_ge(sg("xa_exp"), 8)
            step(dve.reciprocal(rs[:, 0:8], rs[:, 0:8]))
            dve.tensor_tensor(xa_p[:], xa_p[:], rs[:, 0:8].unsqueeze(2).broadcast_to([P, 8, S]), ALU.mult).then_inc(sg("xa_norm"), 1)
            dve.wait_ge(sg("xa_pt_mm"), 1)
            dve.tensor_copy(xa_pt[:].rearrange("p h a n -> p (h a n)"), psf[:, 1024:3072]).then_inc(sg("xa_pt"), 1)
            dve.wait_ge(sg("xa_out"), 1)
            step(dve.tensor_tensor(mixed[:, 12:16, :].rearrange("p h n -> p (h n)"), psf[:, 0:1024],
                                   mixed[:, 12:16, :].rearrange("p h n -> p (h n)"), ALU.mult))
            dve.wait_ge(sg("ln_sum"), 1)
            step(dve.tensor_scalar(mean[:], psf[:, 1024:1024 + S], 1.0 / (GROUPS * P), None, ALU.mult))
            dve.tensor_tensor(gv[:], gv[:], mean[:].unsqueeze(1).broadcast_to([P, GROUPS, S]), ALU.subtract).then_inc(sg("ln_centred"), 1)
            dve.wait_ge(sg("ln_sqsum"), 1)
            dve.tensor_scalar(rstd[:], psf[:, 1536:1536 + S], 1.0 / (GROUPS * P), EPS, ALU.mult, ALU.add).then_inc(sg("ln_var"), 1)
            dve.wait_ge(sg("ln_std"), 1)
            step(dve.reciprocal(rstd[:], rstd[:]))
            step(dve.tensor_tensor(gv[:], gv[:], rstd[:].unsqueeze(1).broadcast_to([P, GROUPS, S]), ALU.mult))
            for g in range(GROUPS):
                ins = dve.tensor_scalar(gv[:, g, :], gv[:, g, :], small[:, 5 + g:6 + g], small[:, 9 + g:10 + g], ALU.mult, ALU.add)
            ins.then_inc(sg("ln_out"), 1)
            dve.wait_ge(ws_ld, 32)
            dve.tensor_tensor(wst[:], wst[:], c(TRI_LE).unsqueeze(1).broadcast_to([P, GROUPS, P]), ALU.mult).then_inc(sg("ws_masked"), 1)
            dve.wait_ge(sg("v_t"), 1)
            dve.tensor_copy(vt[:].rearrange("p g a n -> p (g a n)"), psf[:, 0:1024]).then_inc(sg("v_tc"), 1)
            dve.wait_ge(sg("sgu"), 1)
            oa = mixed[:, 0:4, :].rearrange("p g n -> p (g n)")
            step(dve.tensor_tensor(oa, psf[:, 1024:2048], oa, ALU.mult))
            step(dve.tensor_tensor(oa, oa, gz[:].rearrange("p g n -> p (g n)"), ALU.mult))

            dve.wait_ge(sg("ab_mm"), 1)
            dve.tensor_scalar(gb8[:, 0, :], psf[0:8, 0:S], small[0:8, 0:1], None, ALU.add).then_inc(sg("ab_in"), 1)
            dve.wait_ge(sg("softplus"), 1)
            step(dve.scalar_tensor_tensor(gb8[:, 0, :], gb8[:, 0, :], 0.0, tm8[:, 0, :], ALU.max, ALU.add))
            dve.tensor_scalar(gb8[:, 0, :], gb8[:, 0, :], small[0:8, 4:5], -1.0, ALU.mult, ALU.mult).then_inc(sg("g_row"), 1)
            dve.wait_ge(sg("beta"), 1)
            dve.tensor_copy(bt8[:], gb8[:, 1, :]).then_inc(sg("beta_kept"), 1)
            for w in range(2):
                dst = qkv[:, 8 - 8 * w:16 - 8 * w, :].rearrange("p h n -> p (h n)")
                flat = qt[:].rearrange("p a n -> p (a n)")
                dve.wait_ge(sg("qk_ss"), w + 1)
                dve.tensor_scalar(flat, psf[:, 1024:3072], EPS, None, ALU.add).then_inc(sg("qk_var"), 1)
                dve.wait_ge(sg("qk_std"), w + 1)
                step(dve.reciprocal(flat, flat))
                if w == 0:
                    dve.tensor_tensor(dst, dst, flat, ALU.mult).then_inc(sg("qk_scaled"), 1)
                else:
                    dve.scalar_tensor_tensor(dst, flat, SCALE, dst, ALU.mult, ALU.mult).then_inc(sg("qk_scaled"), 1)
            dve.wait_ge(sg("gb_t"), 1)
            dve.tensor_copy(gbt[:].rearrange("p a b h -> p (a b h)"), psf[:, 0:32]).then_inc(sg("gbt"), 1)
            dve.wait_ge(sg("gsum_mm"), 1)
            step(dve.tensor_copy(gc8[:], psf[0:8, 512:512 + S]))
            dve.tensor_copy(gcol[:].rearrange("p a b h -> p (a b h)"), psf[:, 768:800]).then_inc(sg("gcol_in"), 1)
            dve.wait_ge(sg("ecol"), 1)
            step(dve.tensor_tensor(bex[:], gbt[:, :, 1, :], ecol[:, :, 0, :], ALU.mult))
            dve.wait_ge(sg("row_bc"), 1)
            for h in range(8):
                for t in range(TT):
                    dve.tensor_scalar(dec[:, 2 * h + t, :], psf[:, 1024 + h * S + t * P:1024 + h * S + (t + 1) * P],
                                      gcol[:, t, 0, h:h + 1], 0.0, ALU.subtract, ALU.min).then_inc(sg("dec_arg"), 1)
            dve.wait_ge(sg("dec_exp"), 1)
            step(dve.tensor_tensor(dec[:], dec[:], c(C64_LE).unsqueeze(1).broadcast_to([P, 16, P]), ALU.mult))
            dve.wait_ge(sg("exp_row"), 1)
            step(dve.tensor_copy(egl[:], expr[:].rearrange("p h (c n) -> p h c n", n=CHUNK)[:, :, :, CHUNK - 1]))
            dve.wait_ge(sg("k_t"), 1)
            pk = psf[:, 1024:3072].rearrange("p (h a n) -> p h a n", h=8, a=2)

            def cols(t):
                return t.rearrange("p a h -> p h a").unsqueeze(3).broadcast_to([P, 8, TT, P])

            v4 = lambda t: t[:].rearrange("p (h a) n -> p h a n", a=2)
            for t in range(TT):
                step(dve.tensor_tensor(v4(kbg)[:, :, t, :], pk[:, :, t, :], bex[:, t, :].unsqueeze(2).broadcast_to([P, 8, P]), ALU.mult))
                ins = dve.tensor_tensor(v4(kd)[:, :, t, :], pk[:, :, t, :], ecol[:, t, 1, :].unsqueeze(2).broadcast_to([P, 8, P]), ALU.mult)
                if t == 0:
                    step(ins)
                else:
                    ins.then_inc(sg("k_tok"), 1)
            dve.wait_ge(sg("v_dt"), 1)
            for t in range(TT):
                ins = dve.tensor_tensor(v4(vb)[:, :, t, :], pk[:, :, t, :], gbt[:, t, 1, :].unsqueeze(2).broadcast_to([P, 8, P]), ALU.mult)
                if t == 0:
                    step(ins)
                else:
                    ins.then_inc(sg("v_tok"), 1)
            f3 = lambda t: t[:].rearrange("p a n -> p (a n)")
            dve.wait_ge(sg("kk"), 1)
            dve.tensor_tensor(f3(at_), psf[:, 1024:3072], f3(dec), ALU.mult).then_inc(sg("kk_out"), 1)
            dve.wait_ge(sg("qk"), 1)
            dve.tensor_tensor(f3(ait), psf[:, 1024:3072], f3(dec), ALU.mult).then_inc(sg("qk_out"), 1)
            qf = qkv[:, 0:8, :].rearrange("p h n -> p (h n)")
            step(dve.tensor_tensor(qf, qf, expr[:].rearrange("p h n -> p (h n)"), ALU.mult))
            dve.wait_ge(sg("beta_bc"), 1)
            step(dve.tensor_tensor(f3(at_), psf[:, 1024:3072], f3(at_), ALU.mult))
            step(dve.tensor_copy(pt[:], ident.unsqueeze(1).broadcast_to([P, 16, P])))
            step(dve.tensor_copy(qt[:], ident.unsqueeze(1).broadcast_to([P, 16, P])))

            def level(lev):
                for g in range(4):
                    m = cst[:, bass.ds(lev + LEVEL0, 1), :].broadcast_to([P, 4, P])
                    dve.tensor_tensor(dec[:, 4 * g:4 * g + 4, :], at_[:, 4 * g:4 * g + 4, :], m, ALU.mult).then_inc(sg("inv_a"), 1)
                for g in range(4):
                    b = 3 * (g % 2)
                    pg, qg = (t[:, 4 * g:4 * g + 4, :].rearrange("p a n -> p (a n)") for t in (pt, qt))
                    dve.wait_ge(sg("inv_pq"), lev * 4 + (g + 1))
                    step(dve.tensor_tensor(pg, pg, ps[:, b + 1, :], ALU.subtract))
                    dve.tensor_tensor(qg, qg, ps[:, b + 2, :], ALU.subtract).then_inc(sg("inv_upd"), 1)

            step.loop(0, LEVELS, 4, level)
            for cch in range(CHUNKS):
                po = CHUNK * (cch % 2)
                pr = slice(po, po + CHUNK)
                dve.wait_ge(sg("vnew_mm"), cch + 1)
                dve.tensor_copy(vn[pr].rearrange("p h n -> p (h n)"), psf[pr, 0:1024]).then_inc(sg("vnew"), 1)
                dve.wait_ge(sg("o_mm"), cch + 1)
                ins = dve.tensor_copy(odn[:, :, cch * CHUNK:(cch + 1) * CHUNK], ps[:, 2, :].rearrange("p (h n) -> p h n", h=8))
                ins.then_inc(sg("odn_full") if cch == CHUNKS - 1 else sg("o_out"), 1)
                if cch < CHUNKS - 1:
                    dve.wait_ge(sg("ds_mm"), cch + 1)
                    if cch == 0:
                        dve.tensor_copy(st[:].rearrange("p h n -> p (h n)"), psf[:, 1536:2560]).then_inc(sg("state"), 1)
                    else:
                        for h in range(8):
                            ins = dve.scalar_tensor_tensor(st[:, h, :], st[:, h, :], egl[:, h, cch:cch + 1],
                                                           psf[:, 1536 + h * P:1536 + (h + 1) * P], ALU.mult, ALU.add)
                        ins.then_inc(sg("state"), 1)
            dve.wait_ge(sg("odn_ss"), 1)
            dve.tensor_scalar(f3(qt), psf[:, 1024:3072], 1.0 / P, EPS, ALU.mult, ALU.add).then_inc(sg("odn_var"), 1)
            dve.wait_ge(sg("odn_std"), 1)
            of = odn[:].rearrange("p h n -> p (h n)")
            ob = mixed[:, 4:12, :].rearrange("p h n -> p (h n)")
            step(dve.reciprocal(f3(qt), f3(qt)))
            step(dve.scalar_tensor_tensor(of, of, small[:, 3:4], f3(qt), ALU.mult, ALU.mult))
            dve.tensor_tensor(ob, ob, of, ALU.mult).then_inc(sg("mixed_done"), 1)

            lower(2, mixed)
            segment(U_OUT, OUT_UNITS, add_to_x)
            norm(2, X, G_FINAL, X, sg("x2_done"))
            dve.wait_ge(sg("x2_done"), 1)
            norm(3, X, G_MIX, T16)
            lower(3)
            dve.wait_ge(lin_lo, 16)
            segment(U_IN2 + 32, 8, into(qa, SCALE))
            segment(U_IN2 + 40, 8, into(ka))
            segment(U_IN2 + 48, 8, into(va))
            segment(U_IN2 + 56, 8, into(qb, SCALE))
            segment(U_IN2 + 64, 8, into(kb))
            segment(U_IN2 + 72, 8, into(vb2))

            dve.wait_ge(sg("f_mm"), 1)
            dve.tensor_scalar(f8[:], psf[0:8, 0:S], small[0:8, 2:3], None, ALU.add).then_inc(sg("f_in"), 1)
            dve.wait_ge(sg("f_ln"), 1)
            dve.scalar_tensor_tensor(f8[:], f8[:], 0.0, ft8[:], ALU.min, ALU.subtract).then_inc(sg("log_f"), 1)
            dve.wait_ge(sg("f_t"), 1)
            dve.tensor_copy(fcol[:].rearrange("p a h -> p (a h)"), psf[:, 512:528]).then_inc(sg("f_col"), 1)
            dve.wait_ge(sg("cumf_mm"), 1)
            step(dve.tensor_scalar(ft8[:], psf[0:8, 1024:1024 + S], -1.0, None, ALU.mult))
            dve.tensor_copy(cf8[:], psf[0:8, 1024:1024 + S]).then_inc(sg("cumf"), 1)

            fa, fb = (t[:].rearrange("p h n -> p (h n)") for t in (za, zb))
            strict = c(TRI_LT).unsqueeze(1).broadcast_to([P, 8, P])
            dve.wait_ge(sg("sb_ln"), 1)
            step(dve.scalar_tensor_tensor(fa, psf, 0.0, fa, ALU.max, ALU.add))
            step(dve.tensor_tensor(fb, psf, fa, ALU.subtract))
            d0 = lambda f: f[:, 0:2048].rearrange("p (h n) -> p h n", h=8)[:, :, 0:P]
            d1 = lambda f: f[:, 2048:3072].rearrange("p (h n) -> p h n", h=8)
            step(dve.tensor_tensor(d0(fa), d0(fa), strict, ALU.mult))
            dve.tensor_tensor(d1(fa), d1(fa), strict, ALU.mult).then_inc(sg("sb_sp"), 1)
            dve.wait_ge(sg("sb_suffix"), 1)
            dve.tensor_tensor(fb, fb, psf, ALU.subtract).then_inc(sg("sb_arg"), 1)
            dve.wait_ge(sg("sb_exp"), 1)
            step(dve.tensor_tensor(d0(fb), d0(fb), strict, ALU.mult))
            dve.tensor_tensor(d1(fb), d1(fb), strict, ALU.mult).then_inc(sg("sb_w"), 1)
            vk = vtk[:].rearrange("p h a n -> p (h a n)")
            dve.wait_ge(sg("sb_vt_mm"), 1)
            dve.tensor_copy(vk, psf[:, 0:2048]).then_inc(sg("sb_vt"), 1)
            dve.wait_ge(sg("sb_out"), 1)
            dve.tensor_copy(T16[:, 0:8, :].rearrange("p h n -> p (h n)"), psf[:, 0:2048]).then_inc(sg("sb_done"), 1)

            later = c(TRI_LT).unsqueeze(1).broadcast_to([P, 8, P])
            l0 = lambda f: f[:, 0:1024].rearrange("p (h n) -> p h n", h=8)
            l1 = lambda f, x: f[:, 1024:3072].rearrange("p (h n) -> p h n", h=8)[:, :, x * P:(x + 1) * P]
            dve.wait_ge(sg("fx_logits"), 1)
            step(dve.scalar_tensor_tensor(l0(fa), later, NEG_INF, l0(psf), ALU.mult, ALU.add))
            step(dve.scalar_tensor_tensor(l1(fa, 1), later, NEG_INF, l1(psf, 1), ALU.mult, ALU.add))
            step(dve.tensor_copy(l1(fa, 0), l1(psf, 0)))
            step(dve.tensor_reduce(nfx[:, 0:8], l0(fa), AX, ALU.max, negate=True))
            dve.tensor_reduce(nfx[:, 8:16], fa[:, 1024:3072].rearrange("p (h n) -> p h n", h=8), AX, ALU.max, negate=True).then_inc(sg("fx_max"), 1)
            dve.wait_ge(sg("fx_exp"), 16)
            step(dve.reciprocal(rfx[:], rfx[:]))
            step(dve.tensor_tensor(l0(fa), l0(fa), rfx[:, 0:8].unsqueeze(2).broadcast_to([P, 8, P]), ALU.mult))
            f1 = fa[:, 1024:3072].rearrange("p (h n) -> p h n", h=8)
            dve.tensor_tensor(f1, f1, rfx[:, 8:16].unsqueeze(2).broadcast_to([P, 8, S]), ALU.mult).then_inc(sg("fx_p"), 1)
            dve.wait_ge(sg("fx_pt_mm"), 1)
            dve.tensor_copy(fb, psf).then_inc(sg("fx_pt"), 1)
            dve.wait_ge(sg("fx_vt_mm"), 1)
            dve.tensor_copy(vk, psf[:, 0:2048]).then_inc(sg("fx_vt"), 1)
            dve.wait_ge(sg("fx_out"), 1)
            dve.tensor_copy(T16[:, 8:16, :].rearrange("p h n -> p (h n)"), psf[:, 0:2048]).then_inc(sg("fx_done"), 1)

            lower(4)
            with dve.Fori(0, BR_UNITS // 2) as i:
                ga = sga[:, bass.ds(i * 2, 2), :].rearrange("p a n -> p (a n)")
                gb = sgb[:, bass.ds(i * 2, 2), :].rearrange("p a n -> p (a n)")
                dve.wait_ge(pe_half, i * 4 + (2 * U_BR + 2))
                dve.tensor_tensor(ga, unit_ps[:, 0, :], ga, ALU.mult).then_inc(evac[0], 1)
                dve.wait_ge(pe_half, i * 4 + (2 * U_BR + 4))
                dve.tensor_tensor(gb, unit_ps[:, 1, :], gb, ALU.mult).then_inc(evac[1], 1)
                dve.wait_ge(evac[1], i + (U_BR // 2 + 1))
                dve.tensor_tensor(ga, ga, gb, ALU.add).then_inc(sg("merged"), 1)
            lower(5, sga)
            segment(U_OUT2, OUT_UNITS, add_to_x)
            norm(4, X, G_FFN, T16)
            lower(6)
            dve.wait_ge(lin_lo, 28)
            segment(U_Q, OUT_UNITS, into(T16))

            def top16(vals, idx, src, work):
                step(dve.max(vals[:, 0:8], src))
                step(dve.max_index(idx[:, 0:8], vals[:, 0:8], src))
                step(dve.match_replace(work, vals[:, 0:8], src, -3.0e38))
                step(dve.max(vals[:, 8:16], work))
                step(dve.max_index(idx[:, 8:16], vals[:, 8:16], work))

            for t in range(TT):
                dve.wait_ge(sg("key_scores"), t + 1)
                dve.tensor_copy(sc[:].rearrange("p a n -> p (a n)"), psf[:, 0:2048]).then_inc(sg("key_out"), 1)
                dve.wait_ge(sg("key_out"), t + 1)
                for hp in range(16):
                    top16(v16[:, hp, :], i16[:, hp, :], sc[:, hp, :], sc2[:, hp, :])
                step(dve.tensor_copy(if16[:], i16[:]))
                v4_ = v16[:].rearrange("p (h two) k -> p h two k", two=2)
                i4_ = if16[:].rearrange("p (h two) k -> p h two k", two=2)
                for h in range(8):
                    step(dve.tensor_tensor(cand[:, h, :].rearrange("p (i j) -> p i j", i=TOPK),
                                           v4_[:, h, 0, :].unsqueeze(2).broadcast_to([P, TOPK, TOPK]),
                                           v4_[:, h, 1, :].unsqueeze(1).broadcast_to([P, TOPK, TOPK]), ALU.add))
                for h in range(8):
                    top16(ts[:, h, :], ti[:, h, :], cand[:, h, :], cand2[:, h, :])
                step(dve.tensor_scalar(th[:], ti[:], 4, None, ALU.logical_shift_right))
                step(dve.tensor_scalar(tl[:], ti[:], 15, None, ALU.bitwise_and))
                step(dve.tensor_copy(thf[:], th[:]))
                step(dve.tensor_copy(tlf[:], tl[:]))
                iota16 = cst[:, IOTA, 0:TOPK].unsqueeze(1).broadcast_to([P, P, TOPK])
                c3 = cand[:].rearrange("p h (k j) -> p (h k) j", j=TOPK)
                c4 = cand[:].rearrange("p h (k j) -> p h k j", j=TOPK)
                for half, (pos, dst) in enumerate(((thf, e1), (tlf, e2))):
                    step(dve.tensor_tensor(c3, iota16, pos[:].rearrange("p h k -> p (h k)").unsqueeze(2).broadcast_to([P, P, TOPK]), ALU.is_equal))
                    step(dve.tensor_tensor(c4, c4, i4_[:, :, half, :].unsqueeze(2).broadcast_to([P, 8, TOPK, TOPK]), ALU.mult))
                    step(dve.tensor_reduce(dst[:], c3, AX, ALU.add))
                dve.tensor_tensor(gt[:], ts[:], ts[:, :, 0:1].broadcast_to([P, 8, TOPK]), ALU.subtract).then_inc(sg("gate_arg"), 1)
                dve.wait_ge(sg("gate_exp"), t + 1)
                step(dve.tensor_reduce(gs[:], gt[:], AX, ALU.add))
                step(dve.reciprocal(gs[:], gs[:]))
                dve.tensor_tensor(gt[:], gt[:], gs[:].unsqueeze(2).broadcast_to([P, 8, TOPK]), ALU.mult).then_inc(sg("picks"), 1)
                dve.wait_ge(sg("picks_t"), t + 1)
                dve.tensor_copy(sel[:, :, t * P:(t + 1) * P], psf[:, 2048:2048 + 3 * P].rearrange("p (a n) -> p a n", a=3)).then_inc(sg("sel"), 1)
            dve.wait_ge(sg("sel"), 2)

            def onehots(q4):
                for b in range(4):
                    col = lambda a: sel[:, a, bass.ds(q4 * 4 + b, 1)]
                    if not isinstance(q4, int):
                        dve.wait_ge(sg("gate_mm"), q4 * 4 + (b - 3))
                    dve.tensor_scalar(oh1[:, b, :], c(IOTA), col(0), col(2), ALU.is_equal, ALU.mult).then_inc(sg("oh1"), 1)
                    dve.tensor_scalar(oh2[:, b, :], c(IOTA), col(1), None, ALU.is_equal).then_inc(sg("oh"), 1)
            onehots(0)
            with dve.Fori(1, S // 4) as q4:
                onehots(q4)
            def up(e):
                with dve.Fori(0, KT // RING) as i:
                    for j in range(RING):
                        dst = lambda t: t[:, bass.ds(i * RING + j, 1), :].rearrange("p a n -> p (a n)")
                        g = gch[:, :, bass.ds(i * RING + j, 1), :].rearrange("p g a n -> p g (a n)")
                        w = wt[:, j % 2, :]
                        dve.wait_ge(evac[j % 2], e * KT + i * 2 + (U_EXP // 2 + j // 2 + 1))
                        if j == 0:
                            dve.wait_ge(sg("gate_in"), e * 16 + 16)
                        dve.tensor_tensor(w.rearrange("p (g n) -> p g n", g=16), act_u[:, j % 2, :].rearrange("p (g n) -> p g n", g=16), g, ALU.mult).then_inc(sg("hid"), 1)
                        dve.wait_ge(sg("hid"), e * KT + i * RING + (j + 2))
                        dve.tensor_copy(dst(whid), w).then_inc(sg("hid_hi"), 1)
                        dve.wait_ge(sg("hid_hi"), e * KT + i * RING + (j + 1))
                        dve.tensor_tensor(dst(wlod), w, dst(whid).bitcast(F32), ALU.subtract).then_inc(sg("hid_lo"), 1)

            def down(e):
                with dve.Fori(0, KT // RING) as i:
                    for j in range(RING):
                        dve.wait_ge(pe_half, e * (2 * CHUNK_UNITS) + i * 8 + (2 * (U_EXP + KT + j) + 2))
                        add_to_x(i, j).then_inc(evac[j % 2], 1)

            dve.wait_ge(sg("gate_mm"), S)
            dve.memset(wt[:], 0.0).then_inc(sg("hid"), 1)
            with dve.Fori(0, EXPERT_CHUNKS) as e:
                up(e)
                down(e)
            norm(5, X, G_OUT, T16, sg("result"))

        @block.tensor
        def _(pe):
            def mm(o, lhsT, rhs, start=True, stop=True, **k):
                return nc.tensor.matmul(o, lhsT, rhs, start=start, stop=stop, **k)

            def unit_body(u, j, hi, lo, par, paired=False):
                s0 = (2 * j) % 4
                o = unit_ps[:, j % 2, :]
                if not (isinstance(par, int) and par == 0):
                    pe.wait_ge(evac[j % 2], par)
                for h in range(2):
                    pe.wait_ge(lo_ready, u * 2 + (2 * j + h + 1))
                    for k in range(HALF):
                        if paired:
                            x = k + HALF * (j % 2)
                            oo, first, last = o[:, h * S:(h + 1) * S], k == 0, k == HALF - 1
                        else:
                            x = h * HALF + k
                            oo, first, last = o[:, 0:S], h == 0 and k == 0, h == 1 and k == HALF - 1
                        a, b = whi[:, s0 + h, k, :], wlo[:, s0 + h, k, :]
                        mm(oo, a, hi[:, x, :], start=first, stop=False)
                        mm(oo, a, lo[:, x, :], start=False, stop=False)
                        z = mm(oo, b, hi[:, x, :], start=False, stop=last)
                    z.then_inc(pe_half, 1)

            def segment(u0, n, paired=False):
                first = int(u0 == 0)
                for j in range(2 * first):
                    unit_body(0, j, xhi, xlo, 0)
                with pe.Fori(first, n // 2) as i:
                    for j in range(2):
                        unit_body(i * 2 + u0, j, xhi, xlo, i + u0 // 2, paired)

            def norm_sums(n):
                for k in range(KT):
                    pe.wait_ge(norm_sq, 4 * n + k // 4 + 1)
                    z = mm(psf[:, 0:S], ones, T16[:, k, :], k == 0, k == KT - 1)
                z.then_inc(norm_sum, 1)

            def tr(o, i, idn=None):
                return nc.tensor.transpose(o, i, ident if idn is None else idn)

            pe.wait_ge(cst_in, 16 * 7)
            norm_sums(0)
            pe.wait_ge(lin_lo, 4)
            segment(U_KV, KV_UNITS)
            pe.wait_ge(evac[0], KV_UNITS // 2)
            pe.wait_ge(evac[1], KV_UNITS // 2)
            for t in range(TT):
                for h in range(XA_HEADS):
                    z = tr(psf[:, 1024 + (t * 4 + h) * P:1024 + (t * 4 + h + 1) * P], mvf[:, h, t * P:(t + 1) * P])
            z.then_inc(sg("mv_t"), 1)
            norm_sums(1)
            pe.wait_ge(lin_lo, 8)
            segment(U_IN, IN_UNITS)

            pe.wait_ge(evac[0], (U_IN + IN_UNITS) // 2)
            pe.wait_ge(evac[1], (U_IN + IN_UNITS) // 2)
            pe.wait_ge(sg("kv_done"), 1)
            for h in range(XA_HEADS):
                for t in range(TT):
                    n = 2 * h + t
                    z = mm(psf[:, 1024 + n * S:1024 + (n + 1) * S], cq[:, h, t * P:(t + 1) * P], mk[:, h, :])
            z.then_inc(sg("xa_scores"), 1)
            pe.wait_ge(sg("xa_norm"), 1)
            for h in range(XA_HEADS):
                for m in range(TT):
                    for t in range(TT):
                        z = tr(psf[:, 1024 + (2 * h + m) * S + t * P:1024 + (2 * h + m) * S + (t + 1) * P],
                               xa_p[:, 2 * h + t, m * P:(m + 1) * P])
            z.then_inc(sg("xa_pt_mm"), 1)
            pe.wait_ge(sg("xa_pt"), 1)
            for h in range(XA_HEADS):
                for m in range(TT):
                    z = mm(psf[:, h * S:(h + 1) * S], mvt[:, m, h, :], xa_pt[:, h, m, :], m == 0, m == TT - 1)
            z.then_inc(sg("xa_out"), 1)
            for g in range(GROUPS):
                z = mm(psf[:, 1024:1024 + S], ones, gv[:, g, :], g == 0, g == GROUPS - 1)
            z.then_inc(sg("ln_sum"), 1)
            pe.wait_ge(sg("ln_sq"), 1)
            for g in range(GROUPS):
                z = mm(psf[:, 1536:1536 + S], ones, vsq[:, g, :], g == 0, g == GROUPS - 1)
            z.then_inc(sg("ln_sqsum"), 1)
            pe.wait_ge(sg("ln_out"), 1)
            for g in range(GROUPS):
                for t in range(TT):
                    z = tr(psf[:, (2 * g + t) * P:(2 * g + t + 1) * P], gv[:, g, t * P:(t + 1) * P])
            z.then_inc(sg("v_t"), 1)
            pe.wait_ge(sg("v_tc"), 1)
            pe.wait_ge(sg("ws_masked"), 1)
            for g in range(GROUPS):
                for t in range(TT):
                    o = psf[:, 1024 + (2 * g + t) * P:1024 + (2 * g + t + 1) * P]
                    mm(o, vt[:, g, t, :], wst[:, g, :], True, False)
                    z = mm(o, ones[0:1, :], bs_row[0:1, g * P:(g + 1) * P], False, True)
            z.then_inc(sg("sgu"), 1)

            for col, x in ((0, 0), (8, 1)):
                for k in range(KT):
                    for n, src in enumerate((xhi, xlo)):
                        z = mm(psf[0:8, x * S:(x + 1) * S], wab[:, k, col:col + 8], src[:, k, :].bitcast(F32),
                               k == 0 and n == 0, k == KT - 1 and n == 1)
            z.then_inc(sg("ab_mm"), 1)
            for w in range(2):
                pe.wait_ge(sg("qk_sq"), w + 1)
                for h in range(8):
                    z = mm(psf[:, 1024 + h * S:1024 + (h + 1) * S], ones, pt[:, 2 * h:2 * h + 2, :].rearrange("p a n -> p (a n)"))
                z.then_inc(sg("qk_ss"), 1)
            pe.wait_ge(sg("beta_kept"), 1)
            for t in range(TT):
                for x in range(2):
                    z = tr(psf[:, (2 * t + x) * 8:(2 * t + x + 1) * 8], gb8[:, x, t * P:(t + 1) * P], ident[0:8, 0:8])
            z.then_inc(sg("gb_t"), 1)
            pe.wait_ge(sg("gbt"), 1)
            for t in range(TT):
                mm(psf[0:8, 512 + t * P:512 + (t + 1) * P], gbt[:, t, 0, :], c(C64_LE))
            for t in range(TT):
                for x, m in enumerate((C64_LE, C64_GT)):
                    z = mm(psf[:, 768 + (2 * t + x) * 8:768 + (2 * t + x + 1) * 8], c(m), gbt[:, t, 0, :])
            z.then_inc(sg("gsum_mm"), 1)
            pe.wait_ge(sg("gcol_in"), 1)
            pe.wait_ge(sg("qk_scaled"), 2)
            for h in range(8):
                z = mm(psf[:, 1024 + h * S:1024 + (h + 1) * S], ident[0:8, h:h + 1].to_broadcast([8, P]), gc8[:, :])
            z.then_inc(sg("row_bc"), 1)
            pe.wait_ge(sg("dec_arg"), 16)
            pe.wait_ge(sg("exp_row"), 1)
            for n in range(16):
                z = tr(psf[:, 1024 + n * P:1024 + (n + 1) * P], qkv[:, 8 + n // 2, (n % 2) * P:(n % 2 + 1) * P])
            z.then_inc(sg("k_t"), 1)
            pe.wait_ge(sg("k_tok"), 1)
            for n in range(16):
                z = tr(psf[:, 1024 + n * P:1024 + (n + 1) * P], qkv[:, 16 + n // 2, (n % 2) * P:(n % 2 + 1) * P])
            z.then_inc(sg("v_dt"), 1)
            pe.wait_ge(sg("v_tok"), 1)
            for n in range(16):
                kk = qkv[:, 8 + n // 2, (n % 2) * P:(n % 2 + 1) * P]
                z = mm(psf[:, 1024 + n * P:1024 + (n + 1) * P], kk, kk)
            z.then_inc(sg("kk"), 1)
            pe.wait_ge(sg("kk_out"), 1)
            for n in range(16):
                sl = slice((n % 2) * P, (n % 2 + 1) * P)
                z = mm(psf[:, 1024 + n * P:1024 + (n + 1) * P], qkv[:, 8 + n // 2, sl], qkv[:, n // 2, sl])
            z.then_inc(sg("qk"), 1)
            pe.wait_ge(sg("qk_out"), 1)
            for h in range(8):
                z = mm(psf[:, 1024 + h * S:1024 + (h + 1) * S], ident[0:8, h:h + 1].to_broadcast([8, P]), bt8[:, :])
            z.then_inc(sg("beta_bc"), 1)

            def inv_x(lev, g):
                pe.wait_ge(sg("inv_a"), lev * 4 + 4)
                for n in range(4 * g, 4 * g + 4):
                    z = mm(ps[:, 3 * (g % 2), (n % 4) * P:(n % 4 + 1) * P], dec[:, n, :], pt[:, n, :])
                z.then_inc(sg("inv_x"), 1)

            def inv_pq(lev, g):
                pe.wait_ge(sg("inv_xc"), lev * 4 + (g + 1))
                for n in range(4 * g, 4 * g + 4):
                    mm(ps[:, 3 * (g % 2) + 1, (n % 4) * P:(n % 4 + 1) * P], qt[:, n, :], xt[:, n, :])
                for n in range(4 * g, 4 * g + 4):
                    z = mm(ps[:, 3 * (g % 2) + 2, (n % 4) * P:(n % 4 + 1) * P], xt[:, n, :], qt[:, n, :])
                z.then_inc(sg("inv_pq"), 1)

            with pe.Fori(0, LEVELS) as lev:
                inv_x(lev, 0)
                inv_x(lev, 1)
                for g in range(4):
                    inv_pq(lev, g)
                    if g < 2:
                        pe.wait_ge(sg("inv_xc"), lev * 4 + (g + 1))
                        pe.wait_ge(sg("inv_upd"), lev * 4 + (g + 1))
                        inv_x(lev, g + 2)
                pe.wait_ge(sg("inv_upd"), lev * 4 + 4)
            for n in range(16):
                z = mm(psf[:, n * P:(n + 1) * P], kbg[:, n, :], qt[:, n, :])
            z.then_inc(sg("kcd_mm"), 1)
            pe.wait_ge(sg("kcd"), 1)
            for cch in range(CHUNKS):
                t, po = cch // 2, CHUNK * (cch % 2)
                pr = slice(po, po + CHUNK)
                if cch:
                    pe.wait_ge(sg("state"), cch)
                for h in range(8):
                    o = psf[pr, h * P:(h + 1) * P]
                    z = mm(o, qt[pr, 2 * h + t, pr], vb[pr, 2 * h + t, :], True, cch == 0)
                    if cch:
                        z = mm(o, kcd[:, 2 * h + t, pr], st[:, h, :], False, True)
                z.then_inc(sg("vnew_mm"), 1)
                pe.wait_ge(sg("vnew"), cch + 1)
                if cch:
                    pe.wait_ge(sg("o_out"), cch)
                for h in range(8):
                    o = ps[:, 2, h * CHUNK:(h + 1) * CHUNK]
                    if cch:
                        mm(o, st[:, h, :], qkv[:, h, cch * CHUNK:(cch + 1) * CHUNK], True, False)
                    z = mm(o, vn[pr, h, :], ait[pr, 2 * h + t, pr], cch == 0, True)
                z.then_inc(sg("o_mm"), 1)
                if cch < CHUNKS - 1:
                    for h in range(8):
                        z = mm(psf[:, 1536 + h * P:1536 + (h + 1) * P], kd[pr, 2 * h + t, :], vn[pr, h, :])
                    z.then_inc(sg("ds_mm"), 1)
            pe.wait_ge(sg("odn_sq"), 1)
            for h in range(8):
                z = mm(psf[:, 1024 + h * S:1024 + (h + 1) * S], ones, pt[:, 2 * h:2 * h + 2, :].rearrange("p a n -> p (a n)"))
            z.then_inc(sg("odn_ss"), 1)

            pe.wait_ge(lin_lo, 12)
            segment(U_OUT, OUT_UNITS)
            norm_sums(2)
            norm_sums(3)
            pe.wait_ge(lin_lo, 16)
            segment(U_IN2, IN2_UNITS)

            def wait_units(u):
                pe.wait_ge(evac[0], u // 2)
                pe.wait_ge(evac[1], u // 2)

            wait_units(U_BR)
            for k in range(KT):
                for n, src in enumerate((xhi, xlo)):
                    z = mm(psf[0:8, 0:S], wab[:, k, 16:24], src[:, k, :].bitcast(F32), k == 0 and n == 0, k == KT - 1 and n == 1)
            z.then_inc(sg("f_mm"), 1)
            pe.wait_ge(sg("log_f"), 1)
            for t in range(TT):
                z = tr(psf[:, 512 + 8 * t:520 + 8 * t], f8[:, t * P:(t + 1) * P], ident[0:8, 0:8])
            z.then_inc(sg("f_t"), 1)
            pe.wait_ge(sg("f_col"), 1)
            mm(psf[0:8, 1024:1024 + P], fcol[:, 0, :], c(TRI_LE))
            mm(psf[0:8, 1024 + P:1024 + S], fcol[:, 0, :], ones, True, False)
            mm(psf[0:8, 1024 + P:1024 + S], fcol[:, 1, :], c(TRI_LE), False, True).then_inc(sg("cumf_mm"), 1)
            pe.wait_ge(sg("cumf"), 1)

            def tile(t, n):
                return slice(n * P, (n + 1) * P)

            def values_by_token(v, done):
                for n in range(16):
                    z = tr(psf[:, n * P:(n + 1) * P], v[:, n // 2, (n % 2) * P:(n % 2 + 1) * P])
                z.then_inc(done, 1)

            def weighted_values(w, done):
                for h in range(HEADS):
                    mm(psf[:, h * S:(h + 1) * S], vtk[:, h, 0, :], w[:, h * S:(h + 1) * S], True, False)
                    z = mm(psf[:, h * S + P:(h + 1) * S], vtk[:, h, 1, :], w[:, 2048 + h * P:2048 + (h + 1) * P], False, True)
                z.then_inc(done, 1)

            fa, fb = (t[:].rearrange("p h n -> p (h n)") for t in (za, zb))
            for h in range(HEADS):
                mm(psf[:, h * S:(h + 1) * S], ka[:, h, 0:P], qa[:, h, :])
            for h in range(HEADS):
                z = mm(psf[:, 2048 + h * P:2048 + (h + 1) * P], ka[:, h, P:S], qa[:, h, P:S])
            z.then_inc(sg("sb_z"), 1)
            pe.wait_ge(sg("sb_sp"), 1)
            for h in range(HEADS):
                later = fa[:, 2048 + h * P:2048 + (h + 1) * P]
                mm(psf[:, h * S:(h + 1) * S], c(TRI_GT), fa[:, h * S:(h + 1) * S], True, False)
                mm(psf[:, h * S + P:(h + 1) * S], ones, later, False, True)
            for h in range(HEADS):
                z = mm(psf[:, 2048 + h * P:2048 + (h + 1) * P], c(TRI_GT), fa[:, 2048 + h * P:2048 + (h + 1) * P])
            z.then_inc(sg("sb_suffix"), 1)
            pe.wait_ge(sg("sb_arg"), 1)
            values_by_token(va, sg("sb_vt_mm"))
            pe.wait_ge(sg("sb_w"), 1)
            pe.wait_ge(sg("sb_vt"), 1)
            weighted_values(fb, sg("sb_out"))
            pe.wait_ge(sg("sb_done"), 1)
            for h in range(HEADS):
                pick = ident[0:8, h:h + 1]
                for t, o, n in ((0, psf[:, h * P:(h + 1) * P], P), (1, psf[:, 1024 + h * S:1024 + (h + 1) * S], S)):
                    sl = slice(t * P, (t + 1) * P)
                    mm(o, qb[:, h, sl], kb[:, h, 0:n], True, False)
                    mm(o, cf8[:, sl], pick.to_broadcast([8, n]), False, False)
                    z = mm(o, pick.to_broadcast([8, P]), ft8[:, 0:n], False, True)
            z.then_inc(sg("fx_logits"), 1)
            pe.wait_ge(sg("fx_p"), 1)
            for h in range(HEADS):
                tr(psf[:, h * S:h * S + P], fa[:, h * P:(h + 1) * P])
                tr(psf[:, h * S + P:(h + 1) * S], fa[:, 1024 + h * S:1024 + h * S + P])
                z = tr(psf[:, 2048 + h * P:2048 + (h + 1) * P], fa[:, 1024 + h * S + P:1024 + (h + 1) * S])
            z.then_inc(sg("fx_pt_mm"), 1)
            pe.wait_ge(sg("fx_pt"), 1)
            values_by_token(vb2, sg("fx_vt_mm"))
            pe.wait_ge(sg("fx_vt"), 1)
            weighted_values(fb, sg("fx_out"))

            pe.wait_ge(lin_lo, 20)
            segment(U_BR, BR_UNITS, paired=True)
            pe.wait_ge(lin_lo, 24)
            segment(U_OUT2, OUT_UNITS)
            norm_sums(4)
            pe.wait_ge(lin_lo, 28)
            segment(U_Q, OUT_UNITS)

            wait_units(U_EXP)
            pe.wait_ge(sk_ld, 16)
            for t in range(TT):
                if t:
                    pe.wait_ge(sg("key_out"), t)
                for hp in range(16):
                    z = mm(psf[:, hp * P:(hp + 1) * P], T16[:, hp, t * P:(t + 1) * P], skt[:, hp, :])
                z.then_inc(sg("key_scores"), 1)
                pe.wait_ge(sg("picks"), t + 1)
                for n, x in enumerate((e1[:], e2[:], gt[:].rearrange("p h k -> p (h k)"))):
                    z = tr(psf[:, 2048 + n * P:2048 + (n + 1) * P], x)
                z.then_inc(sg("picks_t"), 1)

            def gates(g16):
                for q in range(4):
                    if not isinstance(g16, int):
                        pe.wait_ge(sg("gate_out"), g16 * 4 + (q - 3))
                    for b in range(4):
                        pe.wait_ge(sg("oh"), g16 * 16 + (4 * q + b + 1))
                        mm(ps[:, q, b * P:(b + 1) * P], oh2[:, b, :], oh1[:, b, :]).then_inc(sg("gate_mm"), 1)
            pe.wait_ge(sg("sel"), 2)
            gates(0)
            with pe.Fori(1, S // 16) as g16:
                gates(g16)

            with pe.Fori(0, EXPERT_CHUNKS) as e:
                with pe.Fori(0, KT // 2) as i:
                    for j in range(2):
                        unit_body(e * CHUNK_UNITS + i * 2 + U_EXP, j, xhi, xlo, e * KT + i + U_EXP // 2)
                with pe.Fori(0, KT // 2) as i:
                    for j in range(2):
                        pe.wait_ge(sg("hid_lo"), e * KT + KT)
                        unit_body(e * CHUNK_UNITS + i * 2 + (U_EXP + KT), j, whid, wlod, e * KT + i + (U_EXP + KT) // 2)
            norm_sums(5)


def kernel(**inputs):
    import numpy as np
    import concourse.bacc as bacc
    from concourse.bass_utils import run_bass_kernel_spmd

    def units(w):
        k, n = w.shape
        return w.reshape(k // P, P, n // P, P).transpose(2, 1, 0, 3).reshape(n // P, P, k)

    def features(x):
        return x.T.reshape(KT, P, S).transpose(1, 0, 2)

    def column(v):
        return v.reshape(-1, P).T

    x = {k: np.asarray(v) for k, v in inputs.items()}
    w = x["w_in"][0]
    cuts = np.cumsum([0, 512, 512, 512, 1024, 1024, 1024, 1024, 8, 8, 512, 512])
    seg = lambda i: w[:, cuts[i]:cuts[i + 1]]
    u, v, z, dq, dk, dv, dz, da, db, cq, cz = (seg(i) for i in range(11))
    w2 = x["w_in_2"][0]
    cuts2 = np.cumsum([0] + [1024] * 6 + [8, 2048, 2048])
    qa, ka, va, qb, kb, vb, fl, ga, gb = (w2[:, cuts2[i]:cuts2[i + 1]] for i in range(9))
    br = np.stack([x["w_branch_a_2"][0], x["w_branch_b_2"][0]])
    br = br.reshape(2, KT // 2, P, KT // 2, 2, P).transpose(3, 0, 2, 4, 1, 5).reshape(BR_UNITS, P, D)
    up = units(x["expert_u_2"][0].T).reshape(EXPERT_CHUNKS, KT, P, D)
    down = x["expert_v_2"][0].reshape(EXPERT_CHUNKS, KT, P, KT, P).transpose(0, 3, 2, 1, 4).reshape(EXPERT_CHUNKS, KT, P, D)
    small = np.stack([x["dn_dt_bias"][0], x["dn_a_log"][0], x["b_forget_2"][0]], 1)
    arrays = {
        "mem": features(x["mem"][0]),
        "x": features(x["x"][0]),
        "consts": shape_constants(),
        "gains": np.stack([column(x[n].reshape(-1)) for n in
                           ("mem_norm_g", "ln_g", "final_g", "norm_mix_gain_2", "norm_ffn_gain_2", "norm_final_gain_2")], 1),
        "conv": x["conv_w"][0].reshape(TAPS, 24, P).transpose(2, 1, 0),
        "w_abf": np.concatenate([da, db, fl], 1).reshape(KT, P, 24).transpose(1, 0, 2),
        "small8": small,
        "dn_g": x["dn_norm_g"][0].reshape(P, 1),
        "gmlp_ln": np.concatenate([column(x["gmlp_ln_g"][0]), column(x["gmlp_ln_b"][0])], 1),
        "ws": x["gmlp_ws"][0].transpose(2, 0, 1),
        "bs": x["gmlp_bs"][0].reshape(1, GROUPS * P),
        "sub_keys": x["sub_keys_2"][0].reshape(16, P, P).transpose(2, 0, 1),
        "w_kv": units(x["w_mem_kv"][0]),
        "w_in": units(np.concatenate([cq, cz, z, dz, u, v, dq, dk, dv], 1)),
        "w_out": units(x["w_out"][0]),
        "w_in2": units(np.concatenate([ga, gb, qa, ka, va, qb, kb, vb], 1)),
        "w_br": br,
        "w_out2": units(x["w_out_2"][0]),
        "w_q": units(x["w_query_2"][0]),
        "w_exp": np.concatenate([up, down], 1).reshape(EXPERT_CHUNKS * CHUNK_UNITS, P, D),
    }
    arrays = {k: np.ascontiguousarray(v) for k, v in arrays.items()}
    nc = bacc.Bacc("TRN2", target_bir_lowering=False, num_devices=1)
    ap = {k: nc.dram_tensor(f"in_{k}", v.shape, mybir.dt.from_np(v.dtype), kind="ExternalInput").ap() for k, v in arrays.items()}
    out = nc.dram_tensor("out", (P, KT, S), F32, kind="ExternalOutput").ap()
    g_dram = nc.dram_tensor("gates", (16, P, P * 16), F32, kind="Internal").ap()
    program(nc, ap, out, g_dram)
    r = run_bass_kernel_spmd(nc, [{f"in_{k}": v for k, v in arrays.items()}], core_ids=[0])
    y = r.results[0]["out"]
    return y.transpose(2, 1, 0).reshape(1, S, D)
```

```python
import concourse.bass as bass
from concourse import mybir
from concourse.alu_op_type import AluOpType as ALU
from contextlib import ExitStack

F32 = mybir.dt.float32
F32R = mybir.dt.float32r
U32 = mybir.dt.uint32
ACT = mybir.ActivationFunctionType
AX = mybir.AxisListType.X

P = 128
D = 2048
KT = D // P
S = 256
TT = S // P
EPS = 1e-6
SCALE = float(P) ** -0.5
NEG_INF = -1e30
DN_HEADS = 8
HEADS = 8
XA_HEADS = 4
GROUPS = 4
CHUNK = 64
CHUNKS = S // CHUNK
LEVELS = 6
TAPS = 4
TOPK = 16
RING = 4
HALF = KT // 2
ONEHOTS = 16
GATE_GROUPS = (1, 1, 2) * 4

KV_UNITS, IN_UNITS, OUT_UNITS, IN2_UNITS, BR_UNITS = 8, 52, KT, 80, KT // 2 * 2
EXPERT_CHUNKS = 8
CHUNK_UNITS = 2 * KT
U_KV = 0
U_IN = U_KV + KV_UNITS
U_OUT = U_IN + IN_UNITS
U_IN2 = U_OUT + OUT_UNITS
U_BR = U_IN2 + IN2_UNITS
U_OUT2 = U_BR + BR_UNITS
U_Q = U_OUT2 + OUT_UNITS
U_EXP = U_Q + OUT_UNITS
U_END = U_EXP + EXPERT_CHUNKS * CHUNK_UNITS
AHEAD = 3

IDENT, ONES, TRI_LE, TRI_LT, TRI_GT, C64_LE, C64_GT, IOTA, LEVEL0 = range(9)
NCONST = LEVEL0 + LEVELS
G_MEM, G_LN, G_FINAL, G_MIX, G_FFN, G_OUT = range(6)


def shape_constants():
    import numpy as np
    a, b = np.arange(P)[:, None], np.arange(P)[None, :]
    same = (a // CHUNK) == (b // CHUNK)
    rows = [a == b, a >= 0 * b, a <= b, a < b, a > b, same & (a <= b), same & (a > b), 0 * a + b]
    for lev in range(LEVELS):
        s = 1 << lev
        rows.append((a // (2 * s) == b // (2 * s)) & (a // s < b // s))
    return np.ascontiguousarray(np.stack([(r + 0 * b).astype(np.float32) for r in rows], 1))


def expert_order():
    order = [("up", e) for e in range(AHEAD)] + [("down", 0)]
    for e in range(AHEAD, EXPERT_CHUNKS):
        order += [("up", e), ("down", e - AHEAD + 1)]
    return order + [("down", e) for e in range(EXPERT_CHUNKS - AHEAD + 1, EXPERT_CHUNKS)]


ORDER = expert_order()


def first_unit(kind, e):
    return U_EXP + KT * ORDER.index((kind, e))


class Chain:

    def __init__(self, eng, sem):
        self.eng, self.sem, self.n, self.steps = eng, sem, 0, 0

    def __call__(self, ins):
        ins.then_inc(self.sem, 1)
        self.n = self.n + 1
        self.steps += 1
        self.eng.wait_ge(self.sem, self.n)

    def loop(self, start, end, per, body):
        base, s0 = self.n, self.steps
        with self.eng.Fori(start, end) as i:
            self.n = i * per + (base - start * per)
            body(i)
        assert self.steps - s0 == per, (self.steps - s0, per)
        self.n = base + (end - start) * per


def program(nc, ap, out, g_dram):
    ctx = ExitStack()
    with ctx:
        base = [16512]

        def at(name, shape, off, dt=F32):
            return nc.alloc_sbuf_tensor_at(name, shape, dt, offset=off)

        def take(nbytes):
            off = base[0]
            base[0] += (nbytes + 31) // 32 * 32
            assert base[0] <= 229344, base[0]
            return off

        def sem(name):
            return ctx.enter_context(nc.semaphore(name))

        K = 1024
        raw = at("raw", [P, RING, KT, P], take(32 * K))
        whi = at("whi", [P, 4, HALF, P], take(16 * K), F32R)
        wlo = at("wlo", [P, 4, HALF, P], take(16 * K), F32R)
        X = at("X", [P, KT, S], take(16 * K))
        o_T = take(16 * K)
        T16 = at("T16", [P, KT, S], o_T)
        o_hi, o_lo = take(16 * K), take(16 * K)
        xhi = at("xhi", [P, KT, S], o_hi, F32R)
        xlo = at("xlo", [P, KT, S], o_lo, F32R)
        cst = at("cst", [P, NCONST, P], take(NCONST * 512))
        gains = at("gains", [P, 6, KT], take(6 * KT * 4))
        cw = at("cw", [P, 24, TAPS], take(24 * TAPS * 4))
        wab_hi = at("wab_hi", [P, KT, 24], take(KT * 24 * 4), F32R)
        wab_lo = at("wab_lo", [P, KT, 24], take(KT * 24 * 4), F32R)
        small = at("small", [P, 48], take(192))
        rstd = at("rstd", [P, S], take(S * 4))
        o_A = base[0]
        A = lambda k: o_A + int(k * K)

        def c(n):
            return cst[:, n, :]

        ab_bias, a_log, f_bias, eps = small[:, 16:32], small[:, 32:40], small[:, 40:48], small[:, 9:10]

        ident = c(IDENT)
        ones = c(ONES)

        mixed = at("mixed", [P, KT, S], A(0))
        qkv = at("qkv", [P, 24, S], A(16))
        cq = at("cq", [P, XA_HEADS, S], A(40))
        gv = at("gv", [P, GROUPS, S], A(44))
        gz = at("gz", [P, GROUPS, S], A(48))
        mk = at("mk", [P, XA_HEADS, S], A(52))
        mvt = at("mvt", [P, TT, XA_HEADS, P], A(56))
        stage = at("stage", [P, 2, S + TAPS - 1], A(60))
        ycv = at("ycv", [P, 2, S], A(62.25))
        mem_in = at("mem_in", [P, KT, S], A(16))
        wab = at("wab", [P, KT, 24], A(44))
        mvf = at("mvf", [P, XA_HEADS, S], A(32))
        xa_p = at("xa_p", [P, 8, S], o_T)
        xa_pt = at("xa_pt", [P, XA_HEADS, TT, S], o_T + 8 * K)
        vt = at("vt", [P, GROUPS, TT, P], o_T)
        vsq = at("vsq", [P, GROUPS, S], o_T + 4 * K)
        wst = at("wst", [P, GROUPS, P], A(60))
        bs_row = at("bs_row", [1, GROUPS * P], A(62))
        mean = at("mean", [P, S], o_T + 12 * K)
        kbg = at("kbg", [P, 16, P], o_hi)
        kd = at("kd", [P, 16, P], o_hi + 8 * K)
        at_ = at("at_", [P, 16, P], o_lo)
        ait = at("ait", [P, 16, P], o_lo + 8 * K)
        pt = at("pt", [P, 16, P], o_T)
        qt = at("qt", [P, 16, P], o_T + 8 * K)
        dec = at("dec", [P, 16, P], A(40))
        xt = at("xt", [P, 16, P], A(48))
        expr = at("expr", [P, 8, S], A(48))
        st = at("st", [P, 8, P], A(48))
        vn = at("vn", [P, 8, P], A(52))
        odn = at("odn", [P, 8, S], o_lo)
        vb = at("vb", [P, 16, P], A(32))
        kcd = at("kcd", [P, 16, P], A(24))
        sm = A(64.5)
        nx = at("nx", [P, 16], sm)
        rs = at("rs", [P, 16], sm + 64)
        gbt = at("gbt", [P, TT, 2, 8], sm + 128)
        gcol = at("gcol", [P, TT, 2, 8], sm + 256)
        ecol = at("ecol", [P, TT, 2, 8], sm + 384)
        bex = at("bex", [P, TT, 8], sm + 512)
        gc8 = at("gc8", [8, S], sm + 640)
        bt8 = at("bt8", [8, S], sm + 640 + K)
        ab16 = at("ab16", [16, S], sm + 640)
        egl = at("egl", [P, 8, CHUNKS], sm + 640 + 2 * K)
        splus = at("splus", [P, TT, 8], sm + 768 + 2 * K)
        decay = at("decay", [P, 8], sm + 832 + 2 * K)
        qk_sq = [at("k_sq", [P, 8, S], o_lo), at("q_sq", [P, 8, S], o_hi)]
        qk_rs = [at("k_rs", [P, 8, S], o_lo + 8 * K), at("q_rs", [P, 8, S], o_hi + 8 * K)]
        qa = at("qa", [P, 8, S], o_T)
        ka = at("ka", [P, 8, S], o_T + 8 * K)
        va = at("va", [P, 8, S], A(0))
        qb = at("qb", [P, 8, S], A(8))
        kb = at("kb", [P, 8, S], A(16))
        vb2 = at("vb2", [P, 8, S], A(24))
        sga = at("sga", [P, KT, S], A(32))
        sgb = at("sgb", [P, KT, S], A(48))
        za = at("za", [P, 8, 384], o_hi)
        zb = at("zb", [P, 8, 384], o_hi + 12 * K)
        vtk = at("vtk", [P, 8, TT, P], o_hi + 24 * K)
        nfx = at("nfx", [P, 16], sm)
        rfx = at("rfx", [P, 16], sm + 64)
        fl = at("fl", [P, TT, 8], sm + 128)
        fcol = at("fcol", [P, TT, 8], sm + 192)
        f8 = at("f8", [8, S], sm + 128 + K)
        ft8 = at("ft8", [8, S], sm + 128 + K)
        cf8 = at("cf8", [8, S], sm + 128 + 2 * K)
        skt = at("skt", [P, 16, P], A(16))
        picks = at("picks", [P, TT, 3, P], A(24))
        sc = at("sc", [P, TT, 16, P], A(32))
        cand = at("cand", [P, 8, S], A(48))
        v16 = at("v16", [P, 16, TOPK], A(56))
        i16 = at("i16", [P, 16, TOPK], A(57), U32)
        if16 = at("if16", [P, 16, TOPK], A(58))
        ts = at("ts", [P, 8, TOPK], A(59))
        ti = at("ti", [P, 8, TOPK], A(59.5), U32)
        th = at("th", [P, 8, TOPK], A(60), U32)
        tl = at("tl", [P, 8, TOPK], A(60.5), U32)
        thf = at("thf", [P, 8, TOPK], A(61))
        tlf = at("tlf", [P, 8, TOPK], A(61.5))
        gs = at("gs", [P, 8], A(62))
        rest = at("rest", [P, 2 * P], A(63))
        sel = at("sel", [P, 3, S], A(64.25))
        oh1 = at("oh1", [P, ONEHOTS, P], A(48))
        oh2 = at("oh2", [P, ONEHOTS, P], A(56))
        gst = at("gst", [P, 2, P, 16], A(32))
        offs = (o_T, A(0), A(16))
        hidden = [at(f"hidden{n}", [P, KT, S], o) for n, o in enumerate(offs)]
        hid_lower = [at(f"hid_lower{n}", [P, KT, S], o, F32R) for n, o in enumerate(offs)]
        hid_upper = at("hid_upper", [P, KT, S], A(32), F32R)
        gch = at("gch", [P, 16, KT, 16], A(48))

        banks = ctx.enter_context(nc.psum_tensor("banks", [P, 8, 512], F32))
        unit_ps = banks[:, 0:2, :]
        ps = banks[:, 2:8, :]
        psf = ps.rearrange("p b n -> p (b n)")
        ps_a = banks[:, 4:8, :].rearrange("p b n -> p (b n)")
        ps_b = banks[:, 0:4, :].rearrange("p b n -> p (b n)")

        raw_in = [sem(f"raw_in{r}") for r in range(RING)]
        hi_ready, lo_ready, pe_half = sem("hi_ready"), sem("lo_ready"), sem("pe_half")
        evac = [sem("evac0"), sem("evac1")]
        v_chain, a_chain = sem("v_chain"), sem("a_chain")
        cst_in, mem_ld, x_ld, ws_ld, sk_ld, out_st = (sem(n) for n in ("cst_in", "mem_ld", "x_ld", "ws_ld", "sk_ld", "out_st"))
        norm_sq, norm_sum, norm_std = (sem(n) for n in ("norm_sq", "norm_sum", "norm_std"))
        lin_src, lin_hi, lin_lo, lin_lo2 = sem("lin_src"), sem("lin_hi"), sem("lin_lo"), sem("lin_lo2")
        conv_y, conv_used = sem("conv_y"), sem("conv_used")
        signals = {}

        def sg(name):
            if name not in signals:
                signals[name] = sem(name)
            return signals[name]


        def gated(e):
            up = hid_upper if e < EXPERT_CHUNKS - 2 else (xhi, xlo)[e % 2]
            return up, hid_lower[e % 3]

        def pq(g):
            two = banks[:, 6:8, :] if g % 2 == 0 else banks[:, 0:2, :]
            return two[:, 0, :], two[:, 1, :]

        block = ctx.enter_context(nc.Block())

        @block.sync
        def _(sp):
            sp.dma_start(mem_in[:], ap["mem"]).then_inc(mem_ld, 16)
            sp.dma_start(cst[:], ap["consts"]).then_inc(cst_in, 16)
            sp.dma_start(gains[:], ap["gains"]).then_inc(cst_in, 16)
            sp.dma_start(cw[:], ap["conv"]).then_inc(cst_in, 16)
            sp.dma_start(wab[:], ap["w_abf"]).then_inc(cst_in, 16)
            sp.dma_start(small[:, 0:1], ap["dn_g"]).then_inc(cst_in, 16)
            sp.dma_start(small[:, 1:9], ap["gmlp_ln"]).then_inc(cst_in, 16)
            sp.dma_start(small[:, 16:48], ap["head_rows"]).then_inc(cst_in, 16)
            sp.dma_start(X[:], ap["x"]).then_inc(x_ld, 16)

            def load(src, u0, i, j):
                lead = i * 8 + (2 * (u0 + j) - 6)
                if not (isinstance(lead, int) and lead <= 0):
                    sp.wait_ge(lo_ready, lead)
                n = i * RING + j
                sp.dma_start(raw[:, j, :, :].rearrange("p k m -> p (k m)"),
                             src[bass.ds(n, 1)].rearrange("a p n -> p (a n)")).then_inc(raw_in[j], 16)

            def stream(src, n, u0, first=0):
                with sp.Fori(first, n // RING) as i:
                    for j in range(RING):
                        load(src, u0, i, j)

            for i in range(KV_UNITS // RING):
                for j in range(RING):
                    load(ap["w_kv"], U_KV, i, j)
            stream(ap["w_in"], IN_UNITS, U_IN)
            for j in range(RING):
                load(ap["w_out"], U_OUT, 0, j)
            sp.wait_ge(conv_used, 24)
            sp.dma_start(wst[:], ap["ws"]).then_inc(ws_ld, 16)
            sp.dma_start(bs_row[:], ap["bs"]).then_inc(ws_ld, 16)
            stream(ap["w_out"], OUT_UNITS, U_OUT, 1)
            stream(ap["w_in2"], IN2_UNITS, U_IN2)
            stream(ap["w_br"], BR_UNITS, U_BR)
            stream(ap["w_out2"], OUT_UNITS, U_OUT2)
            sp.wait_ge(lin_lo2, 2 * 6)
            sp.dma_start(skt[:], ap["sub_keys"]).then_inc(sk_ld, 16)
            stream(ap["w_q"], OUT_UNITS, U_Q)
            stream(ap["w_exp"], EXPERT_CHUNKS * CHUNK_UNITS, U_EXP)

        @block.gpsimd
        def _(pool):
            def lower(n):
                with pool.Fori(0, n) as i:
                    for j in range(RING):
                        for h in range(2):
                            s = (2 * j + h) % 4
                            pool.wait_ge(hi_ready, i * 8 + (2 * j + h + 1))
                            pool.tensor_tensor(wlo[:, s, :, :], raw[:, j, h * HALF:(h + 1) * HALF, :],
                                               whi[:, s, :, :].bitcast(F32), ALU.subtract).then_inc(lo_ready, 1)

            lower(U_END // RING)

        @block.scalar
        def _(act):
            step = Chain(act, a_chain)

            def conv_unit(i, u0, d):
                j = d % RING
                act.wait_ge(raw_in[j], i * 16 + 16 * ((u0 + d) // RING + 1))
                for h in range(2):
                    lead = i * 8 + (2 * (u0 + d) + h - 3)
                    if not (isinstance(i, int) and lead <= 0):
                        act.wait_ge(pe_half, lead)
                    act.activation(whi[:, (2 * j + h) % 4, :, :], raw[:, j, h * HALF:(h + 1) * HALF, :],
                                   ACT.Copy).then_inc(hi_ready, 1)

            def segment(u0, n, body=None, first=False, after=None):
                def run(i):
                    for j in range(RING):
                        if u0 + j + 1 < U_END or not isinstance(i, int):
                            conv_unit(i, u0, j + 1)
                        if body:
                            body(i, j, u0)
                        if after and j in after:
                            after[j]()
                if after:
                    assert n == RING
                    return run(0)
                if first:
                    run(0)
                with act.Fori(1 if first else 0, n // RING) as i:
                    run(i)

            def into(dst, func):
                def body(i, j, u0):
                    act.wait_ge(pe_half, i * 8 + (2 * (u0 + j) + 2))
                    act.activation(dst[:, bass.ds(i * RING + j, 1), :], unit_ps[:, j % 2:j % 2 + 1, 0:S], func
                                   ).then_inc(evac[j % 2], 1)
                return body

            def wait_units(u):
                act.wait_ge(evac[0], u // 2)
                act.wait_ge(evac[1], u // 2)

            def norm_squares(n, src):
                for q in range(4):
                    act.activation(T16[:, 4 * q:4 * q + 4, :], src[:, 4 * q:4 * q + 4, :], ACT.Square).then_inc(norm_sq, 1)

            def residual_segment(n, u0):
                segment(u0, 8)
                for q in range(4):
                    act.wait_ge(evac[0], (u0 + 4 * q + 4) // 2)
                    act.wait_ge(evac[1], (u0 + 4 * q + 4) // 2)
                    act.activation(T16[:, 4 * q:4 * q + 4, :], X[:, 4 * q:4 * q + 4, :], ACT.Square).then_inc(norm_sq, 1)
                    if q < 1 or (q < 2 and u0 + KT < U_END):
                        segment(u0 + 8 + 4 * q, 4)
                    elif q == 1:
                        segment(u0 + 12, 4, after={3: lambda: None})

            def rsqrt_of(dst, sums, n):
                step(act.activation(dst, sums, ACT.Ln, scale=1.0 / n, bias=eps))
                return act.activation(dst, dst, ACT.Exp, scale=-0.5)

            def norm_root(n):
                act.wait_ge(norm_sum, n + 1)
                if n == 0:
                    act.wait_ge(sg("eps_set"), 1)
                rsqrt_of(rstd[:], psf[:, 0:S], D).then_inc(norm_std, 1)

            def upper(ready, src=T16):
                for q in range(4):
                    act.wait_ge(*ready[q])
                    act.activation(xhi[:, 4 * q:4 * q + 4, :], src[:, 4 * q:4 * q + 4, :], ACT.Copy).then_inc(lin_hi, 1)

            act.wait_ge(cst_in, 16 * 7)
            act.activation(wab_hi[:], wab[:], ACT.Copy).then_inc(sg("wab_hi"), 1)
            act.wait_ge(mem_ld, 16)
            norm_squares(0, mem_in)
            conv_unit(0, 0, 0)
            norm_root(0)
            upper([(lin_src, q + 1) for q in range(4)])
            segment(U_KV, KV_UNITS, first=True)
            act.wait_ge(x_ld, 16)
            act.wait_ge(lin_lo2, 2)
            norm_squares(1, X)
            norm_root(1)
            act.wait_ge(sg("kv_done"), 1)
            upper([(lin_src, 4 + q + 1) for q in range(4)])
            segment(U_IN, 4)
            cz = mixed[:, 12:16, :]
            segment(U_IN + 4, 4, into(cz, ACT.Silu))
            segment(U_IN + 8, 4, into(gz, ACT.Silu))
            act.wait_ge(sg("ab_in"), 1)
            step(act.activation(splus[:], gbt[:, :, 0, :], ACT.Abs))
            step(act.activation(splus[:], splus[:], ACT.Exp, scale=-1.0))
            step(act.activation(splus[:], splus[:], ACT.Ln, bias=1.0))
            act.activation(decay[:], a_log, ACT.Exp).then_inc(sg("softplus"), 1)
            act.activation(gbt[:, :, 1, :], gbt[:, :, 1, :], ACT.Sigmoid).then_inc(sg("beta"), 1)
            segment(U_IN + 12, 8, into(mixed[:, 4:12, :], ACT.Silu))
            act.wait_ge(sg("gcol_in"), 1)
            act.activation(ecol[:], gcol[:], ACT.Exp).then_inc(sg("ecol"), 1)
            segment(U_IN + 20, 4, into(mixed[:, 0:4, :], ACT.Gelu_apprx_tanh))
            segment(U_IN + 24, 4, into(gv, ACT.Gelu_apprx_tanh))

            def conv_quad(i):
                for j in range(RING):
                    conv_unit(i, U_IN + 28, j + 1)
                    if not (isinstance(i, int) and j == 0):
                        act.wait_ge(conv_y, i * 4 + j)
                        act.activation(qkv[:, bass.ds(i * RING + (j - 1), 1), :], ycv[:, (j + 1) % 2:(j + 1) % 2 + 1, :], ACT.Silu
                                       ).then_inc(conv_used, 1)

            conv_quad(0)
            with act.Fori(1, 6) as i:
                conv_quad(i)
            act.wait_ge(conv_y, 24)
            act.activation(qkv[:, 23, :], ycv[:, 1, :], ACT.Silu).then_inc(conv_used, 1)

            wait_units(U_OUT)
            for w in range(2):
                act.activation(qk_sq[w][:], qkv[:, 8 - 8 * w:16 - 8 * w, :], ACT.Square).then_inc(sg("qk_sq"), 1)

            def qk_ln(r):
                act.wait_ge(sg("qk_ss"), r + 1)
                act.activation(qk_rs[r // 2][:, 4 * (r % 2):4 * (r % 2) + 4, :].rearrange("p h n -> p (h n)"),
                               unit_ps.rearrange("p b n -> p (b n)"), ACT.Ln, bias=eps).then_inc(sg("qk_ln"), 1)

            def qk_exp(w):
                act.wait_ge(sg("qk_ln"), 2 * w + 2)
                act.activation(qk_rs[w][:], qk_rs[w][:], ACT.Exp, scale=-0.5).then_inc(sg("qk_rs"), 1)

            act.wait_ge(sg("xa_max"), 1)
            for n in range(8):
                act.activation(xa_p[:, n, :], psf[:, 1024 + n * S:1024 + (n + 1) * S], ACT.Exp, bias=nx[:, n:n + 1],
                               accum_out=rs[:, n:n + 1]).then_inc(sg("xa_exp"), 1)
            qk_ln(0)
            qk_ln(1)
            qk_exp(0)
            act.wait_ge(sg("ln_centred"), 1)
            act.activation(vsq[:], gv[:], ACT.Square).then_inc(sg("ln_sq"), 1)
            qk_ln(2)
            act.wait_ge(sg("ln_sqsum"), 1)
            rsqrt_of(rstd[:], psf[:, 1536:1536 + S], GROUPS * P).then_inc(sg("ln_std"), 1)
            qk_ln(3)
            qk_exp(1)
            act.wait_ge(sg("dec_arg"), 16)
            act.activation(expr[:].rearrange("p h n -> p (h n)"), ps_a, ACT.Exp).then_inc(sg("exp_row"), 1)
            act.activation(dec[:], dec[:], ACT.Exp).then_inc(sg("dec_exp"), 1)

            for g in range(4):
                act.wait_ge(sg("inv_p0"), g + 1)
                act.activation(pt[:, 4 * g:4 * g + 4, :].rearrange("p a n -> p (a n)"), ps[:, g, :], ACT.Copy
                               ).then_inc(sg("inv_upd"), 1)
            with act.Fori(1, LEVELS) as lev:
                for g in range(4):
                    act.wait_ge(sg("inv_x"), lev * 4 + (g - 3))
                    act.activation(xt[:, 4 * g:4 * g + 4, :].rearrange("p a n -> p (a n)"), ps[:, g, :], ACT.Copy
                                   ).then_inc(sg("inv_xc"), 1)
            act.wait_ge(sg("kcd_mm"), 1)
            act.activation(kcd[:].rearrange("p a n -> p (a n)"), psf[:, 0:2048], ACT.Copy, scale=-1.0).then_inc(sg("kcd"), 1)
            act.wait_ge(sg("odn_full"), 1)
            act.activation(pt[:], odn[:].rearrange("p h (t n) -> p (h t) n", t=2), ACT.Square).then_inc(sg("odn_sq"), 1)
            act.wait_ge(sg("odn_ss"), 1)
            rsqrt_of(qt[:].rearrange("p a n -> p (a n)"), ps_a, P).then_inc(sg("odn_std"), 1)

            upper([(sg("mixed_done"), 1)] * 4, mixed)
            residual_segment(2, U_OUT)
            norm_root(2)
            act.wait_ge(sg("x2_done"), 1)
            norm_squares(3, X)
            norm_root(3)
            upper([(lin_src, 8 + q + 1) for q in range(4)])
            segment(U_IN2, 16, into(sga, ACT.Sigmoid))
            segment(U_IN2 + 16, 16, into(sgb, ACT.Sigmoid))
            act.wait_ge(sg("f_in"), 1)
            step(act.activation(fl[:], fcol[:], ACT.Abs))
            step(act.activation(fl[:], fl[:], ACT.Exp, scale=-1.0))
            act.activation(fl[:], fl[:], ACT.Ln, bias=1.0).then_inc(sg("f_ln"), 1)
            segment(U_IN2 + 32, 48)
            act.wait_ge(sg("sb_z"), 1)
            flat_a = za[:].rearrange("p h n -> p (h n)")
            flat_b = zb[:].rearrange("p h n -> p (h n)")
            step(act.activation(flat_a, psf[:, 0:3072], ACT.Abs))
            step(act.activation(flat_a, flat_a, ACT.Exp, scale=-1.0))
            act.activation(flat_a, flat_a, ACT.Ln, bias=1.0).then_inc(sg("sb_ln"), 1)
            act.wait_ge(sg("sb_arg"), 1)
            act.activation(flat_b, flat_b, ACT.Exp).then_inc(sg("sb_exp"), 1)
            act.wait_ge(sg("fx_max"), 1)
            for n in range(16):
                src = flat_a[:, n * P:(n + 1) * P] if n < 8 else flat_a[:, 1024 + (n - 8) * S:1024 + (n - 7) * S]
                act.activation(src, src, ACT.Exp, bias=nfx[:, n:n + 1], accum_out=rfx[:, n:n + 1]).then_inc(sg("fx_exp"), 1)
            upper([(sg("fx_done"), 1)] * 4)
            segment(U_BR, BR_UNITS)
            upper([(sg("merged"), KT // 2)] * 4, sga)
            residual_segment(4, U_OUT2)
            norm_root(4)
            upper([(lin_src, 12 + q + 1) for q in range(4)])
            segment(U_Q, OUT_UNITS)
            def gather(g16):
                b = g16 % 2
                if g16 >= 2:
                    act.wait_ge(sg(f"gate_store{b}"), g16 // 2 * 16)
                for q in range(4):
                    act.wait_ge(sg("gate_mm"), g16 * 16 + (4 * q + 4))
                    act.activation(gst[:, b, :, 4 * q:4 * q + 4].rearrange("p e t -> p t e"),
                                   ps[:, q, :].rearrange("p (t e) -> p t e", t=4), ACT.Copy).then_inc(sg("gate_out"), 1)
                act.wait_ge(sg("gate_out"), g16 * 4 + 4)
                act.dma_start(g_dram[g16],
                              gst[:, b, :, :].rearrange("p e t -> p (e t)")).then_inc(sg(f"gate_store{b}"), 16)

            def load_gates(e):
                if e:
                    act.wait_ge(sg("gates_used"), 4 * e)
                else:
                    for b in range(2):
                        act.wait_ge(sg(f"gate_store{b}"), 8 * 16)
                act.dma_start(gch[:], g_dram[:, :, e * (KT * 16):(e + 1) * (KT * 16)].rearrange("g p n -> p g n")
                              ).then_inc(sg("gate_in"), 16)

            def exp_gates():
                act.wait_ge(sg("gate_arg"), 1)
                g3 = picks[:, :, 2, :]
                act.activation(g3, g3, ACT.Exp).then_inc(sg("gate_exp"), 1)

            for kind, e in ORDER:
                u0 = first_unit(kind, e)
                gelu = into(hidden[e % 3], ACT.Gelu_apprx_tanh) if kind == "up" else None
                quarter = lambda q, after: segment(u0 + 4 * q, 4, gelu and into_at(hidden[e % 3], 4 * q), after=after)
                into_at = lambda dst, k0: into(dst[:, k0:k0 + 4, :], ACT.Gelu_apprx_tanh)
                if (kind, e) == ("up", 1):
                    segment(u0, 12, gelu)
                    exp_gates()
                    quarter(3, {3: lambda: None})
                elif (kind, e) == ("up", 2):
                    done = 0
                    for q in range(3):
                        after = {}
                        for j in range(4):
                            n = GATE_GROUPS[4 * q + j]
                            after[j] = lambda g0=done, n=n: [gather(g) for g in range(g0, g0 + n)]
                            done += n
                        quarter(q, after)
                    quarter(3, {0: lambda: load_gates(0)})
                elif (kind, e) == ("up", EXPERT_CHUNKS - 1):
                    segment(u0, 12, gelu)
                    load_gates(EXPERT_CHUNKS - 2)
                    quarter(3, {3: lambda: None})
                elif kind == "up":
                    segment(u0, KT, gelu)
                elif e < EXPERT_CHUNKS - 3:
                    segment(u0, 4)
                    load_gates(e + 1)
                    segment(u0 + 4, 12)
                elif e == EXPERT_CHUNKS - 3:
                    segment(u0, 12)
                    quarter(3, {0: lambda: load_gates(EXPERT_CHUNKS - 1)})
                elif e == EXPERT_CHUNKS - 2:
                    segment(u0, KT)
                else:
                    residual_segment(5, u0)
            norm_root(5)
            act.wait_ge(sg("result"), 1)
            act.dma_start(out, T16[:]).then_inc(out_st, 16)
            act.wait_ge(out_st, 16)

        @block.vector
        def _(dve):
            step = Chain(dve, v_chain)

            def norm(n, src, gain, dst, low=None, done=None):
                dve.wait_ge(norm_std, n + 1)
                for k in range(KT):
                    ins = dve.scalar_tensor_tensor(dst[:, k, :], src[:, k, :], gains[:, gain, k:k + 1], rstd[:],
                                                   ALU.mult, ALU.mult)
                    if done is None and k % 4 == 3:
                        ins.then_inc(lin_src, 1)
                        if k == 11:
                            lower_half(low, 0)
                if done is not None:
                    ins.then_inc(done, 1)
                else:
                    lower_half(low, 1)

            def lower_half(n, half, src=T16):
                for q in (2 * half, 2 * half + 1):
                    dve.wait_ge(lin_hi, 4 * n + q + 1)
                    dve.tensor_tensor(xlo[:, 4 * q:4 * q + 4, :], src[:, 4 * q:4 * q + 4, :],
                                      xhi[:, 4 * q:4 * q + 4, :].bitcast(F32), ALU.subtract).then_inc((lin_lo, lin_lo2)[half], 1)

            def lower(n, src=T16):
                lower_half(n, 0, src)
                lower_half(n, 1, src)

            def segment(u0, n, body):
                with dve.Fori(0, n // RING) as i:
                    for j in range(RING):
                        dve.wait_ge(pe_half, i * 8 + (2 * (u0 + j) + 2))
                        body(i, j).then_inc(evac[j % 2], 1)

            def blk(t, i, j):
                return t[:, bass.ds(i * RING + j, 1), :]

            def into(dst, scale=None):
                def body(i, j):
                    src = unit_ps[:, j % 2:j % 2 + 1, 0:S]
                    if scale is None:
                        return dve.tensor_copy(blk(dst, i, j), src)
                    return dve.tensor_scalar(blk(dst, i, j), src, scale, None, ALU.mult)
                return body

            def add_to_x(i, j):
                return dve.tensor_tensor(blk(X, i, j), unit_ps[:, j % 2:j % 2 + 1, 0:S], blk(X, i, j), ALU.add)

            dve.memset(stage[:], 0.0).then_inc(sg("stage_zero"), 1)
            dve.wait_ge(cst_in, 16 * 7)
            dve.wait_ge(sg("wab_hi"), 1)
            dve.tensor_tensor(wab_lo[:], wab[:], wab_hi[:].bitcast(F32), ALU.subtract).then_inc(sg("wab_lo"), 1)
            dve.memset(eps, EPS).then_inc(sg("eps_set"), 1)
            dve.wait_ge(mem_ld, 16)
            norm(0, mem_in, G_MEM, T16, 0)
            segment(U_KV, 4, into(mk))
            segment(U_KV + 4, 4, into(mvf))
            dve.wait_ge(evac[0], KV_UNITS // 2)
            dve.wait_ge(evac[1], KV_UNITS // 2)
            dve.wait_ge(x_ld, 16)
            dve.wait_ge(sg("mv_t"), 1)
            dve.tensor_copy(mvt[:].rearrange("p a h n -> p (a h n)"), psf[:, 1024:2048]).then_inc(sg("kv_done"), 1)
            norm(1, X, G_LN, T16, 1)
            segment(U_IN, 4, into(cq, SCALE))
            dve.wait_ge(sg("ab_mm"), 1)
            dve.tensor_copy(ab16[:], psf[0:16, 0:S]).then_inc(sg("ab_row"), 1)
            dve.wait_ge(sg("ab_t"), 1)
            dve.tensor_tensor(gbt[:].rearrange("p a b h -> p a (b h)"), psf[:, S:S + 32].rearrange("p (a n) -> p a n", a=TT),
                              ab_bias.unsqueeze(1).broadcast_to([P, TT, 16]), ALU.add).then_inc(sg("ab_in"), 1)
            dve.wait_ge(sg("softplus"), 1)
            g_ = gbt[:, :, 0, :]
            step(dve.scalar_tensor_tensor(g_, g_, 0.0, splus[:], ALU.max, ALU.add))
            dve.scalar_tensor_tensor(g_, g_, -1.0, decay[:].unsqueeze(1).broadcast_to([P, TT, 8]), ALU.mult, ALU.mult).then_inc(sg("g_col"), 1)
            dve.wait_ge(sg("gsum_mm"), 1)
            step(dve.tensor_copy(gc8[:], psf[0:8, 512:512 + S]))
            step(dve.tensor_copy(bt8[:], psf[0:8, 256:512]))
            dve.tensor_copy(gcol[:].rearrange("p a b h -> p (a b h)"), psf[:, 768:800]).then_inc(sg("gcol_in"), 1)
            dve.wait_ge(sg("ecol"), 1)
            step(dve.tensor_tensor(bex[:], gbt[:, :, 1, :], ecol[:, :, 0, :], ALU.mult))

            dve.wait_ge(sg("stage_zero"), 1)

            def conv(i):
                for j in range(RING):
                    s = stage[:, j % 2, :]
                    w = lambda k: cw[:, bass.ds(i * RING + j, 1), k:k + 1].rearrange("p a k -> p (a k)")
                    y = ycv[:, j % 2, :]
                    dve.wait_ge(pe_half, i * 8 + (2 * (U_IN + 28 + j) + 2))
                    dve.tensor_copy(s[:, TAPS - 1:], unit_ps[:, j % 2, 0:S]).then_inc(evac[j % 2], 1)
                    dve.wait_ge(evac[j % 2], i * 2 + ((U_IN + 28) // 2 + j // 2 + 1))
                    if j >= 2 or not isinstance(i, int):
                        dve.wait_ge(conv_used, i * 4 + (j - 1))
                    step(dve.tensor_scalar(y, s[:, 0:S], w(0), None, ALU.mult))
                    for k in range(1, TAPS):
                        ins = dve.scalar_tensor_tensor(y, s[:, k:k + S], w(k), y, ALU.mult, ALU.add)
                        if k < TAPS - 1:
                            step(ins)
                        else:
                            ins.then_inc(conv_y, 1)

            conv(0)
            step.loop(1, 6, 12, conv)

            f3 = lambda t: t[:].rearrange("p a n -> p (a n)")
            sc4 = psf[:, 1024:3072].rearrange("p (n m) -> p n m", m=S)
            dve.wait_ge(sg("xa_scores"), 1)
            dve.tensor_reduce(nx[:, 0:8], sc4, AX, ALU.max, negate=True).then_inc(sg("xa_max"), 1)
            dve.wait_ge(sg("xa_exp"), 8)
            step(dve.reciprocal(rs[:, 0:8], rs[:, 0:8]))
            dve.tensor_tensor(xa_p[:], xa_p[:], rs[:, 0:8].unsqueeze(2).broadcast_to([P, 8, S]), ALU.mult).then_inc(sg("xa_norm"), 1)
            dve.wait_ge(sg("xa_pt_mm"), 1)
            dve.tensor_copy(xa_pt[:].rearrange("p h a n -> p (h a n)"), psf[:, 1024:3072]).then_inc(sg("xa_pt"), 1)
            dve.wait_ge(sg("xa_out"), 1)
            step(dve.tensor_tensor(mixed[:, 12:16, :].rearrange("p h n -> p (h n)"), psf[:, 0:1024],
                                   mixed[:, 12:16, :].rearrange("p h n -> p (h n)"), ALU.mult))
            dve.wait_ge(sg("ln_sum"), 1)
            step(dve.tensor_scalar(mean[:], psf[:, 1024:1024 + S], 1.0 / (GROUPS * P), None, ALU.mult))
            dve.tensor_tensor(gv[:], gv[:], mean[:].unsqueeze(1).broadcast_to([P, GROUPS, S]), ALU.subtract).then_inc(sg("ln_centred"), 1)
            kq = [qkv[:, 8 - 8 * w:16 - 8 * w, :] for w in range(2)]
            dve.wait_ge(sg("qk_rs"), 1)
            dve.tensor_tensor(kq[0], kq[0], qk_rs[0][:], ALU.mult).then_inc(sg("qk_scaled"), 1)
            dve.wait_ge(ws_ld, 32)
            dve.tensor_tensor(wst[:], wst[:], c(TRI_LE).unsqueeze(1).broadcast_to([P, GROUPS, P]), ALU.mult).then_inc(sg("ws_masked"), 1)
            dve.wait_ge(sg("ln_std"), 1)
            step(dve.tensor_tensor(gv[:], gv[:], rstd[:].unsqueeze(1).broadcast_to([P, GROUPS, S]), ALU.mult))
            for g in range(GROUPS):
                ins = dve.tensor_scalar(gv[:, g, :], gv[:, g, :], small[:, 1 + g:2 + g], small[:, 5 + g:6 + g], ALU.mult, ALU.add)
            ins.then_inc(sg("ln_out"), 1)
            dve.wait_ge(sg("qk_rs"), 2)
            dve.scalar_tensor_tensor(kq[1], qk_rs[1][:], SCALE, kq[1], ALU.mult, ALU.mult).then_inc(sg("qk_scaled"), 1)
            dve.wait_ge(sg("v_t"), 1)
            dve.tensor_copy(vt[:].rearrange("p g a n -> p (g a n)"), psf[:, 2048:3072]).then_inc(sg("v_tc"), 1)
            dve.wait_ge(sg("sgu"), 1)
            oa = mixed[:, 0:4, :].rearrange("p g n -> p (g n)")
            dve.tensor_tensor(oa, psf[:, 1024:2048], oa, ALU.mult).then_inc(sg("gmlp_out"), 1)
            dve.wait_ge(sg("gmlp_out"), 1)
            step(dve.tensor_tensor(oa, oa, gz[:].rearrange("p g n -> p (g n)"), ALU.mult))

            v4 = lambda t: t[:].rearrange("p (h a) n -> p h a n", a=2)
            pk = ps_b.rearrange("p (h a n) -> p h a n", h=8, a=2)
            dve.wait_ge(sg("row_bc"), 1)
            for h in range(8):
                for t in range(TT):
                    dve.tensor_scalar(dec[:, 2 * h + t, :], ps_a[:, h * S + t * P:h * S + (t + 1) * P],
                                      gcol[:, t, 0, h:h + 1], 0.0, ALU.subtract, ALU.min).then_inc(sg("dec_arg"), 1)
            dve.wait_ge(sg("k_t"), 1)
            for t in range(TT):
                step(dve.tensor_tensor(v4(kbg)[:, :, t, :], pk[:, :, t, :], bex[:, t, :].unsqueeze(2).broadcast_to([P, 8, P]), ALU.mult))
                ins = dve.tensor_tensor(v4(kd)[:, :, t, :], pk[:, :, t, :], ecol[:, t, 1, :].unsqueeze(2).broadcast_to([P, 8, P]), ALU.mult)
                if t == 0:
                    step(ins)
                else:
                    ins.then_inc(sg("k_tok"), 1)
            dve.wait_ge(sg("dec_exp"), 1)
            step(dve.tensor_tensor(dec[:], dec[:], c(C64_LE).unsqueeze(1).broadcast_to([P, 16, P]), ALU.mult))
            dve.wait_ge(sg("kk"), 1)
            dve.tensor_tensor(f3(at_), ps_a, f3(dec), ALU.mult).then_inc(sg("kk_out"), 1)
            dve.wait_ge(sg("v_dt"), 1)
            for t in range(TT):
                ins = dve.tensor_tensor(v4(vb)[:, :, t, :], pk[:, :, t, :], gbt[:, t, 1, :].unsqueeze(2).broadcast_to([P, 8, P]), ALU.mult)
                if t == 0:
                    step(ins)
                else:
                    ins.then_inc(sg("v_tok"), 1)
            dve.wait_ge(sg("qk"), 1)
            dve.tensor_tensor(f3(ait), ps_a, f3(dec), ALU.mult).then_inc(sg("qk_out"), 1)
            dve.wait_ge(sg("exp_row"), 1)
            step(dve.tensor_copy(egl[:], expr[:].rearrange("p h (c n) -> p h c n", n=CHUNK)[:, :, :, CHUNK - 1]))
            qf = qkv[:, 0:8, :].rearrange("p h n -> p (h n)")
            step(dve.tensor_tensor(qf, qf, expr[:].rearrange("p h n -> p (h n)"), ALU.mult))
            dve.wait_ge(sg("beta_bc"), 1)
            dve.wait_ge(sg("kk_out"), 1)
            four = lambda t, g: t[:, 4 * g:4 * g + 4, :]
            flat4 = lambda t, g: four(t, g).rearrange("p a n -> p (a n)")
            for g in range(4):
                step(dve.tensor_tensor(flat4(at_, g), ps_b[:, g * 512:(g + 1) * 512], flat4(at_, g), ALU.mult))
                step(dve.tensor_tensor(four(dec, g), four(at_, g), c(LEVEL0).unsqueeze(1).broadcast_to([P, 4, P]), ALU.mult))
                dve.tensor_tensor(four(qt, g), ident.unsqueeze(1).broadcast_to([P, 4, P]), four(dec, g), ALU.subtract).then_inc(sg("inv_q0"), 1)
            dve.wait_ge(sg("inv_q0"), 4)
            for g in range(4):
                dve.tensor_tensor(four(dec, g), four(at_, g), c(LEVEL0 + 1).unsqueeze(1).broadcast_to([P, 4, P]), ALU.mult).then_inc(sg("inv_a"), 1)

            def level(lev, last=False):
                if not last:
                    for g in range(4):
                        m = cst[:, bass.ds(lev + (LEVEL0 + 1), 1), :].broadcast_to([P, 4, P])
                        dve.wait_ge(sg("inv_x"), lev * 4 + (g - 3))
                        dve.tensor_tensor(four(dec, g), four(at_, g), m, ALU.mult).then_inc(sg("inv_a"), 1)
                for g in range(4):
                    dve.wait_ge(sg("inv_pq"), lev * 4 + (g - 3))
                    step(dve.tensor_tensor(flat4(pt, g), flat4(pt, g), pq(g)[0], ALU.subtract))
                    dve.tensor_tensor(flat4(qt, g), flat4(qt, g), pq(g)[1], ALU.subtract).then_inc(sg("inv_upd"), 1)

            step.loop(1, LEVELS - 1, 4, level)
            level(LEVELS - 1, last=True)
            for cch in range(CHUNKS):
                po = CHUNK * (cch % 2)
                pr = slice(po, po + CHUNK)
                dve.wait_ge(sg("vnew_mm"), cch + 1)
                dve.tensor_copy(vn[pr].rearrange("p h n -> p (h n)"), psf[pr, 0:1024]).then_inc(sg("vnew"), 1)
                dve.wait_ge(sg("o_mm"), cch + 1)
                ins = dve.tensor_copy(odn[:, :, cch * CHUNK:(cch + 1) * CHUNK], ps[:, 2, :].rearrange("p (h n) -> p h n", h=8))
                ins.then_inc(sg("odn_full") if cch == CHUNKS - 1 else sg("o_out"), 1)
                if cch < CHUNKS - 1:
                    dve.wait_ge(sg("ds_mm"), cch + 1)
                    if cch == 0:
                        dve.tensor_copy(st[:].rearrange("p h n -> p (h n)"), psf[:, 1536:2560]).then_inc(sg("state"), 1)
                    else:
                        for h in range(8):
                            ins = dve.scalar_tensor_tensor(st[:, h, :], st[:, h, :], egl[:, h, cch:cch + 1],
                                                           psf[:, 1536 + h * P:1536 + (h + 1) * P], ALU.mult, ALU.add)
                        ins.then_inc(sg("state"), 1)
            dve.wait_ge(sg("odn_std"), 1)
            of = odn[:].rearrange("p h n -> p (h n)")
            ob = mixed[:, 4:12, :].rearrange("p h n -> p (h n)")
            step(dve.scalar_tensor_tensor(of, of, small[:, 0:1], f3(qt), ALU.mult, ALU.mult))
            dve.tensor_tensor(ob, ob, of, ALU.mult).then_inc(sg("mixed_done"), 1)

            lower(2, mixed)
            segment(U_OUT, OUT_UNITS, add_to_x)
            norm(2, X, G_FINAL, X, done=sg("x2_done"))
            dve.wait_ge(sg("x2_done"), 1)
            norm(3, X, G_MIX, T16, 3)
            dve.wait_ge(lin_lo2, 8)
            dve.wait_ge(sg("f_mm"), 1)
            dve.tensor_copy(f8[:], psf[0:8, 0:S]).then_inc(sg("f_row"), 1)
            dve.wait_ge(sg("f_t"), 1)
            dve.tensor_tensor(fcol[:], psf[:, S:S + 16].rearrange("p (a n) -> p a n", a=TT),
                              f_bias.unsqueeze(1).broadcast_to([P, TT, 8]), ALU.add).then_inc(sg("f_in"), 1)
            dve.wait_ge(sg("f_ln"), 1)
            dve.scalar_tensor_tensor(fcol[:], fcol[:], 0.0, fl[:], ALU.min, ALU.subtract).then_inc(sg("f_col"), 1)
            segment(U_IN2 + 32, 8, into(qa, SCALE))
            segment(U_IN2 + 40, 8, into(ka))
            dve.wait_ge(sg("cumf_mm"), 1)
            step(dve.tensor_scalar(ft8[:], psf[0:8, 1024:1024 + S], -1.0, None, ALU.mult))
            dve.tensor_copy(cf8[:], psf[0:8, 1024:1024 + S]).then_inc(sg("cumf"), 1)
            segment(U_IN2 + 48, 8, into(va))
            segment(U_IN2 + 56, 8, into(qb, SCALE))
            segment(U_IN2 + 64, 8, into(kb))
            segment(U_IN2 + 72, 8, into(vb2))

            fa, fb = (t[:].rearrange("p h n -> p (h n)") for t in (za, zb))
            strict = c(TRI_LT).unsqueeze(1).broadcast_to([P, 8, P])
            dve.wait_ge(sg("sb_ln"), 1)
            step(dve.scalar_tensor_tensor(fa, psf, 0.0, fa, ALU.max, ALU.add))
            step(dve.tensor_tensor(fb, psf, fa, ALU.subtract))
            d0 = lambda f: f[:, 0:2048].rearrange("p (h n) -> p h n", h=8)[:, :, 0:P]
            d1 = lambda f: f[:, 2048:3072].rearrange("p (h n) -> p h n", h=8)
            step(dve.tensor_tensor(d0(fa), d0(fa), strict, ALU.mult))
            dve.tensor_tensor(d1(fa), d1(fa), strict, ALU.mult).then_inc(sg("sb_sp"), 1)
            dve.wait_ge(sg("sb_suffix"), 1)
            dve.tensor_tensor(fb, fb, psf, ALU.subtract).then_inc(sg("sb_arg"), 1)
            dve.wait_ge(sg("sb_exp"), 1)
            step(dve.tensor_tensor(d0(fb), d0(fb), strict, ALU.mult))
            dve.tensor_tensor(d1(fb), d1(fb), strict, ALU.mult).then_inc(sg("sb_w"), 1)
            vk = vtk[:].rearrange("p h a n -> p (h a n)")
            dve.wait_ge(sg("sb_vt_mm"), 1)
            dve.tensor_copy(vk, psf[:, 0:2048]).then_inc(sg("sb_vt"), 1)
            dve.wait_ge(sg("sb_out"), 1)
            dve.tensor_copy(T16[:, 0:8, :].rearrange("p h n -> p (h n)"), psf[:, 0:2048]).then_inc(sg("sb_done"), 1)

            later = c(TRI_LT).unsqueeze(1).broadcast_to([P, 8, P])
            l0 = lambda f: f[:, 0:1024].rearrange("p (h n) -> p h n", h=8)
            l1 = lambda f, x: f[:, 1024:3072].rearrange("p (h n) -> p h n", h=8)[:, :, x * P:(x + 1) * P]
            dve.wait_ge(sg("fx_logits"), 1)
            step(dve.scalar_tensor_tensor(l0(fa), later, NEG_INF, l0(psf), ALU.mult, ALU.add))
            step(dve.scalar_tensor_tensor(l1(fa, 1), later, NEG_INF, l1(psf, 1), ALU.mult, ALU.add))
            step(dve.tensor_copy(l1(fa, 0), l1(psf, 0)))
            step(dve.tensor_reduce(nfx[:, 0:8], l0(fa), AX, ALU.max, negate=True))
            dve.tensor_reduce(nfx[:, 8:16], fa[:, 1024:3072].rearrange("p (h n) -> p h n", h=8), AX, ALU.max, negate=True).then_inc(sg("fx_max"), 1)
            dve.wait_ge(sg("fx_exp"), 16)
            step(dve.reciprocal(rfx[:], rfx[:]))
            step(dve.tensor_tensor(l0(fa), l0(fa), rfx[:, 0:8].unsqueeze(2).broadcast_to([P, 8, P]), ALU.mult))
            f1 = fa[:, 1024:3072].rearrange("p (h n) -> p h n", h=8)
            dve.tensor_tensor(f1, f1, rfx[:, 8:16].unsqueeze(2).broadcast_to([P, 8, S]), ALU.mult).then_inc(sg("fx_p"), 1)
            dve.wait_ge(sg("fx_pt_mm"), 1)
            dve.tensor_copy(fb, psf).then_inc(sg("fx_pt"), 1)
            dve.wait_ge(sg("fx_vt_mm"), 1)
            dve.tensor_copy(vk, psf[:, 0:2048]).then_inc(sg("fx_vt"), 1)
            dve.wait_ge(sg("fx_out"), 1)
            dve.tensor_copy(T16[:, 8:16, :].rearrange("p h n -> p (h n)"), psf[:, 0:2048]).then_inc(sg("fx_done"), 1)

            lower(4)
            with dve.Fori(0, BR_UNITS // 2) as i:
                ga = sga[:, bass.ds(i * 2, 2), :].rearrange("p a n -> p (a n)")
                gb = sgb[:, bass.ds(i * 2, 2), :].rearrange("p a n -> p (a n)")
                dve.wait_ge(pe_half, i * 4 + (2 * U_BR + 2))
                dve.tensor_tensor(ga, unit_ps[:, 0, :], ga, ALU.mult).then_inc(evac[0], 1)
                dve.wait_ge(pe_half, i * 4 + (2 * U_BR + 4))
                dve.tensor_tensor(gb, unit_ps[:, 1, :], gb, ALU.mult).then_inc(evac[1], 1)
                dve.wait_ge(evac[1], i + (U_BR // 2 + 1))
                dve.tensor_tensor(ga, ga, gb, ALU.add).then_inc(sg("merged"), 1)
            lower(5, sga)
            segment(U_OUT2, OUT_UNITS, add_to_x)
            norm(4, X, G_FFN, T16, 6)
            dve.wait_ge(lin_lo2, 14)
            segment(U_Q, OUT_UNITS, into(T16))

            def top16(vals, idx, src):
                work = rest[:, 0:src.shape[-1]]
                step(dve.max(vals[:, 0:8], src))
                step(dve.max_index(idx[:, 0:8], vals[:, 0:8], src))
                step(dve.match_replace(work, vals[:, 0:8], src, -3.0e38))
                step(dve.max(vals[:, 8:16], work))
                step(dve.max_index(idx[:, 8:16], vals[:, 8:16], work))

            scf = sc[:].rearrange("p t a n -> p (t a n)")
            for n in range(8):
                dve.wait_ge(sg("key_scores"), n + 1)
                dve.tensor_copy(scf[:, n * 512:(n + 1) * 512], ps[:, n % 6, :]).then_inc(sg("key_out"), 1)
            dve.wait_ge(sg("key_out"), 8)
            heads = lambda t: t.rearrange("p (h k) -> p h k", h=8)
            for t in range(TT):
                for hp in range(16):
                    top16(v16[:, hp, :], i16[:, hp, :], sc[:, t, hp, :])
                step(dve.tensor_copy(if16[:], i16[:]))
                v4_ = v16[:].rearrange("p (h two) k -> p h two k", two=2)
                i4_ = if16[:].rearrange("p (h two) k -> p h two k", two=2)
                for h in range(8):
                    step(dve.tensor_tensor(cand[:, h, :].rearrange("p (i j) -> p i j", i=TOPK),
                                           v4_[:, h, 0, :].unsqueeze(2).broadcast_to([P, TOPK, TOPK]),
                                           v4_[:, h, 1, :].unsqueeze(1).broadcast_to([P, TOPK, TOPK]), ALU.add))
                for h in range(8):
                    top16(ts[:, h, :], ti[:, h, :], cand[:, h, :])
                step(dve.tensor_scalar(th[:], ti[:], 4, None, ALU.logical_shift_right))
                step(dve.tensor_scalar(tl[:], ti[:], 15, None, ALU.bitwise_and))
                step(dve.tensor_copy(thf[:], th[:]))
                step(dve.tensor_copy(tlf[:], tl[:]))
                iota16 = cst[:, IOTA, 0:TOPK].unsqueeze(1).broadcast_to([P, P, TOPK])
                c3 = cand[:].rearrange("p h (k j) -> p (h k) j", j=TOPK)
                c4 = cand[:].rearrange("p h (k j) -> p h k j", j=TOPK)
                for half, pos in enumerate((thf, tlf)):
                    step(dve.tensor_tensor(c3, iota16, pos[:].rearrange("p h k -> p (h k)").unsqueeze(2).broadcast_to([P, P, TOPK]), ALU.is_equal))
                    step(dve.tensor_tensor(c4, c4, i4_[:, :, half, :].unsqueeze(2).broadcast_to([P, 8, TOPK, TOPK]), ALU.mult))
                    step(dve.tensor_reduce(picks[:, t, half, :], c3, AX, ALU.add))
                ins = dve.tensor_tensor(heads(picks[:, t, 2, :]), ts[:], ts[:, :, 0:1].broadcast_to([P, 8, TOPK]), ALU.subtract)
                if t == TT - 1:
                    ins.then_inc(sg("gate_arg"), 1)
                else:
                    step(ins)
            dve.wait_ge(sg("gate_exp"), 1)
            for t in range(TT):
                g3 = heads(picks[:, t, 2, :])
                step(dve.tensor_reduce(gs[:], g3, AX, ALU.add))
                step(dve.reciprocal(gs[:], gs[:]))
                dve.tensor_tensor(g3, g3, gs[:].unsqueeze(2).broadcast_to([P, 8, TOPK]), ALU.mult).then_inc(sg("picked"), 1)
                dve.wait_ge(sg("picked"), t + 1)
            dve.wait_ge(sg("picks_t"), 1)
            for a in range(3):
                dve.tensor_copy(sel[:, a, :].rearrange("p (t n) -> p t n", t=TT),
                                psf[:, 2048:3072].rearrange("p (t a n) -> p t a n", t=TT, a=4)[:, :, a, :]).then_inc(sg("sel"), 1)
            dve.wait_ge(sg("sel"), 3)

            def onehots(g16):
                for b8 in range(0, ONEHOTS, 8):
                    if not isinstance(g16, int):
                        dve.wait_ge(sg("gate_mm"), g16 * ONEHOTS + (b8 + 8 - ONEHOTS))
                    row = sel[:, 1:2, bass.ds(g16 * ONEHOTS + b8, 8)].rearrange("p a n -> p (a n)")
                    dve.tensor_tensor(oh2[:, b8:b8 + 8, :], c(IOTA).unsqueeze(1).broadcast_to([P, 8, P]),
                                      row.unsqueeze(2).broadcast_to([P, 8, P]), ALU.is_equal).then_inc(sg("oh2"), 1)
                    for b in range(b8, b8 + 8):
                        col = lambda a: sel[:, a, bass.ds(g16 * ONEHOTS + b, 1)]
                        dve.tensor_scalar(oh1[:, b, :], c(IOTA), col(0), col(2), ALU.is_equal, ALU.mult).then_inc(sg("oh"), 1)
            onehots(0)
            with dve.Fori(1, S // ONEHOTS) as g16:
                onehots(g16)

            def gate_quarter(e, q):
                upper, lower_ = gated(e)
                if q == 0:
                    u = first_unit("up", e)
                    dve.wait_ge(evac[0], (u + KT) // 2)
                    dve.wait_ge(evac[1], (u + KT) // 2)
                    dve.wait_ge(sg("gate_in"), 16 * (e + 1))
                    if e >= EXPERT_CHUNKS - 2:
                        dve.wait_ge(pe_half, 2 * (first_unit("up", EXPERT_CHUNKS - 1) + KT))
                    elif e:
                        dve.wait_ge(pe_half, 2 * (first_unit("down", e - 1) + KT))
                ks = slice(4 * q, 4 * q + 4)
                h = hidden[e % 3][:, ks, :]
                h4 = h.rearrange("p a (g n) -> p a g n", g=16)
                dve.tensor_tensor(h4, h4, gch[:, :, ks, :].rearrange("p g a n -> p a g n"), ALU.mult).then_inc(sg("gates_used"), 1)
                dve.wait_ge(sg("gates_used"), 4 * e + q + 1)
                step(dve.tensor_copy(upper[:, ks, :], h))
                dve.tensor_tensor(lower_[:, ks, :], h, upper[:, ks, :].bitcast(F32), ALU.subtract).then_inc(sg("hid_lo"), 1)

            for e in range(EXPERT_CHUNKS):
                u0 = first_unit("down", e)
                if e < EXPERT_CHUNKS - 2:
                    for q in range(4):
                        gate_quarter(e, q)
                if e < EXPERT_CHUNKS - 3 or e == EXPERT_CHUNKS - 1:
                    segment(u0, KT, add_to_x)
                else:
                    for q in range(4):
                        gate_quarter(e + 1, q)
                        for j in range(4):
                            dve.wait_ge(pe_half, 2 * (u0 + 4 * q + j) + 2)
                            add_to_x(q, j).then_inc(evac[j % 2], 1)
            norm(5, X, G_OUT, T16, done=sg("result"))

        @block.tensor
        def _(pe):
            def mm(o, lhsT, rhs, start=True, stop=True, **k):
                return nc.tensor.matmul(o, lhsT, rhs, start=start, stop=stop, **k)

            def unit_body(u, j, hi, lo, par, paired=False, ready=None):
                s0 = (2 * j) % 4
                o = unit_ps[:, j % 2, :]
                if not (isinstance(par, int) and par == 0):
                    pe.wait_ge(evac[j % 2], par)
                for h in range(2):
                    if ready is not None and h == 0 and (j == 0 or paired):
                        pe.wait_ge((lin_lo, lin_lo2)[j], 2 * ready + 2)
                    if ready is not None and h == 1 and j == 0 and not paired:
                        pe.wait_ge(lin_lo2, 2 * ready + 2)
                    pe.wait_ge(lo_ready, u * 2 + (2 * j + h + 1))
                    for k in range(HALF):
                        if paired:
                            x = k + HALF * (j % 2)
                            oo, first, last = o[:, h * S:(h + 1) * S], k == 0, k == HALF - 1
                        else:
                            x = h * HALF + k
                            oo, first, last = o[:, 0:S], h == 0 and k == 0, h == 1 and k == HALF - 1
                        a, b = whi[:, s0 + h, k, :], wlo[:, s0 + h, k, :]
                        mm(oo, a, hi[:, x, :], start=first, stop=False)
                        mm(oo, a, lo[:, x, :], start=False, stop=False)
                        z = mm(oo, b, hi[:, x, :], start=False, stop=last)
                    z.then_inc(pe_half, 1)

            def segment(u0, n, paired=False, hi=xhi, lo=xlo, ready=None):
                first = int(ready is not None)
                for j in range(2 * first):
                    unit_body(u0, j, hi, lo, u0 // 2, paired, ready)
                with pe.Fori(first, n // 2) as i:
                    for j in range(2):
                        unit_body(i * 2 + u0, j, hi, lo, i + u0 // 2, paired)

            def norm_sums(n, quarters=range(4)):
                for q in quarters:
                    pe.wait_ge(norm_sq, 4 * n + q + 1)
                    for k in range(4 * q, 4 * q + 4):
                        z = mm(psf[:, 0:S], ones, T16[:, k, :], k == 0, k == KT - 1)
                if q == 3:
                    z.then_inc(norm_sum, 1)

            def residual_segment(n, u0, hi=xhi, lo=xlo, ready=None):
                segment(u0, 12, False, hi, lo, ready)
                norm_sums(n, (0, 1))
                segment(u0 + 12, 4, False, hi, lo)
                norm_sums(n, (2, 3))

            def tr(o, i, idn=None):
                return nc.tensor.transpose(o, i, ident if idn is None else idn)

            pe.wait_ge(cst_in, 16 * 7)
            norm_sums(0)
            segment(U_KV, KV_UNITS, ready=0)
            pe.wait_ge(evac[0], KV_UNITS // 2)
            pe.wait_ge(evac[1], KV_UNITS // 2)
            for t in range(TT):
                for h in range(XA_HEADS):
                    z = tr(psf[:, 1024 + (t * 4 + h) * P:1024 + (t * 4 + h + 1) * P], mvf[:, h, t * P:(t + 1) * P])
            z.then_inc(sg("mv_t"), 1)
            norm_sums(1)
            def narrow(col, n, done):
                for k in range(KT):
                    mm(psf[0:n, 0:S], wab_hi[:, k, col:col + n], xhi[:, k, :], k == 0, False)
                    mm(psf[0:n, 0:S], wab_hi[:, k, col:col + n], xlo[:, k, :], False, False)
                    z = mm(psf[0:n, 0:S], wab_lo[:, k, col:col + n], xhi[:, k, :], False, k == KT - 1)
                z.then_inc(done, 1)

            def by_token(rows, n, done):
                for t in range(TT):
                    z = tr(psf[:, S + t * n:S + (t + 1) * n], rows[:, t * P:(t + 1) * P], ident[0:n, 0:n])
                z.then_inc(done, 1)

            segment(U_IN, 4, ready=1)
            pe.wait_ge(sg("wab_lo"), 1)
            narrow(0, 16, sg("ab_mm"))
            segment(U_IN + 4, 4)
            pe.wait_ge(sg("ab_row"), 1)
            by_token(ab16, 16, sg("ab_t"))
            segment(U_IN + 8, 12)
            pe.wait_ge(sg("g_col"), 1)
            pe.wait_ge(sg("beta"), 1)
            for t in range(TT):
                mm(psf[0:8, 512 + t * P:512 + (t + 1) * P], gbt[:, t, 0, :], c(C64_LE))
                mm(psf[0:8, 256 + t * P:256 + (t + 1) * P], gbt[:, t, 1, :], ident)
            for t in range(TT):
                for x, m in enumerate((C64_LE, C64_GT)):
                    z = mm(psf[:, 768 + (2 * t + x) * 8:768 + (2 * t + x + 1) * 8], c(m), gbt[:, t, 0, :])
            z.then_inc(sg("gsum_mm"), 1)
            segment(U_IN + 20, 32)

            def qk_ss(r):
                pe.wait_ge(sg("qk_sq"), r // 2 + 1)
                if r:
                    pe.wait_ge(sg("qk_ln"), r)
                for h in range(4):
                    z = mm(ps_b[:, h * S:(h + 1) * S], ones, qk_sq[r // 2][:, 4 * (r % 2) + h, :])
                z.then_inc(sg("qk_ss"), 1)

            pe.wait_ge(evac[0], (U_IN + IN_UNITS) // 2)
            pe.wait_ge(evac[1], (U_IN + IN_UNITS) // 2)
            pe.wait_ge(sg("kv_done"), 1)
            for h in range(XA_HEADS):
                for t in range(TT):
                    n = 2 * h + t
                    z = mm(psf[:, 1024 + n * S:1024 + (n + 1) * S], cq[:, h, t * P:(t + 1) * P], mk[:, h, :])
            z.then_inc(sg("xa_scores"), 1)
            qk_ss(0)
            pe.wait_ge(sg("xa_norm"), 1)
            for h in range(XA_HEADS):
                for m in range(TT):
                    for t in range(TT):
                        z = tr(psf[:, 1024 + (2 * h + m) * S + t * P:1024 + (2 * h + m) * S + (t + 1) * P],
                               xa_p[:, 2 * h + t, m * P:(m + 1) * P])
            z.then_inc(sg("xa_pt_mm"), 1)
            qk_ss(1)
            pe.wait_ge(sg("xa_pt"), 1)
            for h in range(XA_HEADS):
                for m in range(TT):
                    z = mm(psf[:, h * S:(h + 1) * S], mvt[:, m, h, :], xa_pt[:, h, m, :], m == 0, m == TT - 1)
            z.then_inc(sg("xa_out"), 1)
            for g in range(GROUPS):
                z = mm(psf[:, 1024:1024 + S], ones, gv[:, g, :], g == 0, g == GROUPS - 1)
            z.then_inc(sg("ln_sum"), 1)
            qk_ss(2)
            pe.wait_ge(sg("ln_sq"), 1)
            for g in range(GROUPS):
                z = mm(psf[:, 1536:1536 + S], ones, vsq[:, g, :], g == 0, g == GROUPS - 1)
            z.then_inc(sg("ln_sqsum"), 1)
            qk_ss(3)
            pe.wait_ge(sg("ln_out"), 1)
            for g in range(GROUPS):
                for t in range(TT):
                    z = tr(psf[:, 2048 + (2 * g + t) * P:2048 + (2 * g + t + 1) * P], gv[:, g, t * P:(t + 1) * P])
            z.then_inc(sg("v_t"), 1)
            pe.wait_ge(sg("qk_ln"), 4)
            pe.wait_ge(sg("gcol_in"), 1)
            pe.wait_ge(sg("qk_scaled"), 2)
            for n in range(16):
                z = tr(ps_b[:, n * P:(n + 1) * P], qkv[:, 8 + n // 2, (n % 2) * P:(n % 2 + 1) * P])
            z.then_inc(sg("k_t"), 1)
            pe.wait_ge(sg("v_tc"), 1)
            pe.wait_ge(sg("ws_masked"), 1)
            for g in range(GROUPS):
                for t in range(TT):
                    o = psf[:, 1024 + (2 * g + t) * P:1024 + (2 * g + t + 1) * P]
                    mm(o, vt[:, g, t, :], wst[:, g, :], True, False)
                    z = mm(o, ones[0:1, :], bs_row[0:1, g * P:(g + 1) * P], False, True)
            z.then_inc(sg("sgu"), 1)

            def rows(dst, src, done):
                for h in range(8):
                    z = mm(dst[:, h * S:(h + 1) * S], ident[0:8, h:h + 1].to_broadcast([8, P]), src[:, :])
                z.then_inc(done, 1)

            pe.wait_ge(sg("gmlp_out"), 1)
            rows(ps_a, gc8, sg("row_bc"))
            pe.wait_ge(sg("k_tok"), 1)
            for n in range(16):
                z = tr(ps_b[:, n * P:(n + 1) * P], qkv[:, 16 + n // 2, (n % 2) * P:(n % 2 + 1) * P])
            z.then_inc(sg("v_dt"), 1)
            pe.wait_ge(sg("exp_row"), 1)
            for n in range(16):
                kk = qkv[:, 8 + n // 2, (n % 2) * P:(n % 2 + 1) * P]
                z = mm(ps_a[:, n * P:(n + 1) * P], kk, kk)
            z.then_inc(sg("kk"), 1)
            pe.wait_ge(sg("kk_out"), 1)
            for n in range(16):
                sl = slice((n % 2) * P, (n % 2 + 1) * P)
                z = mm(ps_a[:, n * P:(n + 1) * P], qkv[:, 8 + n // 2, sl], qkv[:, n // 2, sl])
            z.then_inc(sg("qk"), 1)
            pe.wait_ge(sg("v_tok"), 1)
            rows(ps_b, bt8, sg("beta_bc"))
            for g in range(4):
                if g == 0:
                    pe.wait_ge(sg("inv_q0"), 4)
                for n in range(4 * g, 4 * g + 4):
                    z = tr(ps[:, g, (n % 4) * P:(n % 4 + 1) * P], qt[:, n, :])
                z.then_inc(sg("inv_p0"), 1)
            pe.wait_ge(sg("inv_upd"), 4)
            with pe.Fori(1, LEVELS) as lev:
                for g in range(4):
                    pe.wait_ge(sg("inv_a"), lev * 4 + (g - 3))
                    pe.wait_ge(sg("inv_upd"), lev * 4 + (g - 3))
                    for n in range(4 * g, 4 * g + 4):
                        z = mm(ps[:, g, (n % 4) * P:(n % 4 + 1) * P], dec[:, n, :], pt[:, n, :])
                    z.then_inc(sg("inv_x"), 1)
                for g in range(4):
                    pe.wait_ge(sg("inv_xc"), lev * 4 + (g - 3))
                    if g >= 2:
                        pe.wait_ge(sg("inv_upd"), lev * 4 + (g - 1))
                    for n in range(4 * g, 4 * g + 4):
                        mm(pq(g)[0][:, (n % 4) * P:(n % 4 + 1) * P], qt[:, n, :], xt[:, n, :])
                    for n in range(4 * g, 4 * g + 4):
                        z = mm(pq(g)[1][:, (n % 4) * P:(n % 4 + 1) * P], xt[:, n, :], qt[:, n, :])
                    z.then_inc(sg("inv_pq"), 1)
            pe.wait_ge(sg("inv_upd"), LEVELS * 4)
            for n in range(16):
                z = mm(psf[:, n * P:(n + 1) * P], kbg[:, n, :], qt[:, n, :])
            z.then_inc(sg("kcd_mm"), 1)
            pe.wait_ge(sg("kcd"), 1)
            for cch in range(CHUNKS):
                t, po = cch // 2, CHUNK * (cch % 2)
                pr = slice(po, po + CHUNK)
                if cch:
                    pe.wait_ge(sg("state"), cch)
                for h in range(8):
                    o = psf[pr, h * P:(h + 1) * P]
                    z = mm(o, qt[pr, 2 * h + t, pr], vb[pr, 2 * h + t, :], True, cch == 0)
                    if cch:
                        z = mm(o, kcd[:, 2 * h + t, pr], st[:, h, :], False, True)
                z.then_inc(sg("vnew_mm"), 1)
                pe.wait_ge(sg("vnew"), cch + 1)
                if cch:
                    pe.wait_ge(sg("o_out"), cch)
                for h in range(8):
                    o = ps[:, 2, h * CHUNK:(h + 1) * CHUNK]
                    if cch:
                        mm(o, st[:, h, :], qkv[:, h, cch * CHUNK:(cch + 1) * CHUNK], True, False)
                    z = mm(o, vn[pr, h, :], ait[pr, 2 * h + t, pr], cch == 0, True)
                z.then_inc(sg("o_mm"), 1)
                if cch < CHUNKS - 1:
                    for h in range(8):
                        z = mm(psf[:, 1536 + h * P:1536 + (h + 1) * P], kd[pr, 2 * h + t, :], vn[pr, h, :])
                    z.then_inc(sg("ds_mm"), 1)
            pe.wait_ge(sg("odn_sq"), 1)
            for h in range(8):
                z = mm(psf[:, 1024 + h * S:1024 + (h + 1) * S], ones, pt[:, 2 * h:2 * h + 2, :].rearrange("p a n -> p (a n)"))
            z.then_inc(sg("odn_ss"), 1)

            residual_segment(2, U_OUT, ready=2)
            norm_sums(3)
            segment(U_IN2, 16, ready=3)
            narrow(16, 8, sg("f_mm"))
            segment(U_IN2 + 16, 16)
            pe.wait_ge(sg("f_row"), 1)
            by_token(f8, 8, sg("f_t"))
            segment(U_IN2 + 32, 16)
            pe.wait_ge(sg("f_col"), 1)
            mm(psf[0:8, 1024:1024 + P], fcol[:, 0, :], c(TRI_LE))
            mm(psf[0:8, 1024 + P:1024 + S], fcol[:, 0, :], ones, True, False)
            mm(psf[0:8, 1024 + P:1024 + S], fcol[:, 1, :], c(TRI_LE), False, True).then_inc(sg("cumf_mm"), 1)
            segment(U_IN2 + 48, 32)

            def wait_units(u):
                pe.wait_ge(evac[0], u // 2)
                pe.wait_ge(evac[1], u // 2)

            wait_units(U_BR)
            pe.wait_ge(sg("cumf"), 1)

            def values_by_token(v, done):
                for n in range(16):
                    z = tr(psf[:, n * P:(n + 1) * P], v[:, n // 2, (n % 2) * P:(n % 2 + 1) * P])
                z.then_inc(done, 1)

            def weighted_values(w, done):
                for h in range(HEADS):
                    mm(psf[:, h * S:(h + 1) * S], vtk[:, h, 0, :], w[:, h * S:(h + 1) * S], True, False)
                    z = mm(psf[:, h * S + P:(h + 1) * S], vtk[:, h, 1, :], w[:, 2048 + h * P:2048 + (h + 1) * P], False, True)
                z.then_inc(done, 1)

            fa, fb = (t[:].rearrange("p h n -> p (h n)") for t in (za, zb))
            for h in range(HEADS):
                mm(psf[:, h * S:(h + 1) * S], ka[:, h, 0:P], qa[:, h, :])
            for h in range(HEADS):
                z = mm(psf[:, 2048 + h * P:2048 + (h + 1) * P], ka[:, h, P:S], qa[:, h, P:S])
            z.then_inc(sg("sb_z"), 1)
            pe.wait_ge(sg("sb_sp"), 1)
            for h in range(HEADS):
                later = fa[:, 2048 + h * P:2048 + (h + 1) * P]
                mm(psf[:, h * S:(h + 1) * S], c(TRI_GT), fa[:, h * S:(h + 1) * S], True, False)
                mm(psf[:, h * S + P:(h + 1) * S], ones, later, False, True)
            for h in range(HEADS):
                z = mm(psf[:, 2048 + h * P:2048 + (h + 1) * P], c(TRI_GT), fa[:, 2048 + h * P:2048 + (h + 1) * P])
            z.then_inc(sg("sb_suffix"), 1)
            pe.wait_ge(sg("sb_arg"), 1)
            values_by_token(va, sg("sb_vt_mm"))
            pe.wait_ge(sg("sb_w"), 1)
            pe.wait_ge(sg("sb_vt"), 1)
            weighted_values(fb, sg("sb_out"))
            pe.wait_ge(sg("sb_done"), 1)
            for h in range(HEADS):
                pick = ident[0:8, h:h + 1]
                for t, o, n in ((0, psf[:, h * P:(h + 1) * P], P), (1, psf[:, 1024 + h * S:1024 + (h + 1) * S], S)):
                    sl = slice(t * P, (t + 1) * P)
                    mm(o, qb[:, h, sl], kb[:, h, 0:n], True, False)
                    mm(o, cf8[:, sl], pick.to_broadcast([8, n]), False, False)
                    z = mm(o, pick.to_broadcast([8, P]), ft8[:, 0:n], False, True)
            z.then_inc(sg("fx_logits"), 1)
            pe.wait_ge(sg("fx_p"), 1)
            for h in range(HEADS):
                tr(psf[:, h * S:h * S + P], fa[:, h * P:(h + 1) * P])
                tr(psf[:, h * S + P:(h + 1) * S], fa[:, 1024 + h * S:1024 + h * S + P])
                z = tr(psf[:, 2048 + h * P:2048 + (h + 1) * P], fa[:, 1024 + h * S + P:1024 + (h + 1) * S])
            z.then_inc(sg("fx_pt_mm"), 1)
            pe.wait_ge(sg("fx_pt"), 1)
            values_by_token(vb2, sg("fx_vt_mm"))
            pe.wait_ge(sg("fx_vt"), 1)
            weighted_values(fb, sg("fx_out"))

            segment(U_BR, BR_UNITS, paired=True, ready=4)
            residual_segment(4, U_OUT2, ready=5)
            segment(U_Q, OUT_UNITS, ready=6)

            wait_units(U_EXP)
            pe.wait_ge(sk_ld, 16)
            for n in range(8):
                if n >= 6:
                    pe.wait_ge(sg("key_out"), n - 5)
                for b in range(4):
                    t, hp = n // 4, 4 * (n % 4) + b
                    z = mm(ps[:, n % 6, b * P:(b + 1) * P], T16[:, hp, t * P:(t + 1) * P], skt[:, hp, :])
                z.then_inc(sg("key_scores"), 1)

            def transpose_picks():
                pe.wait_ge(sg("picked"), TT)
                for t in range(TT):
                    for a in range(3):
                        z = tr(psf[:, 2048 + (4 * t + a) * P:2048 + (4 * t + a + 1) * P], picks[:, t, a, :])
                z.then_inc(sg("picks_t"), 1)

            def gates(g16):
                for q in range(4):
                    if g16:
                        pe.wait_ge(sg("gate_out"), g16 * 4 + (q - 3))
                    if q % 2 == 0:
                        pe.wait_ge(sg("oh2"), g16 * 2 + (q // 2 + 1))
                    for b in range(4 * q, 4 * q + 4):
                        pe.wait_ge(sg("oh"), g16 * 16 + (b + 1))
                        mm(ps[:, q, (b % 4) * P:(b % 4 + 1) * P], oh2[:, b, :], oh1[:, b, :]).then_inc(sg("gate_mm"), 1)

            for kind, e in ORDER:
                u0 = first_unit(kind, e)
                if (kind, e) == ("up", 2):
                    transpose_picks()
                    g16 = 0
                    for n, groups in enumerate(GATE_GROUPS):
                        unit_body(u0 + n - n % 2, n % 2, xhi, xlo, (u0 + n) // 2)
                        for _ in range(groups):
                            gates(g16)
                            g16 += 1
                    segment(u0 + 12, 4)
                elif kind == "up":
                    segment(u0, KT)
                else:
                    pe.wait_ge(sg("hid_lo"), 4 * e + 4)
                    if e < EXPERT_CHUNKS - 1:
                        segment(u0, KT, False, *gated(e))
                    else:
                        residual_segment(5, u0, *gated(e))


def kernel(**inputs):
    import numpy as np
    import concourse.bacc as bacc
    from concourse.bass_utils import run_bass_kernel_spmd

    def units(w):
        k, n = w.shape
        return w.reshape(k // P, P, n // P, P).transpose(2, 1, 0, 3).reshape(n // P, P, k)

    def features(x):
        return x.T.reshape(KT, P, S).transpose(1, 0, 2)

    def column(v):
        return v.reshape(-1, P).T

    x = {k: np.asarray(v) for k, v in inputs.items()}
    w = x["w_in"][0]
    cuts = np.cumsum([0, 512, 512, 512, 1024, 1024, 1024, 1024, 8, 8, 512, 512])
    seg = lambda i: w[:, cuts[i]:cuts[i + 1]]
    u, v, z, dq, dk, dv, dz, da, db, cq, cz = (seg(i) for i in range(11))
    w2 = x["w_in_2"][0]
    cuts2 = np.cumsum([0] + [1024] * 6 + [8, 2048, 2048])
    qa, ka, va, qb, kb, vb, fl, ga, gb = (w2[:, cuts2[i]:cuts2[i + 1]] for i in range(9))
    br = np.stack([x["w_branch_a_2"][0], x["w_branch_b_2"][0]])
    br = br.reshape(2, KT // 2, P, KT // 2, 2, P).transpose(3, 0, 2, 4, 1, 5).reshape(BR_UNITS, P, D)
    up = units(x["expert_u_2"][0].T).reshape(EXPERT_CHUNKS, KT, P, D)
    down = x["expert_v_2"][0].reshape(EXPERT_CHUNKS, KT, P, KT, P).transpose(0, 3, 2, 1, 4).reshape(EXPERT_CHUNKS, KT, P, D)
    small = np.stack([x["dn_dt_bias"][0], np.zeros(8, np.float32), x["dn_a_log"][0], x["b_forget_2"][0]])
    arrays = {
        "mem": features(x["mem"][0]),
        "x": features(x["x"][0]),
        "consts": shape_constants(),
        "gains": np.stack([column(x[n].reshape(-1)) for n in
                           ("mem_norm_g", "ln_g", "final_g", "norm_mix_gain_2", "norm_ffn_gain_2", "norm_final_gain_2")], 1),
        "conv": x["conv_w"][0].reshape(TAPS, 24, P).transpose(2, 1, 0),
        "w_abf": np.concatenate([da, db, fl], 1).reshape(KT, P, 24).transpose(1, 0, 2),
        "head_rows": np.broadcast_to(small.reshape(1, 32), (P, 32)),
        "dn_g": x["dn_norm_g"][0].reshape(P, 1),
        "gmlp_ln": np.concatenate([column(x["gmlp_ln_g"][0]), column(x["gmlp_ln_b"][0])], 1),
        "ws": x["gmlp_ws"][0].transpose(2, 0, 1),
        "bs": x["gmlp_bs"][0].reshape(1, GROUPS * P),
        "sub_keys": x["sub_keys_2"][0].reshape(16, P, P).transpose(2, 0, 1),
        "w_kv": units(x["w_mem_kv"][0]),
        "w_in": units(np.concatenate([cq, cz, z, dz, u, v, dq, dk, dv], 1)),
        "w_out": units(x["w_out"][0]),
        "w_in2": units(np.concatenate([ga, gb, qa, ka, va, qb, kb, vb], 1)),
        "w_br": br,
        "w_out2": units(x["w_out_2"][0]),
        "w_q": units(x["w_query_2"][0]),
        "w_exp": np.concatenate([(up if kind == "up" else down)[e] for kind, e in ORDER]),
    }
    arrays = {k: np.ascontiguousarray(v) for k, v in arrays.items()}
    nc = bacc.Bacc("TRN2", target_bir_lowering=False, num_devices=1)
    ap = {k: nc.dram_tensor(f"in_{k}", v.shape, mybir.dt.from_np(v.dtype), kind="ExternalInput").ap() for k, v in arrays.items()}
    out = nc.dram_tensor("out", (P, KT, S), F32, kind="ExternalOutput").ap()
    g_dram = nc.dram_tensor("gates", (16, P, P * 16), F32, kind="Internal").ap()
    program(nc, ap, out, g_dram)
    r = run_bass_kernel_spmd(nc, [{f"in_{k}": v for k, v in arrays.items()}], core_ids=[0])
    y = r.results[0]["out"]
    return y.transpose(2, 1, 0).reshape(1, S, D)
```

```python
import concourse.bass as bass
from concourse import mybir
from concourse.alu_op_type import AluOpType as ALU
from contextlib import ExitStack

F32 = mybir.dt.float32
F32R = mybir.dt.float32r
U32 = mybir.dt.uint32
ACT = mybir.ActivationFunctionType
AX = mybir.AxisListType.X

P = 128
D = 2048
KT = D // P
S = 256
TT = S // P
EPS = 1e-6
SCALE = float(P) ** -0.5
NEG_INF = -1e30
DN_HEADS = 8
HEADS = 8
XA_HEADS = 4
GROUPS = 4
CHUNK = 64
CHUNKS = S // CHUNK
LEVELS = 6
TAPS = 4
TOPK = 16
RING = 4
HALF = KT // 2
ONEHOTS = 16
GATE_GROUPS = (1, 1, 2) * 4

KV_UNITS, IN_UNITS, OUT_UNITS, IN2_UNITS, BR_UNITS = 8, 52, KT, 80, KT // 2 * 2
EXPERT_CHUNKS = 8
CHUNK_UNITS = 2 * KT
U_KV = 0
U_IN = U_KV + KV_UNITS
U_OUT = U_IN + IN_UNITS
U_IN2 = U_OUT + OUT_UNITS
U_BR = U_IN2 + IN2_UNITS
U_OUT2 = U_BR + BR_UNITS
U_Q = U_OUT2 + OUT_UNITS
U_EXP = U_Q + OUT_UNITS
U_END = U_EXP + EXPERT_CHUNKS * CHUNK_UNITS
AHEAD = 3

IDENT, ONES, TRI_LE, TRI_LT, TRI_GT, C64_LE, C64_GT, IOTA, LEVEL0 = range(9)
NCONST = LEVEL0 + LEVELS
G_MEM, G_LN, G_FINAL, G_MIX, G_FFN, G_OUT = range(6)


def shape_constants():
    import numpy as np
    a, b = np.arange(P)[:, None], np.arange(P)[None, :]
    same = (a // CHUNK) == (b // CHUNK)
    rows = [a == b, a >= 0 * b, a <= b, a < b, a > b, same & (a <= b), same & (a > b), 0 * a + b]
    for lev in range(LEVELS):
        s = 1 << lev
        rows.append((a // (2 * s) == b // (2 * s)) & (a // s < b // s))
    return np.ascontiguousarray(np.stack([(r + 0 * b).astype(np.float32) for r in rows], 1))


def expert_order():
    order = [("up", e) for e in range(AHEAD)] + [("down", 0)]
    for e in range(AHEAD, EXPERT_CHUNKS):
        order += [("up", e), ("down", e - AHEAD + 1)]
    return order + [("down", e) for e in range(EXPERT_CHUNKS - AHEAD + 1, EXPERT_CHUNKS)]


ORDER = expert_order()


def first_unit(kind, e):
    return U_EXP + KT * ORDER.index((kind, e))


class Chain:

    def __init__(self, eng, sem):
        self.eng, self.sem, self.n, self.steps = eng, sem, 0, 0

    def __call__(self, ins):
        ins.then_inc(self.sem, 1)
        self.n = self.n + 1
        self.steps += 1
        self.eng.wait_ge(self.sem, self.n)

    def loop(self, start, end, per, body):
        base, s0 = self.n, self.steps
        with self.eng.Fori(start, end) as i:
            self.n = i * per + (base - start * per)
            body(i)
        assert self.steps - s0 == per, (self.steps - s0, per)
        self.n = base + (end - start) * per


def program(nc, ap, out, g_dram):
    ctx = ExitStack()
    with ctx:
        base = [16512]

        def at(name, shape, off, dt=F32):
            return nc.alloc_sbuf_tensor_at(name, shape, dt, offset=off)

        def take(nbytes):
            off = base[0]
            base[0] += (nbytes + 31) // 32 * 32
            assert base[0] <= 229344, base[0]
            return off

        def sem(name):
            return ctx.enter_context(nc.semaphore(name))

        K = 1024
        raw = at("raw", [P, RING, KT, P], take(32 * K))
        whi = at("whi", [P, 4, HALF, P], take(16 * K), F32R)
        wlo = at("wlo", [P, 4, HALF, P], take(16 * K), F32R)
        X = at("X", [P, KT, S], take(16 * K))
        o_T = take(16 * K)
        T16 = at("T16", [P, KT, S], o_T)
        o_hi, o_lo = take(16 * K), take(16 * K)
        xhi = at("xhi", [P, KT, S], o_hi, F32R)
        xlo = at("xlo", [P, KT, S], o_lo, F32R)
        cst = at("cst", [P, NCONST, P], take(NCONST * 512))
        gains = at("gains", [P, 6, KT], take(6 * KT * 4))
        cw = at("cw", [P, 24, TAPS], take(24 * TAPS * 4))
        wab_hi = at("wab_hi", [P, KT, 24], take(KT * 24 * 4), F32R)
        wab_lo = at("wab_lo", [P, KT, 24], take(KT * 24 * 4), F32R)
        small = at("small", [P, 48], take(192))
        rstd = at("rstd", [P, S], take(S * 4))
        o_A = base[0]
        A = lambda k: o_A + int(k * K)

        def c(n):
            return cst[:, n, :]

        ab_bias, a_log, f_bias, eps = small[:, 16:32], small[:, 32:40], small[:, 40:48], small[:, 9:10]

        ident = c(IDENT)
        ones = c(ONES)

        mixed = at("mixed", [P, KT, S], A(0))
        qkv = at("qkv", [P, 24, S], A(16))
        cq = at("cq", [P, XA_HEADS, S], A(40))
        gv = at("gv", [P, GROUPS, S], A(44))
        gz = at("gz", [P, GROUPS, S], A(48))
        mk = at("mk", [P, XA_HEADS, S], A(52))
        mvt = at("mvt", [P, TT, XA_HEADS, P], A(56))
        stage = at("stage", [P, 2, S + TAPS - 1], A(60))
        ycv = at("ycv", [P, 2, S], A(62.25))
        mem_in = at("mem_in", [P, KT, S], A(16))
        wab = at("wab", [P, KT, 24], A(44))
        mvf = at("mvf", [P, XA_HEADS, S], A(32))
        xa_p = at("xa_p", [P, 8, S], o_T)
        xa_pt = at("xa_pt", [P, XA_HEADS, TT, S], o_T + 8 * K)
        vt = at("vt", [P, GROUPS, TT, P], o_T)
        vsq = at("vsq", [P, GROUPS, S], o_T + 4 * K)
        mean = at("mean", [P, S], o_T + 8 * K)
        wst = at("wst", [P, GROUPS, P], o_T + 10 * K)
        bs_row = at("bs_row", [1, GROUPS * P], o_T + 12 * K)
        kbg = at("kbg", [P, 16, P], o_hi)
        kd = at("kd", [P, 16, P], o_hi + 8 * K)
        at_ = at("at_", [P, 16, P], o_lo)
        ait = at("ait", [P, 16, P], o_lo + 8 * K)
        pt = at("pt", [P, 16, P], o_T)
        qt = at("qt", [P, 16, P], o_T + 8 * K)
        dec = at("dec", [P, 16, P], A(40))
        xt = at("xt", [P, 16, P], A(56))
        expr = at("expr", [P, 8, S], A(48))
        st = [at("st0", [P, 8, P], A(48)), at("st1", [P, 8, P], A(56))]
        vn = at("vn", [P, 8, P], A(52))
        odn = at("odn", [P, 8, S], o_lo)
        odn_sq = at("odn_sq", [P, 8, S], o_T)
        odn_rs = at("odn_rs", [P, 8, S], A(40))
        vb = at("vb", [P, 16, P], A(32))
        kcd = at("kcd", [P, 16, P], A(24))
        sm = A(64.5)
        nx = at("nx", [P, 16], sm)
        rs = at("rs", [P, 16], sm + 64)
        gbt = at("gbt", [P, TT, 2, 8], sm + 128)
        gcol = at("gcol", [P, TT, 2, 8], sm + 256)
        ecol = at("ecol", [P, TT, 2, 8], sm + 384)
        bex = at("bex", [P, TT, 8], sm + 512)
        gc8 = at("gc8", [8, S], sm + 640)
        bt8 = at("bt8", [8, S], sm + 640 + K)
        ab16 = at("ab16", [16, S], sm + 640)
        egl = at("egl", [P, 8, CHUNKS], sm + 640 + 2 * K)
        splus = at("splus", [P, TT, 8], sm + 768 + 2 * K)
        decay = at("decay", [P, 8], sm + 832 + 2 * K)
        qk_sq = at("qk_sq", [P, 8, S], o_T)
        qk_rs = at("qk_rs", [P, 8, S], o_T + 8 * K)
        qa = at("qa", [P, 8, S], o_T)
        ka = at("ka", [P, 8, S], o_T + 8 * K)
        va = at("va", [P, 8, S], A(0))
        qb = at("qb", [P, 8, S], A(8))
        kb = at("kb", [P, 8, S], A(16))
        vb2 = at("vb2", [P, 8, S], A(24))
        sga = at("sga", [P, KT, S], A(32))
        sgb = at("sgb", [P, KT, S], A(48))
        za = at("za", [P, 8, 384], o_hi)
        zb = at("zb", [P, 8, 384], o_hi + 12 * K)
        vtk = at("vtk", [P, 8, TT, P], o_hi + 24 * K)
        nfx = at("nfx", [P, 16], sm)
        rfx = at("rfx", [P, 16], sm + 64)
        fl = at("fl", [P, TT, 8], sm + 128)
        fcol = at("fcol", [P, TT, 8], sm + 192)
        f8 = at("f8", [8, S], sm + 128 + K)
        ft8 = at("ft8", [8, S], sm + 128 + K)
        cf8 = at("cf8", [8, S], sm + 128 + 2 * K)
        skt = at("skt", [P, 16, P], A(16))
        picks = at("picks", [P, TT, 3, P], A(24))
        sc = at("sc", [P, TT, 16, P], A(32))
        cand = at("cand", [P, 8, S], A(48))
        v16 = at("v16", [P, 16, TOPK], A(56))
        i16 = at("i16", [P, 16, TOPK], A(57), U32)
        if16 = at("if16", [P, 16, TOPK], A(58))
        ts = at("ts", [P, 8, TOPK], A(59))
        ti = at("ti", [P, 8, TOPK], A(59.5), U32)
        th = at("th", [P, 8, TOPK], A(60), U32)
        tl = at("tl", [P, 8, TOPK], A(60.5), U32)
        thf = at("thf", [P, 8, TOPK], A(61))
        tlf = at("tlf", [P, 8, TOPK], A(61.5))
        gs = at("gs", [P, 8], A(62))
        rest = at("rest", [P, 2 * P], A(63))
        sel = at("sel", [P, 3, S], A(64.25))
        oh1 = at("oh1", [P, ONEHOTS, P], A(48))
        oh2 = at("oh2", [P, ONEHOTS, P], A(56))
        gst = at("gst", [P, 2, P, 16], A(32))
        offs = (o_T, A(0), A(16))
        hidden = [at(f"hidden{n}", [P, KT, S], o) for n, o in enumerate(offs)]
        hid_lower = [at(f"hid_lower{n}", [P, KT, S], o, F32R) for n, o in enumerate(offs)]
        hid_upper = at("hid_upper", [P, KT, S], A(32), F32R)
        gch = at("gch", [P, 16, KT, 16], A(48))

        banks = ctx.enter_context(nc.psum_tensor("banks", [P, 8, 512], F32))
        unit_ps = banks[:, 0:2, :]
        ps = banks[:, 2:8, :]
        psf = ps.rearrange("p b n -> p (b n)")
        ps_a = banks[:, 4:8, :].rearrange("p b n -> p (b n)")
        ps_b = banks[:, 0:4, :].rearrange("p b n -> p (b n)")

        raw_in = [sem(f"raw_in{r}") for r in range(RING)]
        hi_ready, lo_ready, pe_half = sem("hi_ready"), sem("lo_ready"), sem("pe_half")
        evac = [sem("evac0"), sem("evac1")]
        v_chain, a_chain = sem("v_chain"), sem("a_chain")
        cst_in, x_ld, ws_ld, sk_ld, out_st = (sem(n) for n in ("cst_in", "x_ld", "ws_ld", "sk_ld", "out_st"))
        mem_ld = [sem(f"mem_ld{q}") for q in range(4)]
        norm_sq, norm_sum, norm_std = (sem(n) for n in ("norm_sq", "norm_sum", "norm_std"))
        lin_src, lin_hi, lin_lo, lin_lo2 = sem("lin_src"), sem("lin_hi"), sem("lin_lo"), sem("lin_lo2")
        conv_y, conv_used = sem("conv_y"), sem("conv_used")
        signals = {}

        def sg(name):
            if name not in signals:
                signals[name] = sem(name)
            return signals[name]


        def gated(e):
            up = hid_upper if e < EXPERT_CHUNKS - 2 else (xhi, xlo)[e % 2]
            return up, hid_lower[e % 3]

        GH = HEADS // 2
        SCORES = GH * 3 * P
        at_banks = (ps_a, ps_b)
        za_g = [za[:].rearrange("p h n -> p (h n)")[:, g * SCORES:(g + 1) * SCORES] for g in range(2)]
        zb_g = [zb[:].rearrange("p h n -> p (h n)")[:, g * SCORES:(g + 1) * SCORES] for g in range(2)]

        def pq(g):
            two = banks[:, 6:8, :] if g % 2 == 0 else banks[:, 0:2, :]
            return two[:, 0, :], two[:, 1, :]

        block = ctx.enter_context(nc.Block())

        @block.sync
        def _(sp):
            for q in range(4):
                sp.dma_start(mem_in[:, 4 * q:4 * q + 4, :], ap["mem"][:, 4 * q:4 * q + 4, :]).then_inc(mem_ld[q], 16)
            sp.dma_start(cst[:], ap["consts"]).then_inc(cst_in, 16)
            sp.dma_start(gains[:], ap["gains"]).then_inc(cst_in, 16)
            sp.dma_start(cw[:], ap["conv"]).then_inc(cst_in, 16)
            sp.dma_start(wab[:], ap["w_abf"]).then_inc(cst_in, 16)
            sp.dma_start(small[:, 0:1], ap["dn_g"]).then_inc(cst_in, 16)
            sp.dma_start(small[:, 1:9], ap["gmlp_ln"]).then_inc(cst_in, 16)
            sp.dma_start(small[:, 16:48], ap["head_rows"]).then_inc(cst_in, 16)
            sp.dma_start(X[:], ap["x"]).then_inc(x_ld, 16)

            def load(src, u0, i, j):
                lead = i * 8 + (2 * (u0 + j) - 6)
                if not (isinstance(lead, int) and lead <= 0):
                    sp.wait_ge(lo_ready, lead)
                n = i * RING + j
                sp.dma_start(raw[:, j, :, :].rearrange("p k m -> p (k m)"),
                             src[bass.ds(n, 1)].rearrange("a p n -> p (a n)")).then_inc(raw_in[j], 16)

            def stream(src, n, u0, first=0):
                with sp.Fori(first, n // RING) as i:
                    for j in range(RING):
                        load(src, u0, i, j)

            for i in range(KV_UNITS // RING):
                for j in range(RING):
                    load(ap["w_kv"], U_KV, i, j)
            stream(ap["w_in"], 28, U_IN)
            sp.wait_ge(sg("xa_out"), 1)
            sp.dma_start(wst[:], ap["ws"]).then_inc(ws_ld, 16)
            sp.dma_start(bs_row[:], ap["bs"]).then_inc(ws_ld, 16)
            stream(ap["w_in"], IN_UNITS, U_IN, 28 // RING)
            for j in range(RING):
                load(ap["w_out"], U_OUT, 0, j)
            stream(ap["w_out"], OUT_UNITS, U_OUT, 1)
            stream(ap["w_in2"], IN2_UNITS, U_IN2)
            stream(ap["w_br"], BR_UNITS, U_BR)
            stream(ap["w_out2"], OUT_UNITS, U_OUT2)
            sp.wait_ge(lin_lo2, 2 * 6)
            sp.dma_start(skt[:], ap["sub_keys"]).then_inc(sk_ld, 16)
            stream(ap["w_q"], OUT_UNITS, U_Q)
            stream(ap["w_exp"], EXPERT_CHUNKS * CHUNK_UNITS, U_EXP)

        @block.gpsimd
        def _(pool):
            def lower(u0, u1):
                with pool.Fori(u0 // RING, u1 // RING) as i:
                    for j in range(RING):
                        for h in range(2):
                            s = (2 * j + h) % 4
                            pool.wait_ge(hi_ready, i * 8 + (2 * j + h + 1))
                            pool.tensor_tensor(wlo[:, s, :, :], raw[:, j, h * HALF:(h + 1) * HALF, :],
                                               whi[:, s, :, :].bitcast(F32), ALU.subtract).then_inc(lo_ready, 1)

            lower(0, U_OUT)
            pool.wait_ge(sg("exp_row"), 1)
            pool.wait_ge(sg("qk"), 1)
            pool.tensor_tensor(qkv[:, 0:8, :], qkv[:, 0:8, :], expr[:], ALU.mult).then_inc(sg("q_decayed"), 1)
            lower(U_OUT, U_END)

        @block.scalar
        def _(act):
            step = Chain(act, a_chain)

            def conv_unit(i, u0, d):
                j = d % RING
                act.wait_ge(raw_in[j], i * 16 + 16 * ((u0 + d) // RING + 1))
                for h in range(2):
                    lead = i * 8 + (2 * (u0 + d) + h - 3)
                    if not (isinstance(i, int) and lead <= 0):
                        act.wait_ge(pe_half, lead)
                    act.activation(whi[:, (2 * j + h) % 4, :, :], raw[:, j, h * HALF:(h + 1) * HALF, :],
                                   ACT.Copy).then_inc(hi_ready, 1)

            def segment(u0, n, body=None, first=False, after=None):
                def run(i):
                    for j in range(RING):
                        if u0 + j + 1 < U_END or not isinstance(i, int):
                            conv_unit(i, u0, j + 1)
                        if body:
                            body(i, j, u0)
                        if after and j in after:
                            after[j]()
                if after is not None:
                    assert n == RING
                    return run(0)
                if first:
                    run(0)
                with act.Fori(1 if first else 0, n // RING) as i:
                    run(i)

            def into(dst, func):
                def body(i, j, u0):
                    act.wait_ge(pe_half, i * 8 + (2 * (u0 + j) + 2))
                    act.activation(dst[:, bass.ds(i * RING + j, 1), :], unit_ps[:, j % 2:j % 2 + 1, 0:S], func
                                   ).then_inc(evac[j % 2], 1)
                return body

            def wait_units(u):
                act.wait_ge(evac[0], u // 2)
                act.wait_ge(evac[1], u // 2)

            def norm_squares(n, src, ready):
                for q in range(4):
                    act.wait_ge(*ready[q])
                    act.activation(T16[:, 4 * q:4 * q + 4, :], src[:, 4 * q:4 * q + 4, :], ACT.Square).then_inc(norm_sq, 1)

            def residual_segment(n, u0):
                segment(u0, 8)
                for q in range(4):
                    act.wait_ge(evac[0], (u0 + 4 * q + 4) // 2)
                    act.wait_ge(evac[1], (u0 + 4 * q + 4) // 2)
                    act.activation(T16[:, 4 * q:4 * q + 4, :], X[:, 4 * q:4 * q + 4, :], ACT.Square).then_inc(norm_sq, 1)
                    if q < 1 or (q < 2 and u0 + KT < U_END):
                        segment(u0 + 8 + 4 * q, 4)
                    elif q == 1:
                        segment(u0 + 12, 4, after={})

            def rsqrt_of(dst, sums, n):
                step(act.activation(dst, sums, ACT.Ln, scale=1.0 / n, bias=eps))
                return act.activation(dst, dst, ACT.Exp, scale=-0.5)

            def norm_root(n):
                act.wait_ge(norm_sum, n + 1)
                if n == 0:
                    act.wait_ge(sg("eps_set"), 1)
                rsqrt_of(rstd[:], psf[:, 0:S], D).then_inc(norm_std, 1)

            def upper(ready, src=T16):
                for q in range(4):
                    act.wait_ge(*ready[q])
                    act.activation(xhi[:, 4 * q:4 * q + 4, :], src[:, 4 * q:4 * q + 4, :], ACT.Copy).then_inc(lin_hi, 1)

            norm_squares(0, mem_in, [(mem_ld[q], 16) for q in range(4)])
            act.wait_ge(cst_in, 16 * 7)
            act.activation(wab_hi[:], wab[:], ACT.Copy).then_inc(sg("wab_hi"), 1)
            conv_unit(0, 0, 0)
            norm_root(0)
            upper([(lin_src, q + 1) for q in range(4)])
            segment(U_KV, KV_UNITS, first=True)
            act.wait_ge(x_ld, 16)
            act.wait_ge(lin_lo2, 2)
            norm_squares(1, X, [(x_ld, 16)] * 4)
            norm_root(1)
            act.wait_ge(sg("kv_done"), 1)
            upper([(lin_src, 4 + q + 1) for q in range(4)])
            segment(U_IN, 4)
            cz = mixed[:, 12:16, :]
            segment(U_IN + 4, 4, into(cz, ACT.Silu))
            segment(U_IN + 8, 4, into(gz, ACT.Silu))
            act.wait_ge(sg("ab_in"), 1)
            step(act.activation(splus[:], gbt[:, :, 0, :], ACT.Abs))
            step(act.activation(splus[:], splus[:], ACT.Exp, scale=-1.0))
            step(act.activation(splus[:], splus[:], ACT.Ln, bias=1.0))
            act.activation(decay[:], a_log, ACT.Exp).then_inc(sg("softplus"), 1)
            act.activation(gbt[:, :, 1, :], gbt[:, :, 1, :], ACT.Sigmoid).then_inc(sg("beta"), 1)
            segment(U_IN + 12, 4, into(mixed[:, 0:4, :], ACT.Gelu_apprx_tanh))
            act.wait_ge(sg("xa_max"), 1)
            for n in range(8):
                act.activation(xa_p[:, n, :], psf[:, 1024 + n * S:1024 + (n + 1) * S], ACT.Exp, bias=nx[:, n:n + 1],
                               accum_out=rs[:, n:n + 1]).then_inc(sg("xa_exp"), 1)
            segment(U_IN + 16, 4, into(gv, ACT.Gelu_apprx_tanh))
            segment(U_IN + 20, 4, into(mixed[:, 4:8, :], ACT.Silu))

            def centred_squares():
                act.wait_ge(sg("ln_centred"), 1)
                act.activation(vsq[:], gv[:], ACT.Square).then_inc(sg("ln_sq"), 1)

            segment(U_IN + 24, 4, into(mixed[:, 8:12, :], ACT.Silu), after={1: centred_squares})

            def exp_sums():
                act.wait_ge(sg("gcol_in"), 1)
                act.activation(ecol[:], gcol[:], ACT.Exp).then_inc(sg("ecol"), 1)

            def layer_std():
                act.wait_ge(sg("ln_sqsum"), 1)
                rsqrt_of(rstd[:], psf[:, 1536:1536 + S], GROUPS * P).then_inc(sg("ln_std"), 1)

            def head_squares(w):
                if w == 0:
                    act.wait_ge(sg("sgu"), 1)
                act.activation(qk_sq[:], qkv[:, 8 * w:8 * w + 8, :], ACT.Square).then_inc(sg("qk_sq"), 1)

            def head_norms(w):
                act.wait_ge(sg("qk_ss"), w + 1)
                if w:
                    act.wait_ge(sg("qk_scaled"), w)
                rsqrt_of(qk_rs[:].rearrange("p h n -> p (h n)"), ps_a, 1).then_inc(sg("qk_rs"), 1)

            def conv_quad(i, after={}):
                for j in range(RING):
                    conv_unit(i, U_IN + 28, j + 1)
                    if i or j:
                        act.wait_ge(conv_y, i * 4 + j)
                        act.activation(qkv[:, bass.ds(i * RING + (j - 1), 1), :], ycv[:, (j + 1) % 2:(j + 1) % 2 + 1, :], ACT.Silu
                                       ).then_inc(conv_used, 1)
                    if j in after:
                        after[j]()

            conv_quad(0, {1: layer_std, 2: exp_sums})
            conv_quad(1)
            conv_quad(2)
            conv_quad(3, {1: lambda: head_squares(0)})
            conv_quad(4, {1: lambda: head_norms(0), 2: lambda: head_squares(1)})
            conv_quad(5, {2: lambda: head_norms(1)})
            act.wait_ge(conv_y, 24)
            act.activation(qkv[:, 23, :], ycv[:, 1, :], ACT.Silu).then_inc(conv_used, 1)

            act.wait_ge(sg("dec_arg"), 16)
            act.activation(expr[:].rearrange("p h n -> p (h n)"), ps_a, ACT.Exp).then_inc(sg("exp_row"), 1)
            act.activation(dec[:], dec[:], ACT.Exp).then_inc(sg("dec_exp"), 1)

            act.wait_ge(sg("k_t"), 1)
            act.wait_ge(sg("kbg"), 2)
            for n in range(16):
                h, t = n // 2, n % 2
                act.activation(kd[:, n, :], ps_b[:, n * P:(n + 1) * P], ACT.Copy, scale=ecol[:, t, 1, h:h + 1]).then_inc(sg("kd"), 1)
            act.wait_ge(sg("v_dt"), 1)
            for n in range(16):
                h, t = n // 2, n % 2
                act.activation(vb[:, n, :], ps_b[:, n * P:(n + 1) * P], ACT.Copy, scale=gbt[:, t, 1, h:h + 1]).then_inc(sg("vb"), 1)
            for g in range(4):
                act.wait_ge(sg("inv_p0"), g + 1)
                act.activation(pt[:, 4 * g:4 * g + 4, :].rearrange("p a n -> p (a n)"), ps[:, g, :], ACT.Copy
                               ).then_inc(sg("inv_upd"), 1)
            with act.Fori(1, LEVELS) as lev:
                for g in range(4):
                    act.wait_ge(sg("inv_x"), lev * 4 + (g - 3))
                    act.activation(xt[:, 4 * g:4 * g + 4, :].rearrange("p a n -> p (a n)"), ps[:, g, :], ACT.Copy
                                   ).then_inc(sg("inv_xc"), 1)
            act.wait_ge(sg("kcd_mm"), 1)
            act.activation(kcd[:].rearrange("p a n -> p (a n)"), psf[:, 0:2048], ACT.Copy, scale=-1.0).then_inc(sg("kcd"), 1)
            for cch in range(CHUNKS):
                cols = slice(cch * CHUNK, (cch + 1) * CHUNK)
                act.wait_ge(sg("odn_ss"), cch + 1)
                rsqrt_of(odn_rs[:, :, cols], ps[:, 5, :].rearrange("p (h n) -> p h n", h=8), P).then_inc(sg("odn_rs"), 1)

            upper([(sg("mixed_done"), 1)] + [(sg("mixed_done"), CHUNKS)] * 3, mixed)
            residual_segment(2, U_OUT)
            norm_root(2)
            norm_squares(3, X, [(sg("x2_done"), q + 1) for q in range(4)])
            norm_root(3)
            upper([(lin_src, 8 + q + 1) for q in range(4)])
            segment(U_IN2, 16, into(sga, ACT.Sigmoid))
            segment(U_IN2 + 16, 16, into(sgb, ACT.Sigmoid))
            act.wait_ge(sg("f_in"), 1)
            step(act.activation(fl[:], fcol[:], ACT.Abs))
            step(act.activation(fl[:], fl[:], ACT.Exp, scale=-1.0))
            act.activation(fl[:], fl[:], ACT.Ln, bias=1.0).then_inc(sg("f_ln"), 1)
            segment(U_IN2 + 32, 48)
            for g in range(2):
                act.wait_ge(sg("sb_z"), g + 1)
                step(act.activation(za_g[g], at_banks[g][:, 0:SCORES], ACT.Abs))
                step(act.activation(za_g[g], za_g[g], ACT.Exp, scale=-1.0))
                act.activation(za_g[g], za_g[g], ACT.Ln, bias=1.0).then_inc(sg("sb_ln"), 1)
            for g in range(2):
                act.wait_ge(sg("sb_arg"), g + 1)
                act.activation(zb_g[g], zb_g[g], ACT.Exp).then_inc(sg("sb_exp"), 1)
            for g in range(2):
                act.wait_ge(sg("fx_max"), g + 1)
                for n in range(2 * GH):
                    src = za_g[g][:, n * P:(n + 1) * P] if n < GH else za_g[g][:, GH * P + (n - GH) * S:GH * P + (n - GH + 1) * S]
                    col = slice(2 * GH * g + n, 2 * GH * g + n + 1)
                    act.activation(src, src, ACT.Exp, bias=nfx[:, col], accum_out=rfx[:, col]).then_inc(sg("fx_exp"), 1)
            for g in range(2):
                act.wait_ge(sg("fx_pt_mm"), g + 1)
                act.activation(zb_g[g], at_banks[g][:, 0:SCORES], ACT.Copy).then_inc(sg("fx_pt"), 1)
            upper([(sg("sb_done"), 1), (sg("sb_done"), 2), (sg("fx_done"), 1), (sg("fx_done"), 2)])
            segment(U_BR, BR_UNITS)
            upper([(sg("merged"), KT // 2)] * 4, sga)
            residual_segment(4, U_OUT2)
            norm_root(4)
            upper([(lin_src, 12 + q + 1) for q in range(4)])
            segment(U_Q, OUT_UNITS)
            def gather(g16):
                b = g16 % 2
                if g16 >= 2:
                    act.wait_ge(sg(f"gate_store{b}"), g16 // 2 * 16)
                for q in range(4):
                    act.wait_ge(sg("gate_mm"), g16 * 16 + (4 * q + 4))
                    act.activation(gst[:, b, :, 4 * q:4 * q + 4].rearrange("p e t -> p t e"),
                                   ps[:, q, :].rearrange("p (t e) -> p t e", t=4), ACT.Copy).then_inc(sg("gate_out"), 1)
                act.wait_ge(sg("gate_out"), g16 * 4 + 4)
                act.dma_start(g_dram[g16],
                              gst[:, b, :, :].rearrange("p e t -> p (e t)")).then_inc(sg(f"gate_store{b}"), 16)

            def load_gates(e):
                if e:
                    act.wait_ge(sg("gates_used"), 4 * e)
                else:
                    for b in range(2):
                        act.wait_ge(sg(f"gate_store{b}"), 8 * 16)
                act.dma_start(gch[:], g_dram[:, :, e * (KT * 16):(e + 1) * (KT * 16)].rearrange("g p n -> p g n")
                              ).then_inc(sg("gate_in"), 16)

            def exp_gates():
                act.wait_ge(sg("gate_arg"), 1)
                g3 = picks[:, :, 2, :]
                act.activation(g3, g3, ACT.Exp).then_inc(sg("gate_exp"), 1)

            for kind, e in ORDER:
                u0 = first_unit(kind, e)
                gelu = into(hidden[e % 3], ACT.Gelu_apprx_tanh) if kind == "up" else None
                quarter = lambda q, after: segment(u0 + 4 * q, 4, gelu and into_at(hidden[e % 3], 4 * q), after=after)
                into_at = lambda dst, k0: into(dst[:, k0:k0 + 4, :], ACT.Gelu_apprx_tanh)
                if (kind, e) == ("up", 1):
                    segment(u0, 12, gelu)
                    exp_gates()
                    quarter(3, {})
                elif (kind, e) == ("up", 2):
                    done = 0
                    for q in range(3):
                        after = {}
                        for j in range(4):
                            n = GATE_GROUPS[4 * q + j]
                            after[j] = lambda g0=done, n=n: [gather(g) for g in range(g0, g0 + n)]
                            done += n
                        quarter(q, after)
                    quarter(3, {0: lambda: load_gates(0)})
                elif (kind, e) == ("up", EXPERT_CHUNKS - 1):
                    segment(u0, 12, gelu)
                    load_gates(EXPERT_CHUNKS - 2)
                    quarter(3, {})
                elif kind == "up":
                    segment(u0, KT, gelu)
                elif e < EXPERT_CHUNKS - 3:
                    segment(u0, 4)
                    load_gates(e + 1)
                    segment(u0 + 4, 12)
                elif e == EXPERT_CHUNKS - 3:
                    segment(u0, 12)
                    quarter(3, {0: lambda: load_gates(EXPERT_CHUNKS - 1)})
                elif e == EXPERT_CHUNKS - 2:
                    segment(u0, KT)
                else:
                    residual_segment(5, u0)
            norm_root(5)
            for q in range(4):
                act.wait_ge(sg("result"), q + 1)
                act.dma_start(out[:, 4 * q:4 * q + 4, :], T16[:, 4 * q:4 * q + 4, :]).then_inc(out_st, 16)
            act.wait_ge(out_st, 4 * 16)

        @block.vector
        def _(dve):
            step = Chain(dve, v_chain)

            def norm(n, src, gain, dst, low=None, done=None):
                dve.wait_ge(norm_std, n + 1)
                for k in range(KT):
                    ins = dve.scalar_tensor_tensor(dst[:, k, :], src[:, k, :], gains[:, gain, k:k + 1], rstd[:],
                                                   ALU.mult, ALU.mult)
                    if k % 4 == 3:
                        ins.then_inc(lin_src if done is None else done, 1)
                    if done is None and k == 11:
                        lower_half(low, 0)
                if done is None:
                    lower_half(low, 1)

            def lower_half(n, half, src=T16):
                for q in (2 * half, 2 * half + 1):
                    dve.wait_ge(lin_hi, 4 * n + q + 1)
                    dve.tensor_tensor(xlo[:, 4 * q:4 * q + 4, :], src[:, 4 * q:4 * q + 4, :],
                                      xhi[:, 4 * q:4 * q + 4, :].bitcast(F32), ALU.subtract).then_inc((lin_lo, lin_lo2)[half], 1)

            def lower(n, src=T16):
                lower_half(n, 0, src)
                lower_half(n, 1, src)

            def segment(u0, n, body):
                with dve.Fori(0, n // RING) as i:
                    for j in range(RING):
                        dve.wait_ge(pe_half, i * 8 + (2 * (u0 + j) + 2))
                        body(i, j).then_inc(evac[j % 2], 1)

            def blk(t, i, j):
                return t[:, bass.ds(i * RING + j, 1), :]

            def into(dst, scale=None):
                def body(i, j):
                    src = unit_ps[:, j % 2:j % 2 + 1, 0:S]
                    if scale is None:
                        return dve.tensor_copy(blk(dst, i, j), src)
                    return dve.tensor_scalar(blk(dst, i, j), src, scale, None, ALU.mult)
                return body

            def add_to_x(i, j):
                return dve.tensor_tensor(blk(X, i, j), unit_ps[:, j % 2:j % 2 + 1, 0:S], blk(X, i, j), ALU.add)

            dve.memset(stage[:], 0.0).then_inc(sg("stage_zero"), 1)
            dve.wait_ge(cst_in, 16 * 7)
            dve.wait_ge(sg("wab_hi"), 1)
            dve.tensor_tensor(wab_lo[:], wab[:], wab_hi[:].bitcast(F32), ALU.subtract).then_inc(sg("wab_lo"), 1)
            dve.memset(eps, EPS).then_inc(sg("eps_set"), 1)
            for q in range(4):
                dve.wait_ge(mem_ld[q], 16)
            norm(0, mem_in, G_MEM, T16, 0)
            segment(U_KV, 4, into(mk))
            segment(U_KV + 4, 4, into(mvf))
            dve.wait_ge(evac[0], KV_UNITS // 2)
            dve.wait_ge(evac[1], KV_UNITS // 2)
            dve.wait_ge(x_ld, 16)
            dve.wait_ge(sg("mv_t"), 1)
            dve.tensor_copy(mvt[:].rearrange("p a h n -> p (a h n)"), psf[:, 1024:2048]).then_inc(sg("kv_done"), 1)
            norm(1, X, G_LN, T16, 1)
            segment(U_IN, 4, into(cq, SCALE))
            dve.wait_ge(sg("ab_mm"), 1)
            dve.tensor_copy(ab16[:], psf[0:16, 0:S]).then_inc(sg("ab_row"), 1)
            dve.wait_ge(sg("ab_t"), 1)
            dve.tensor_tensor(gbt[:].rearrange("p a b h -> p a (b h)"), psf[:, S:S + 32].rearrange("p (a n) -> p a n", a=TT),
                              ab_bias.unsqueeze(1).broadcast_to([P, TT, 16]), ALU.add).then_inc(sg("ab_in"), 1)
            f3 = lambda t: t[:].rearrange("p a n -> p (a n)")
            sc4 = psf[:, 1024:3072].rearrange("p (n m) -> p n m", m=S)
            dve.wait_ge(sg("xa_scores"), 1)
            dve.tensor_reduce(nx[:, 0:8], sc4, AX, ALU.max, negate=True).then_inc(sg("xa_max"), 1)
            dve.wait_ge(sg("softplus"), 1)
            g_ = gbt[:, :, 0, :]
            step(dve.scalar_tensor_tensor(g_, g_, 0.0, splus[:], ALU.max, ALU.add))
            dve.scalar_tensor_tensor(g_, g_, -1.0, decay[:].unsqueeze(1).broadcast_to([P, TT, 8]), ALU.mult, ALU.mult).then_inc(sg("g_col"), 1)
            dve.wait_ge(sg("xa_exp"), 8)
            step(dve.reciprocal(rs[:, 0:8], rs[:, 0:8]))
            dve.tensor_tensor(xa_p[:], xa_p[:], rs[:, 0:8].unsqueeze(2).broadcast_to([P, 8, S]), ALU.mult).then_inc(sg("xa_norm"), 1)
            dve.wait_ge(sg("xa_pt_mm"), 1)
            dve.tensor_copy(xa_pt[:].rearrange("p h a n -> p (h a n)"), psf[:, 1024:3072]).then_inc(sg("xa_pt"), 1)
            dve.wait_ge(sg("xa_out"), 1)
            dve.tensor_tensor(mixed[:, 12:16, :].rearrange("p h n -> p (h n)"), psf[:, 0:1024],
                              mixed[:, 12:16, :].rearrange("p h n -> p (h n)"), ALU.mult).then_inc(sg("xa_done"), 1)
            dve.wait_ge(sg("ln_sum"), 1)
            step(dve.tensor_scalar(mean[:], psf[:, 1024:1024 + S], 1.0 / (GROUPS * P), None, ALU.mult))
            dve.tensor_tensor(gv[:], gv[:], mean[:].unsqueeze(1).broadcast_to([P, GROUPS, S]), ALU.subtract).then_inc(sg("ln_centred"), 1)
            dve.wait_ge(ws_ld, 32)
            dve.tensor_tensor(wst[:], wst[:], c(TRI_LE).unsqueeze(1).broadcast_to([P, GROUPS, P]), ALU.mult).then_inc(sg("ws_masked"), 1)
            dve.wait_ge(sg("gsum_mm"), 1)
            step(dve.tensor_copy(gc8[:], psf[0:8, 512:512 + S]))
            step(dve.tensor_copy(bt8[:], psf[0:8, 256:512]))
            dve.tensor_copy(gcol[:].rearrange("p a b h -> p (a b h)"), psf[:, 768:800]).then_inc(sg("gcol_in"), 1)

            dve.wait_ge(sg("stage_zero"), 1)

            def conv(i):
                for j in range(RING):
                    s = stage[:, j % 2, :]
                    w = lambda k: cw[:, bass.ds(i * RING + j, 1), k:k + 1].rearrange("p a k -> p (a k)")
                    y = ycv[:, j % 2, :]
                    dve.wait_ge(pe_half, i * 8 + (2 * (U_IN + 28 + j) + 2))
                    dve.tensor_copy(s[:, TAPS - 1:], unit_ps[:, j % 2, 0:S]).then_inc(evac[j % 2], 1)
                    dve.wait_ge(evac[j % 2], i * 2 + ((U_IN + 28) // 2 + j // 2 + 1))
                    if j >= 2 or i:
                        dve.wait_ge(conv_used, i * 4 + (j - 1))
                    step(dve.tensor_scalar(y, s[:, 0:S], w(0), None, ALU.mult))
                    for k in range(1, TAPS):
                        ins = dve.scalar_tensor_tensor(y, s[:, k:k + S], w(k), y, ALU.mult, ALU.add)
                        if k < TAPS - 1:
                            step(ins)
                        else:
                            ins.then_inc(conv_y, 1)

            def scale_heads(w):
                t = qkv[:, 8 * w:8 * w + 8, :]
                dve.wait_ge(sg("qk_rs"), w + 1)
                dve.scalar_tensor_tensor(t, qk_rs[:], (SCALE, 1.0)[w], t, ALU.mult, ALU.mult).then_inc(sg("qk_scaled"), 1)

            conv(0)
            dve.wait_ge(sg("ecol"), 1)
            step(dve.tensor_tensor(bex[:], gbt[:, :, 1, :], ecol[:, :, 0, :], ALU.mult))
            dve.wait_ge(sg("ln_std"), 1)
            step(dve.tensor_tensor(gv[:], gv[:], rstd[:].unsqueeze(1).broadcast_to([P, GROUPS, S]), ALU.mult))
            for g in range(GROUPS):
                ins = dve.tensor_scalar(gv[:, g, :], gv[:, g, :], small[:, 1 + g:2 + g], small[:, 5 + g:6 + g], ALU.mult, ALU.add)
            ins.then_inc(sg("ln_out"), 1)
            conv(1)
            dve.wait_ge(sg("v_t"), 1)
            dve.tensor_copy(vt[:].rearrange("p g a n -> p (g a n)"), psf[:, 2048:3072]).then_inc(sg("v_tc"), 1)
            conv(2)
            dve.wait_ge(sg("sgu"), 1)
            oa = mixed[:, 0:4, :].rearrange("p g n -> p (g n)")
            dve.tensor_tensor(oa, psf[:, 1024:2048], oa, ALU.mult).then_inc(sg("gmlp_out"), 1)
            dve.wait_ge(sg("gmlp_out"), 1)
            step(dve.tensor_tensor(oa, oa, gz[:].rearrange("p g n -> p (g n)"), ALU.mult))
            conv(3)
            conv(4)
            scale_heads(0)
            conv(5)
            scale_heads(1)

            v4 = lambda t: t[:].rearrange("p (h a) n -> p h a n", a=2)
            pk = ps_b.rearrange("p (h a n) -> p h a n", h=8, a=2)
            dve.wait_ge(sg("row_bc"), 1)
            for h in range(8):
                for t in range(TT):
                    dve.tensor_scalar(dec[:, 2 * h + t, :], ps_a[:, h * S + t * P:h * S + (t + 1) * P],
                                      gcol[:, t, 0, h:h + 1], 0.0, ALU.subtract, ALU.min).then_inc(sg("dec_arg"), 1)
            dve.wait_ge(sg("k_t"), 1)
            for t in range(TT):
                dve.tensor_tensor(v4(kbg)[:, :, t, :], pk[:, :, t, :], bex[:, t, :].unsqueeze(2).broadcast_to([P, 8, P]), ALU.mult).then_inc(sg("kbg"), 1)
            dve.wait_ge(sg("dec_exp"), 1)
            step(dve.tensor_tensor(dec[:], dec[:], c(C64_LE).unsqueeze(1).broadcast_to([P, 16, P]), ALU.mult))
            dve.wait_ge(sg("kk"), 1)
            dve.tensor_tensor(f3(at_), ps_a, f3(dec), ALU.mult).then_inc(sg("kk_out"), 1)
            dve.wait_ge(sg("qk"), 1)
            dve.tensor_tensor(f3(ait), ps_a, f3(dec), ALU.mult).then_inc(sg("qk_out"), 1)
            dve.wait_ge(sg("exp_row"), 1)
            step(dve.tensor_copy(egl[:], expr[:].rearrange("p h (c n) -> p h c n", n=CHUNK)[:, :, :, CHUNK - 1]))
            dve.wait_ge(sg("beta_bc"), 1)
            dve.wait_ge(sg("kk_out"), 1)
            four = lambda t, g: t[:, 4 * g:4 * g + 4, :]
            flat4 = lambda t, g: four(t, g).rearrange("p a n -> p (a n)")
            for g in range(4):
                step(dve.tensor_tensor(flat4(at_, g), ps_b[:, g * 512:(g + 1) * 512], flat4(at_, g), ALU.mult))
                step(dve.tensor_tensor(four(dec, g), four(at_, g), c(LEVEL0).unsqueeze(1).broadcast_to([P, 4, P]), ALU.mult))
                dve.tensor_tensor(four(qt, g), ident.unsqueeze(1).broadcast_to([P, 4, P]), four(dec, g), ALU.subtract).then_inc(sg("inv_q0"), 1)
            dve.wait_ge(sg("inv_q0"), 4)
            for g in range(4):
                dve.tensor_tensor(four(dec, g), four(at_, g), c(LEVEL0 + 1).unsqueeze(1).broadcast_to([P, 4, P]), ALU.mult).then_inc(sg("inv_a"), 1)

            def level(lev, last=False):
                if not last:
                    for g in range(4):
                        m = cst[:, bass.ds(lev + (LEVEL0 + 1), 1), :].broadcast_to([P, 4, P])
                        dve.wait_ge(sg("inv_x"), lev * 4 + (g - 3))
                        dve.tensor_tensor(four(dec, g), four(at_, g), m, ALU.mult).then_inc(sg("inv_a"), 1)
                for g in range(4):
                    dve.wait_ge(sg("inv_pq"), lev * 4 + (g - 3))
                    step(dve.tensor_tensor(flat4(pt, g), flat4(pt, g), pq(g)[0], ALU.subtract))
                    dve.tensor_tensor(flat4(qt, g), flat4(qt, g), pq(g)[1], ALU.subtract).then_inc(sg("inv_upd"), 1)

            step.loop(1, LEVELS - 1, 4, level)
            level(LEVELS - 1, last=True)
            def finish(cch):
                cols = slice(cch * CHUNK, (cch + 1) * CHUNK)
                o, gate = odn[:, :, cols], mixed[:, 4:12, cols]
                dve.wait_ge(sg("odn_rs"), cch + 1)
                step(dve.scalar_tensor_tensor(o, o, small[:, 0:1], odn_rs[:, :, cols], ALU.mult, ALU.mult))
                dve.tensor_tensor(gate, gate, o, ALU.mult).then_inc(sg("mixed_done"), 1)

            for cch in range(CHUNKS):
                po = CHUNK * (cch % 2)
                pr = slice(po, po + CHUNK)
                dve.wait_ge(sg("vnew_mm"), cch + 1)
                dve.tensor_copy(vn[pr].rearrange("p h n -> p (h n)"), psf[pr, 0:1024]).then_inc(sg("vnew"), 1)
                if cch < CHUNKS - 1:
                    dve.wait_ge(sg("ds_mm"), cch + 1)
                    if cch == 0:
                        dve.tensor_copy(st[1][:].rearrange("p h n -> p (h n)"), psf[:, 1536:2560]).then_inc(sg("state"), 1)
                    else:
                        for h in range(8):
                            ins = dve.scalar_tensor_tensor(st[(cch + 1) % 2][:, h, :], st[cch % 2][:, h, :], egl[:, h, cch:cch + 1],
                                                           psf[:, 1536 + h * P:1536 + (h + 1) * P], ALU.mult, ALU.add)
                        ins.then_inc(sg("state"), 1)
                if cch:
                    finish(cch - 1)
                dve.wait_ge(sg("o_mm"), cch + 1)
                o_, sq = (t[:, :, cch * CHUNK:(cch + 1) * CHUNK] for t in (odn, odn_sq))
                dve.tensor_copy(o_, ps[:, 2, :].rearrange("p (h n) -> p h n", h=8)).then_inc(sg("o_out"), 1)
                dve.wait_ge(sg("o_out"), cch + 1)
                dve.tensor_tensor(sq, o_, o_, ALU.mult).then_inc(sg("odn_sq"), 1)
            finish(CHUNKS - 1)

            dve.wait_ge(sg("mixed_done"), CHUNKS)
            lower(2, mixed)
            segment(U_OUT, OUT_UNITS, add_to_x)
            norm(2, X, G_FINAL, X, done=sg("x2_done"))
            dve.wait_ge(sg("x2_done"), 4)
            norm(3, X, G_MIX, T16, 3)
            dve.wait_ge(lin_lo2, 8)
            dve.wait_ge(sg("f_mm"), 1)
            dve.tensor_copy(f8[:], psf[0:8, 0:S]).then_inc(sg("f_row"), 1)
            dve.wait_ge(sg("f_t"), 1)
            dve.tensor_tensor(fcol[:], psf[:, S:S + 16].rearrange("p (a n) -> p a n", a=TT),
                              f_bias.unsqueeze(1).broadcast_to([P, TT, 8]), ALU.add).then_inc(sg("f_in"), 1)
            dve.wait_ge(sg("f_ln"), 1)
            dve.scalar_tensor_tensor(fcol[:], fcol[:], 0.0, fl[:], ALU.min, ALU.subtract).then_inc(sg("f_col"), 1)
            segment(U_IN2 + 32, 8, into(qa, SCALE))
            segment(U_IN2 + 40, 8, into(ka))
            dve.wait_ge(sg("cumf_mm"), 1)
            step(dve.tensor_scalar(ft8[:], psf[0:8, 1024:1024 + S], -1.0, None, ALU.mult))
            dve.tensor_copy(cf8[:], psf[0:8, 1024:1024 + S]).then_inc(sg("cumf"), 1)
            segment(U_IN2 + 48, 8, into(va))
            segment(U_IN2 + 56, 8, into(qb, SCALE))
            segment(U_IN2 + 64, 8, into(kb))
            segment(U_IN2 + 72, 8, into(vb2))

            strict = c(TRI_LT).unsqueeze(1).broadcast_to([P, GH, P])
            d0 = lambda f: f[:, 0:GH * S].rearrange("p (h n) -> p h n", h=GH)[:, :, 0:P]
            d1 = lambda f: f[:, GH * S:SCORES].rearrange("p (h n) -> p h n", h=GH)
            group = lambda t, g: t[:, GH * g:GH * (g + 1)]
            for g in range(2):
                fa, fb, z = za_g[g], zb_g[g], at_banks[g][:, 0:SCORES]
                dve.wait_ge(sg("sb_ln"), g + 1)
                step(dve.scalar_tensor_tensor(fa, z, 0.0, fa, ALU.max, ALU.add))
                step(dve.tensor_tensor(fb, z, fa, ALU.subtract))
                step(dve.tensor_tensor(d0(fa), d0(fa), strict, ALU.mult))
                dve.tensor_tensor(d1(fa), d1(fa), strict, ALU.mult).then_inc(sg("sb_sp"), 1)
            for g in range(2):
                dve.wait_ge(sg("sb_suffix"), g + 1)
                dve.tensor_tensor(zb_g[g], zb_g[g], at_banks[g][:, 0:SCORES], ALU.subtract).then_inc(sg("sb_arg"), 1)
            values = lambda g: group(vtk, g).rearrange("p h a n -> p (h a n)")

            def keep_values(g, moved, kept):
                dve.wait_ge(moved, g + 1)
                dve.tensor_copy(values(g), at_banks[g][:, 0:GH * S]).then_inc(kept, 1)

            for g in range(2):
                keep_values(g, sg("sb_vt_mm"), sg("sb_vt"))
                dve.wait_ge(sg("sb_exp"), g + 1)
                step(dve.tensor_tensor(d0(zb_g[g]), d0(zb_g[g]), strict, ALU.mult))
                dve.tensor_tensor(d1(zb_g[g]), d1(zb_g[g]), strict, ALU.mult).then_inc(sg("sb_w"), 1)

            l0 = lambda f: f[:, 0:GH * P].rearrange("p (h n) -> p h n", h=GH)
            l1 = lambda f: f[:, GH * P:SCORES].rearrange("p (h n) -> p h n", h=GH)
            for g in range(2):
                dve.wait_ge(sg("sb_out"), g + 1)
                dve.tensor_copy(T16[:, GH * g:GH * (g + 1), :].rearrange("p h n -> p (h n)"), at_banks[g][:, GH * S:2 * GH * S]
                                ).then_inc(sg("sb_done"), 1)
            for g in range(2):
                fa, z = za_g[g], at_banks[g][:, 0:SCORES]
                dve.wait_ge(sg("fx_logits"), g + 1)
                step(dve.scalar_tensor_tensor(l0(fa), strict, NEG_INF, l0(z), ALU.mult, ALU.add))
                step(dve.scalar_tensor_tensor(l1(fa)[:, :, P:S], strict, NEG_INF, l1(z)[:, :, P:S], ALU.mult, ALU.add))
                step(dve.tensor_copy(l1(fa)[:, :, 0:P], l1(z)[:, :, 0:P]))
                n = 2 * GH * g
                step(dve.tensor_reduce(nfx[:, n:n + GH], l0(fa), AX, ALU.max, negate=True))
                dve.tensor_reduce(nfx[:, n + GH:n + 2 * GH], l1(fa), AX, ALU.max, negate=True).then_inc(sg("fx_max"), 1)
            for g in range(2):
                n = 2 * GH * g
                fa = za_g[g]
                dve.wait_ge(sg("fx_exp"), 2 * GH * (g + 1))
                step(dve.reciprocal(rfx[:, n:n + 2 * GH], rfx[:, n:n + 2 * GH]))
                step(dve.tensor_tensor(l0(fa), l0(fa), rfx[:, n:n + GH].unsqueeze(2).broadcast_to([P, GH, P]), ALU.mult))
                dve.tensor_tensor(l1(fa), l1(fa), rfx[:, n + GH:n + 2 * GH].unsqueeze(2).broadcast_to([P, GH, S]), ALU.mult).then_inc(sg("fx_p"), 1)
            for g in range(2):
                keep_values(g, sg("fx_vt_mm"), sg("fx_vt"))
            for g in range(2):
                dve.wait_ge(sg("fx_out"), g + 1)
                dve.tensor_copy(T16[:, 8 + GH * g:8 + GH * (g + 1), :].rearrange("p h n -> p (h n)"), at_banks[g][:, GH * S:2 * GH * S]
                                ).then_inc(sg("fx_done"), 1)

            lower(4)
            with dve.Fori(0, BR_UNITS // 2) as i:
                ga = sga[:, bass.ds(i * 2, 2), :].rearrange("p a n -> p (a n)")
                gb = sgb[:, bass.ds(i * 2, 2), :].rearrange("p a n -> p (a n)")
                dve.wait_ge(pe_half, i * 4 + (2 * U_BR + 2))
                dve.tensor_tensor(ga, unit_ps[:, 0, :], ga, ALU.mult).then_inc(evac[0], 1)
                dve.wait_ge(pe_half, i * 4 + (2 * U_BR + 4))
                dve.tensor_tensor(gb, unit_ps[:, 1, :], gb, ALU.mult).then_inc(evac[1], 1)
                dve.wait_ge(evac[1], i + (U_BR // 2 + 1))
                dve.tensor_tensor(ga, ga, gb, ALU.add).then_inc(sg("merged"), 1)
            lower(5, sga)
            segment(U_OUT2, OUT_UNITS, add_to_x)
            norm(4, X, G_FFN, T16, 6)
            dve.wait_ge(lin_lo2, 14)
            segment(U_Q, OUT_UNITS, into(T16))

            def top16(vals, idx, src):
                work = rest[:, 0:src.shape[-1]]
                step(dve.max(vals[:, 0:8], src))
                step(dve.max_index(idx[:, 0:8], vals[:, 0:8], src))
                step(dve.match_replace(work, vals[:, 0:8], src, -3.0e38))
                step(dve.max(vals[:, 8:16], work))
                step(dve.max_index(idx[:, 8:16], vals[:, 8:16], work))

            scf = sc[:].rearrange("p t a n -> p (t a n)")
            for n in range(8):
                dve.wait_ge(sg("key_scores"), n + 1)
                dve.tensor_copy(scf[:, n * 512:(n + 1) * 512], ps[:, n % 6, :]).then_inc(sg("key_out"), 1)
            dve.wait_ge(sg("key_out"), 8)
            heads = lambda t: t.rearrange("p (h k) -> p h k", h=8)
            for t in range(TT):
                for hp in range(16):
                    top16(v16[:, hp, :], i16[:, hp, :], sc[:, t, hp, :])
                step(dve.tensor_copy(if16[:], i16[:]))
                v4_ = v16[:].rearrange("p (h two) k -> p h two k", two=2)
                i4_ = if16[:].rearrange("p (h two) k -> p h two k", two=2)
                for h in range(8):
                    step(dve.tensor_tensor(cand[:, h, :].rearrange("p (i j) -> p i j", i=TOPK),
                                           v4_[:, h, 0, :].unsqueeze(2).broadcast_to([P, TOPK, TOPK]),
                                           v4_[:, h, 1, :].unsqueeze(1).broadcast_to([P, TOPK, TOPK]), ALU.add))
                for h in range(8):
                    top16(ts[:, h, :], ti[:, h, :], cand[:, h, :])
                step(dve.tensor_scalar(th[:], ti[:], 4, None, ALU.logical_shift_right))
                step(dve.tensor_scalar(tl[:], ti[:], 15, None, ALU.bitwise_and))
                step(dve.tensor_copy(thf[:], th[:]))
                step(dve.tensor_copy(tlf[:], tl[:]))
                iota16 = cst[:, IOTA, 0:TOPK].unsqueeze(1).broadcast_to([P, P, TOPK])
                c3 = cand[:].rearrange("p h (k j) -> p (h k) j", j=TOPK)
                c4 = cand[:].rearrange("p h (k j) -> p h k j", j=TOPK)
                for half, pos in enumerate((thf, tlf)):
                    step(dve.tensor_tensor(c3, iota16, pos[:].rearrange("p h k -> p (h k)").unsqueeze(2).broadcast_to([P, P, TOPK]), ALU.is_equal))
                    step(dve.tensor_tensor(c4, c4, i4_[:, :, half, :].unsqueeze(2).broadcast_to([P, 8, TOPK, TOPK]), ALU.mult))
                    step(dve.tensor_reduce(picks[:, t, half, :], c3, AX, ALU.add))
                ins = dve.tensor_tensor(heads(picks[:, t, 2, :]), ts[:], ts[:, :, 0:1].broadcast_to([P, 8, TOPK]), ALU.subtract)
                if t == TT - 1:
                    ins.then_inc(sg("gate_arg"), 1)
                else:
                    step(ins)
            dve.wait_ge(sg("gate_exp"), 1)
            for t in range(TT):
                g3 = heads(picks[:, t, 2, :])
                step(dve.tensor_reduce(gs[:], g3, AX, ALU.add))
                step(dve.reciprocal(gs[:], gs[:]))
                dve.tensor_tensor(g3, g3, gs[:].unsqueeze(2).broadcast_to([P, 8, TOPK]), ALU.mult).then_inc(sg("picked"), 1)
                dve.wait_ge(sg("picked"), t + 1)
            dve.wait_ge(sg("picks_t"), 1)
            for a in range(3):
                dve.tensor_copy(sel[:, a, :].rearrange("p (t n) -> p t n", t=TT),
                                psf[:, 2048:3072].rearrange("p (t a n) -> p t a n", t=TT, a=4)[:, :, a, :]).then_inc(sg("sel"), 1)
            dve.wait_ge(sg("sel"), 3)

            def onehots(g16):
                for b8 in range(0, ONEHOTS, 8):
                    if not isinstance(g16, int):
                        dve.wait_ge(sg("gate_mm"), g16 * ONEHOTS + (b8 + 8 - ONEHOTS))
                    row = sel[:, 1:2, bass.ds(g16 * ONEHOTS + b8, 8)].rearrange("p a n -> p (a n)")
                    dve.tensor_tensor(oh2[:, b8:b8 + 8, :], c(IOTA).unsqueeze(1).broadcast_to([P, 8, P]),
                                      row.unsqueeze(2).broadcast_to([P, 8, P]), ALU.is_equal).then_inc(sg("oh2"), 1)
                    for b in range(b8, b8 + 8):
                        col = lambda a: sel[:, a, bass.ds(g16 * ONEHOTS + b, 1)]
                        dve.tensor_scalar(oh1[:, b, :], c(IOTA), col(0), col(2), ALU.is_equal, ALU.mult).then_inc(sg("oh"), 1)
            onehots(0)
            with dve.Fori(1, S // ONEHOTS) as g16:
                onehots(g16)

            def gate_quarter(e, q):
                upper, lower_ = gated(e)
                if q == 0:
                    u = first_unit("up", e)
                    dve.wait_ge(evac[0], (u + KT) // 2)
                    dve.wait_ge(evac[1], (u + KT) // 2)
                    dve.wait_ge(sg("gate_in"), 16 * (e + 1))
                    if e >= EXPERT_CHUNKS - 2:
                        dve.wait_ge(pe_half, 2 * (first_unit("up", EXPERT_CHUNKS - 1) + KT))
                    elif e:
                        dve.wait_ge(pe_half, 2 * (first_unit("down", e - 1) + KT))
                ks = slice(4 * q, 4 * q + 4)
                h = hidden[e % 3][:, ks, :]
                h4 = h.rearrange("p a (g n) -> p a g n", g=16)
                dve.tensor_tensor(h4, h4, gch[:, :, ks, :].rearrange("p g a n -> p a g n"), ALU.mult).then_inc(sg("gates_used"), 1)
                dve.wait_ge(sg("gates_used"), 4 * e + q + 1)
                step(dve.tensor_copy(upper[:, ks, :], h))
                dve.tensor_tensor(lower_[:, ks, :], h, upper[:, ks, :].bitcast(F32), ALU.subtract).then_inc(sg("hid_lo"), 1)

            for e in range(EXPERT_CHUNKS):
                u0 = first_unit("down", e)
                if e < EXPERT_CHUNKS - 2:
                    for q in range(4):
                        gate_quarter(e, q)
                if e < EXPERT_CHUNKS - 3 or e == EXPERT_CHUNKS - 1:
                    segment(u0, KT, add_to_x)
                else:
                    for q in range(4):
                        gate_quarter(e + 1, q)
                        for j in range(4):
                            dve.wait_ge(pe_half, 2 * (u0 + 4 * q + j) + 2)
                            add_to_x(q, j).then_inc(evac[j % 2], 1)
            norm(5, X, G_OUT, T16, done=sg("result"))

        @block.tensor
        def _(pe):
            def mm(o, lhsT, rhs, start=True, stop=True, **k):
                return nc.tensor.matmul(o, lhsT, rhs, start=start, stop=stop, **k)

            def unit_body(u, j, hi, lo, par, paired=False, ready=None):
                s0 = (2 * j) % 4
                o = unit_ps[:, j % 2, :]
                if not (isinstance(par, int) and par == 0):
                    pe.wait_ge(evac[j % 2], par)
                for h in range(2):
                    if ready is not None and h == 0 and (j == 0 or paired):
                        pe.wait_ge((lin_lo, lin_lo2)[j], 2 * ready + 2)
                    if ready is not None and h == 1 and j == 0 and not paired:
                        pe.wait_ge(lin_lo2, 2 * ready + 2)
                    pe.wait_ge(lo_ready, u * 2 + (2 * j + h + 1))
                    for k in range(HALF):
                        if paired:
                            x = k + HALF * (j % 2)
                            oo, first, last = o[:, h * S:(h + 1) * S], k == 0, k == HALF - 1
                        else:
                            x = h * HALF + k
                            oo, first, last = o[:, 0:S], h == 0 and k == 0, h == 1 and k == HALF - 1
                        a, b = whi[:, s0 + h, k, :], wlo[:, s0 + h, k, :]
                        mm(oo, a, hi[:, x, :], start=first, stop=False)
                        mm(oo, a, lo[:, x, :], start=False, stop=False)
                        z = mm(oo, b, hi[:, x, :], start=False, stop=last)
                    z.then_inc(pe_half, 1)

            def segment(u0, n, paired=False, hi=xhi, lo=xlo, ready=None):
                first = int(ready is not None)
                for j in range(2 * first):
                    unit_body(u0, j, hi, lo, u0 // 2, paired, ready)
                with pe.Fori(first, n // 2) as i:
                    for j in range(2):
                        unit_body(i * 2 + u0, j, hi, lo, i + u0 // 2, paired)

            def norm_sums(n, quarters=range(4)):
                for q in quarters:
                    pe.wait_ge(norm_sq, 4 * n + q + 1)
                    for k in range(4 * q, 4 * q + 4):
                        z = mm(psf[:, 0:S], ones, T16[:, k, :], k == 0, k == KT - 1)
                if q == 3:
                    z.then_inc(norm_sum, 1)

            def residual_segment(n, u0, hi=xhi, lo=xlo, ready=None):
                segment(u0, 12, False, hi, lo, ready)
                norm_sums(n, (0, 1))
                segment(u0 + 12, 4, False, hi, lo)
                norm_sums(n, (2, 3))

            def tr(o, i, idn=None):
                return nc.tensor.transpose(o, i, ident if idn is None else idn)

            pe.wait_ge(cst_in, 16 * 7)
            norm_sums(0)
            segment(U_KV, KV_UNITS, ready=0)
            pe.wait_ge(evac[0], KV_UNITS // 2)
            pe.wait_ge(evac[1], KV_UNITS // 2)
            for t in range(TT):
                for h in range(XA_HEADS):
                    z = tr(psf[:, 1024 + (t * 4 + h) * P:1024 + (t * 4 + h + 1) * P], mvf[:, h, t * P:(t + 1) * P])
            z.then_inc(sg("mv_t"), 1)
            norm_sums(1)
            def narrow(col, n, done):
                for k in range(KT):
                    mm(psf[0:n, 0:S], wab_hi[:, k, col:col + n], xhi[:, k, :], k == 0, False)
                    mm(psf[0:n, 0:S], wab_hi[:, k, col:col + n], xlo[:, k, :], False, False)
                    z = mm(psf[0:n, 0:S], wab_lo[:, k, col:col + n], xhi[:, k, :], False, k == KT - 1)
                z.then_inc(done, 1)

            def by_token(rows, n, done):
                for t in range(TT):
                    z = tr(psf[:, S + t * n:S + (t + 1) * n], rows[:, t * P:(t + 1) * P], ident[0:n, 0:n])
                z.then_inc(done, 1)

            segment(U_IN, 4, ready=1)
            pe.wait_ge(sg("wab_lo"), 1)
            narrow(0, 16, sg("ab_mm"))
            segment(U_IN + 4, 4)
            pe.wait_ge(sg("ab_row"), 1)
            by_token(ab16, 16, sg("ab_t"))
            pe.wait_ge(sg("kv_done"), 1)
            pe.wait_ge(evac[0], U_IN // 2 + 2)
            pe.wait_ge(evac[1], U_IN // 2 + 2)
            for h in range(XA_HEADS):
                for t in range(TT):
                    n = 2 * h + t
                    z = mm(psf[:, 1024 + n * S:1024 + (n + 1) * S], cq[:, h, t * P:(t + 1) * P], mk[:, h, :])
            z.then_inc(sg("xa_scores"), 1)
            segment(U_IN + 8, 12)
            pe.wait_ge(sg("xa_norm"), 1)
            for h in range(XA_HEADS):
                for m in range(TT):
                    for t in range(TT):
                        z = tr(psf[:, 1024 + (2 * h + m) * S + t * P:1024 + (2 * h + m) * S + (t + 1) * P],
                               xa_p[:, 2 * h + t, m * P:(m + 1) * P])
            z.then_inc(sg("xa_pt_mm"), 1)
            segment(U_IN + 20, 4)
            pe.wait_ge(sg("xa_pt"), 1)
            pe.wait_ge(sg("ab_in"), 1)
            for h in range(XA_HEADS):
                for m in range(TT):
                    z = mm(psf[:, h * S:(h + 1) * S], mvt[:, m, h, :], xa_pt[:, h, m, :], m == 0, m == TT - 1)
            z.then_inc(sg("xa_out"), 1)
            pe.wait_ge(evac[0], (U_IN + 20) // 2)
            pe.wait_ge(evac[1], (U_IN + 20) // 2)
            for g in range(GROUPS):
                z = mm(psf[:, 1024:1024 + S], ones, gv[:, g, :], g == 0, g == GROUPS - 1)
            z.then_inc(sg("ln_sum"), 1)
            segment(U_IN + 24, 4)
            pe.wait_ge(sg("g_col"), 1)
            pe.wait_ge(sg("beta"), 1)
            pe.wait_ge(sg("xa_done"), 1)
            for t in range(TT):
                mm(psf[0:8, 512 + t * P:512 + (t + 1) * P], gbt[:, t, 0, :], c(C64_LE))
                mm(psf[0:8, 256 + t * P:256 + (t + 1) * P], gbt[:, t, 1, :], ident)
            for t in range(TT):
                for x, m in enumerate((C64_LE, C64_GT)):
                    z = mm(psf[:, 768 + (2 * t + x) * 8:768 + (2 * t + x + 1) * 8], c(m), gbt[:, t, 0, :])
            z.then_inc(sg("gsum_mm"), 1)
            pe.wait_ge(sg("ln_sq"), 1)
            for g in range(GROUPS):
                z = mm(psf[:, 1536:1536 + S], ones, vsq[:, g, :], g == 0, g == GROUPS - 1)
            z.then_inc(sg("ln_sqsum"), 1)
            segment(U_IN + 28, 8)
            pe.wait_ge(sg("ln_out"), 1)
            for g in range(GROUPS):
                for t in range(TT):
                    z = tr(psf[:, 2048 + (2 * g + t) * P:2048 + (2 * g + t + 1) * P], gv[:, g, t * P:(t + 1) * P])
            z.then_inc(sg("v_t"), 1)
            segment(U_IN + 36, 4)
            pe.wait_ge(sg("v_tc"), 1)
            pe.wait_ge(sg("ws_masked"), 1)
            for g in range(GROUPS):
                for t in range(TT):
                    o = psf[:, 1024 + (2 * g + t) * P:1024 + (2 * g + t + 1) * P]
                    mm(o, vt[:, g, t, :], wst[:, g, :], True, False)
                    z = mm(o, ones[0:1, :], bs_row[0:1, g * P:(g + 1) * P], False, True)
            z.then_inc(sg("sgu"), 1)

            def head_sums(w):
                pe.wait_ge(sg("qk_sq"), w + 1)
                for h in range(8):
                    z = mm(ps_a[:, h * S:(h + 1) * S], ones, qk_sq[:, h, :])
                z.then_inc(sg("qk_ss"), 1)

            segment(U_IN + 40, 4)
            pe.wait_ge(sg("gmlp_out"), 1)
            head_sums(0)
            segment(U_IN + 44, 4)
            pe.wait_ge(sg("qk_rs"), 1)
            head_sums(1)
            segment(U_IN + 48, 4)
            def rows(dst, src, done):
                for h in range(8):
                    z = mm(dst[:, h * S:(h + 1) * S], ident[0:8, h:h + 1].to_broadcast([8, P]), src[:, :])
                z.then_inc(done, 1)

            pe.wait_ge(sg("gcol_in"), 1)
            pe.wait_ge(sg("qk_rs"), 2)
            rows(ps_a, gc8, sg("row_bc"))
            pe.wait_ge(evac[0], U_OUT // 2)
            pe.wait_ge(evac[1], U_OUT // 2)
            pe.wait_ge(sg("qk_scaled"), 2)
            for n in range(16):
                z = tr(ps_b[:, n * P:(n + 1) * P], qkv[:, 8 + n // 2, (n % 2) * P:(n % 2 + 1) * P])
            z.then_inc(sg("k_t"), 1)
            pe.wait_ge(sg("exp_row"), 1)
            for n in range(16):
                kk = qkv[:, 8 + n // 2, (n % 2) * P:(n % 2 + 1) * P]
                z = mm(ps_a[:, n * P:(n + 1) * P], kk, kk)
            z.then_inc(sg("kk"), 1)
            pe.wait_ge(sg("kd"), 16)
            pe.wait_ge(sg("kbg"), 2)
            pe.wait_ge(conv_used, 24)
            for n in range(16):
                z = tr(ps_b[:, n * P:(n + 1) * P], qkv[:, 16 + n // 2, (n % 2) * P:(n % 2 + 1) * P])
            z.then_inc(sg("v_dt"), 1)
            pe.wait_ge(sg("kk_out"), 1)
            for n in range(16):
                sl = slice((n % 2) * P, (n % 2 + 1) * P)
                z = mm(ps_a[:, n * P:(n + 1) * P], qkv[:, 8 + n // 2, sl], qkv[:, n // 2, sl])
            z.then_inc(sg("qk"), 1)
            pe.wait_ge(sg("vb"), 16)
            rows(ps_b, bt8, sg("beta_bc"))
            for g in range(4):
                if g == 0:
                    pe.wait_ge(sg("inv_q0"), 4)
                for n in range(4 * g, 4 * g + 4):
                    z = tr(ps[:, g, (n % 4) * P:(n % 4 + 1) * P], qt[:, n, :])
                z.then_inc(sg("inv_p0"), 1)
            pe.wait_ge(sg("inv_upd"), 4)
            with pe.Fori(1, LEVELS) as lev:
                for g in range(4):
                    pe.wait_ge(sg("inv_a"), lev * 4 + (g - 3))
                    pe.wait_ge(sg("inv_upd"), lev * 4 + (g - 3))
                    for n in range(4 * g, 4 * g + 4):
                        z = mm(ps[:, g, (n % 4) * P:(n % 4 + 1) * P], dec[:, n, :], pt[:, n, :])
                    z.then_inc(sg("inv_x"), 1)
                for g in range(4):
                    pe.wait_ge(sg("inv_xc"), lev * 4 + (g - 3))
                    if g >= 2:
                        pe.wait_ge(sg("inv_upd"), lev * 4 + (g - 1))
                    for n in range(4 * g, 4 * g + 4):
                        mm(pq(g)[0][:, (n % 4) * P:(n % 4 + 1) * P], qt[:, n, :], xt[:, n, :])
                    for n in range(4 * g, 4 * g + 4):
                        z = mm(pq(g)[1][:, (n % 4) * P:(n % 4 + 1) * P], xt[:, n, :], qt[:, n, :])
                    z.then_inc(sg("inv_pq"), 1)
            pe.wait_ge(sg("inv_upd"), LEVELS * 4)
            for n in range(16):
                z = mm(psf[:, n * P:(n + 1) * P], kbg[:, n, :], qt[:, n, :])
            z.then_inc(sg("kcd_mm"), 1)
            pe.wait_ge(sg("kcd"), 1)

            def out_sums(cch):
                pe.wait_ge(sg("odn_sq"), cch + 1)
                if cch:
                    pe.wait_ge(sg("odn_rs"), cch)
                mm(ps[:, 5, :], ones, odn_sq[:, :, cch * CHUNK:(cch + 1) * CHUNK]).then_inc(sg("odn_ss"), 1)

            pe.wait_ge(sg("q_decayed"), 1)
            for cch in range(CHUNKS):
                t, po = cch // 2, CHUNK * (cch % 2)
                pr = slice(po, po + CHUNK)
                if cch:
                    pe.wait_ge(sg("state"), cch)
                for h in range(8):
                    o = psf[pr, h * P:(h + 1) * P]
                    z = mm(o, qt[pr, 2 * h + t, pr], vb[pr, 2 * h + t, :], True, cch == 0)
                    if cch:
                        z = mm(o, kcd[:, 2 * h + t, pr], st[cch % 2][:, h, :], False, True)
                z.then_inc(sg("vnew_mm"), 1)
                o = lambda h: ps[:, 2, h * CHUNK:(h + 1) * CHUNK]
                if cch:
                    out_sums(cch - 1)
                    pe.wait_ge(sg("o_out"), cch)
                pe.wait_ge(sg("vnew"), cch + 1)
                if cch < CHUNKS - 1:
                    for h in range(8):
                        z = mm(psf[:, 1536 + h * P:1536 + (h + 1) * P], kd[pr, 2 * h + t, :], vn[pr, h, :])
                    z.then_inc(sg("ds_mm"), 1)
                for h in range(8):
                    if cch:
                        mm(o(h), st[cch % 2][:, h, :], qkv[:, h, cch * CHUNK:(cch + 1) * CHUNK], True, False)
                    z = mm(o(h), vn[pr, h, :], ait[pr, 2 * h + t, pr], cch == 0, True)
                z.then_inc(sg("o_mm"), 1)
            out_sums(CHUNKS - 1)

            residual_segment(2, U_OUT, ready=2)
            norm_sums(3)
            segment(U_IN2, 16, ready=3)
            narrow(16, 8, sg("f_mm"))
            segment(U_IN2 + 16, 16)
            pe.wait_ge(sg("f_row"), 1)
            by_token(f8, 8, sg("f_t"))
            segment(U_IN2 + 32, 16)
            pe.wait_ge(sg("f_col"), 1)
            mm(psf[0:8, 1024:1024 + P], fcol[:, 0, :], c(TRI_LE))
            mm(psf[0:8, 1024 + P:1024 + S], fcol[:, 0, :], ones, True, False)
            mm(psf[0:8, 1024 + P:1024 + S], fcol[:, 1, :], c(TRI_LE), False, True).then_inc(sg("cumf_mm"), 1)
            segment(U_IN2 + 48, 32)

            def wait_units(u):
                pe.wait_ge(evac[0], u // 2)
                pe.wait_ge(evac[1], u // 2)

            wait_units(U_BR)
            pe.wait_ge(sg("cumf"), 1)

            def values_by_token(v, g, done):
                for n in range(2 * GH):
                    z = tr(at_banks[g][:, n * P:(n + 1) * P], v[:, GH * g + n // 2, (n % 2) * P:(n % 2 + 1) * P])
                z.then_inc(done, 1)

            def weighted_values(g, done):
                w = zb_g[g]
                for h in range(GH):
                    o = at_banks[g][:, (GH + h) * S:(GH + h + 1) * S]
                    mm(o, vtk[:, GH * g + h, 0, :], w[:, h * S:(h + 1) * S], True, False)
                    z = mm(o[:, P:S], vtk[:, GH * g + h, 1, :], w[:, GH * S + h * P:GH * S + (h + 1) * P], False, True)
                z.then_inc(done, 1)

            tile1 = lambda t, h: t[:, GH * S + h * P:GH * S + (h + 1) * P]
            for g in range(2):
                for h in range(GH):
                    k_, q_ = ka[:, GH * g + h, :], qa[:, GH * g + h, :]
                    mm(at_banks[g][:, h * S:(h + 1) * S], k_[:, 0:P], q_)
                    z = mm(tile1(at_banks[g], h), k_[:, P:S], q_[:, P:S])
                z.then_inc(sg("sb_z"), 1)
            for g in range(2):
                pe.wait_ge(sg("sb_sp"), g + 1)
                for h in range(GH):
                    o, sp_ = at_banks[g][:, h * S:(h + 1) * S], za_g[g]
                    mm(o, c(TRI_GT), sp_[:, h * S:(h + 1) * S], True, False)
                    mm(o[:, P:S], ones, tile1(sp_, h), False, True)
                    z = mm(tile1(at_banks[g], h), c(TRI_GT), tile1(sp_, h))
                z.then_inc(sg("sb_suffix"), 1)
            for g in range(2):
                pe.wait_ge(sg("sb_arg"), g + 1)
                values_by_token(va, g, sg("sb_vt_mm"))

            def logits(g):
                pe.wait_ge(sg("sb_vt"), g + 1)
                for h in range(GH):
                    pick = ident[0:8, GH * g + h:GH * g + h + 1]
                    b = at_banks[g]
                    for t, o, n in ((0, b[:, h * P:(h + 1) * P], P), (1, b[:, GH * P + h * S:GH * P + (h + 1) * S], S)):
                        sl = slice(t * P, (t + 1) * P)
                        mm(o, qb[:, GH * g + h, sl], kb[:, GH * g + h, 0:n], True, False)
                        mm(o, cf8[:, sl], pick.to_broadcast([8, n]), False, False)
                        z = mm(o, pick.to_broadcast([8, P]), ft8[:, 0:n], False, True)
                z.then_inc(sg("fx_logits"), 1)

            for g in range(2):
                pe.wait_ge(sg("sb_w"), g + 1)
                weighted_values(g, sg("sb_out"))
            for g in range(2):
                pe.wait_ge(sg("sb_done"), g + 1)
                logits(g)
            for g in range(2):
                pe.wait_ge(sg("fx_p"), g + 1)
                b, p_ = at_banks[g], za_g[g]
                for h in range(GH):
                    l1_ = p_[:, GH * P + h * S:GH * P + (h + 1) * S]
                    tr(b[:, h * S:h * S + P], p_[:, h * P:(h + 1) * P])
                    tr(b[:, h * S + P:(h + 1) * S], l1_[:, 0:P])
                    z = tr(tile1(b, h), l1_[:, P:S])
                z.then_inc(sg("fx_pt_mm"), 1)
            for g in range(2):
                pe.wait_ge(sg("fx_pt"), g + 1)
                values_by_token(vb2, g, sg("fx_vt_mm"))
            for g in range(2):
                pe.wait_ge(sg("fx_vt"), g + 1)
                weighted_values(g, sg("fx_out"))

            segment(U_BR, BR_UNITS, paired=True, ready=4)
            residual_segment(4, U_OUT2, ready=5)
            segment(U_Q, OUT_UNITS, ready=6)

            wait_units(U_EXP)
            pe.wait_ge(sk_ld, 16)
            for n in range(8):
                if n >= 6:
                    pe.wait_ge(sg("key_out"), n - 5)
                for b in range(4):
                    t, hp = n // 4, 4 * (n % 4) + b
                    z = mm(ps[:, n % 6, b * P:(b + 1) * P], T16[:, hp, t * P:(t + 1) * P], skt[:, hp, :])
                z.then_inc(sg("key_scores"), 1)

            def transpose_picks():
                pe.wait_ge(sg("picked"), TT)
                for t in range(TT):
                    for a in range(3):
                        z = tr(psf[:, 2048 + (4 * t + a) * P:2048 + (4 * t + a + 1) * P], picks[:, t, a, :])
                z.then_inc(sg("picks_t"), 1)

            def gates(g16):
                for q in range(4):
                    if g16:
                        pe.wait_ge(sg("gate_out"), g16 * 4 + (q - 3))
                    if q % 2 == 0:
                        pe.wait_ge(sg("oh2"), g16 * 2 + (q // 2 + 1))
                    for b in range(4 * q, 4 * q + 4):
                        pe.wait_ge(sg("oh"), g16 * 16 + (b + 1))
                        mm(ps[:, q, (b % 4) * P:(b % 4 + 1) * P], oh2[:, b, :], oh1[:, b, :]).then_inc(sg("gate_mm"), 1)

            for kind, e in ORDER:
                u0 = first_unit(kind, e)
                if (kind, e) == ("up", 2):
                    transpose_picks()
                    g16 = 0
                    for n, groups in enumerate(GATE_GROUPS):
                        unit_body(u0 + n - n % 2, n % 2, xhi, xlo, (u0 + n) // 2)
                        for _ in range(groups):
                            gates(g16)
                            g16 += 1
                    segment(u0 + 12, 4)
                elif kind == "up":
                    segment(u0, KT)
                else:
                    pe.wait_ge(sg("hid_lo"), 4 * e + 4)
                    if e < EXPERT_CHUNKS - 1:
                        segment(u0, KT, False, *gated(e))
                    else:
                        residual_segment(5, u0, *gated(e))


def kernel(**inputs):
    import numpy as np
    import concourse.bacc as bacc
    from concourse.bass_utils import run_bass_kernel_spmd

    def units(w):
        k, n = w.shape
        return w.reshape(k // P, P, n // P, P).transpose(2, 1, 0, 3).reshape(n // P, P, k)

    def features(x):
        return x.T.reshape(KT, P, S).transpose(1, 0, 2)

    def column(v):
        return v.reshape(-1, P).T

    x = {k: np.asarray(v) for k, v in inputs.items()}
    w = x["w_in"][0]
    cuts = np.cumsum([0, 512, 512, 512, 1024, 1024, 1024, 1024, 8, 8, 512, 512])
    seg = lambda i: w[:, cuts[i]:cuts[i + 1]]
    u, v, z, dq, dk, dv, dz, da, db, cq, cz = (seg(i) for i in range(11))
    w2 = x["w_in_2"][0]
    cuts2 = np.cumsum([0] + [1024] * 6 + [8, 2048, 2048])
    qa, ka, va, qb, kb, vb, fl, ga, gb = (w2[:, cuts2[i]:cuts2[i + 1]] for i in range(9))
    br = np.stack([x["w_branch_a_2"][0], x["w_branch_b_2"][0]])
    br = br.reshape(2, KT // 2, P, KT // 2, 2, P).transpose(3, 0, 2, 4, 1, 5).reshape(BR_UNITS, P, D)
    up = units(x["expert_u_2"][0].T).reshape(EXPERT_CHUNKS, KT, P, D)
    down = x["expert_v_2"][0].reshape(EXPERT_CHUNKS, KT, P, KT, P).transpose(0, 3, 2, 1, 4).reshape(EXPERT_CHUNKS, KT, P, D)
    small = np.stack([x["dn_dt_bias"][0], np.zeros(8, np.float32), x["dn_a_log"][0], x["b_forget_2"][0]])
    arrays = {
        "mem": features(x["mem"][0]),
        "x": features(x["x"][0]),
        "consts": shape_constants(),
        "gains": np.stack([column(x[n].reshape(-1)) for n in
                           ("mem_norm_g", "ln_g", "final_g", "norm_mix_gain_2", "norm_ffn_gain_2", "norm_final_gain_2")], 1),
        "conv": x["conv_w"][0].reshape(TAPS, 24, P).transpose(2, 1, 0),
        "w_abf": np.concatenate([da, db, fl], 1).reshape(KT, P, 24).transpose(1, 0, 2),
        "head_rows": np.broadcast_to(small.reshape(1, 32), (P, 32)),
        "dn_g": x["dn_norm_g"][0].reshape(P, 1),
        "gmlp_ln": np.concatenate([column(x["gmlp_ln_g"][0]), column(x["gmlp_ln_b"][0])], 1),
        "ws": x["gmlp_ws"][0].transpose(2, 0, 1),
        "bs": x["gmlp_bs"][0].reshape(1, GROUPS * P),
        "sub_keys": x["sub_keys_2"][0].reshape(16, P, P).transpose(2, 0, 1),
        "w_kv": units(x["w_mem_kv"][0]),
        "w_in": units(np.concatenate([cq, cz, z, u, v, dz, dq, dk, dv], 1)),
        "w_out": units(x["w_out"][0]),
        "w_in2": units(np.concatenate([ga, gb, qa, ka, va, qb, kb, vb], 1)),
        "w_br": br,
        "w_out2": units(x["w_out_2"][0]),
        "w_q": units(x["w_query_2"][0]),
        "w_exp": np.concatenate([(up if kind == "up" else down)[e] for kind, e in ORDER]),
    }
    arrays = {k: np.ascontiguousarray(v) for k, v in arrays.items()}
    nc = bacc.Bacc("TRN2", target_bir_lowering=False, num_devices=1)
    ap = {k: nc.dram_tensor(f"in_{k}", v.shape, mybir.dt.from_np(v.dtype), kind="ExternalInput").ap() for k, v in arrays.items()}
    out = nc.dram_tensor("out", (P, KT, S), F32, kind="ExternalOutput").ap()
    g_dram = nc.dram_tensor("gates", (16, P, P * 16), F32, kind="Internal").ap()
    program(nc, ap, out, g_dram)
    r = run_bass_kernel_spmd(nc, [{f"in_{k}": v for k, v in arrays.items()}], core_ids=[0])
    y = r.results[0]["out"]
    return y.transpose(2, 1, 0).reshape(1, S, D)
```
